# Optimizing a Trainium2 kernel written in Bass

```python
import math
import jax, jax.numpy as jnp
from jax import lax
import numpy as np

D_MODEL = 1024
BATCH = 1
SEQ = 256
DEPTH = 2

DA_HEADS = 4
DA_HEAD_DIM = 64
DA_V_DIM = 2 * DA_HEAD_DIM
ROPE_THETA = 500000.0
ROPE_ROT_DIM = DA_HEAD_DIM // 4
Q_BLOCK = 128
RET_HEADS = 4
RET_QK_DIM = 64
RET_V_DIM = 2 * RET_QK_DIM
RET_CHUNK = 128
RET_ROPE_THETA = 10000.0
DA_Q_W = DA_HEADS * 2 * DA_HEAD_DIM
DA_K_W = DA_HEADS * 2 * DA_HEAD_DIM
DA_V_W = DA_HEADS * DA_V_DIM
RET_Q_W = RET_HEADS * RET_QK_DIM
RET_K_W = RET_HEADS * RET_QK_DIM
RET_V_W = RET_HEADS * RET_V_DIM
RET_G_W = RET_V_W
GATE_W = 2 * D_MODEL
IN_W = DA_Q_W + DA_K_W + DA_V_W + RET_Q_W + RET_K_W + RET_V_W + RET_G_W + GATE_W
D_FF = 2816
N_EXPERTS = 8
TOP_K = 2
N_DENSE = (DEPTH + 1) // 2
N_MOE = DEPTH // 2
EPS = 1e-6

kernel_name = "hybrid_diffattn_retention_gated_moe"

def rms_norm(x, g):
    xf = x.astype(jnp.float32)
    y = xf * lax.rsqrt(jnp.mean(xf * xf, axis=-1, keepdims=True) + EPS)
    return (y * g.astype(jnp.float32)).astype(x.dtype)

def group_norm(x):
    xf = x.astype(jnp.float32)
    mu = jnp.mean(xf, axis=-1, keepdims=True)
    xc = xf - mu
    return xc * lax.rsqrt(jnp.mean(xc * xc, axis=-1, keepdims=True) + EPS)

def rope(x, pos, rot_dim, theta):
    half = rot_dim // 2
    inv = 1.0 / (theta ** (jnp.arange(half, dtype=jnp.float32) / half))
    ang = pos.astype(jnp.float32)[..., None] * inv
    cos = jnp.cos(ang)[:, :, None, :].astype(x.dtype)
    sin = jnp.sin(ang)[:, :, None, :].astype(x.dtype)
    x1 = x[..., :half]
    x2 = x[..., half:rot_dim]
    rot = jnp.concatenate([x1 * cos - x2 * sin, x1 * sin + x2 * cos], axis=-1)
    return jnp.concatenate([rot, x[..., rot_dim:]], axis=-1)

def diff_attention(q, k, v, lam):
    B, S = q.shape[0], q.shape[1]
    nb = S // Q_BLOCK
    scale = DA_HEAD_DIM ** -0.5
    qb = q.reshape(B, nb, Q_BLOCK, DA_HEADS, 2, DA_HEAD_DIM).transpose(1, 0, 2, 3, 4, 5)
    kpos = jnp.arange(S)

    def block(args):
        qi, i = args
        s = jnp.einsum('bqhcd,bkhcd->bhcqk', qi, k,
                       preferred_element_type=jnp.float32) * scale
        qpos = i * Q_BLOCK + jnp.arange(Q_BLOCK)
        mask = kpos[None, :] <= qpos[:, None]
        p = jax.nn.softmax(jnp.where(mask, s, -jnp.inf), axis=-1)
        pd = p[:, :, 0] - lam * p[:, :, 1]
        return jnp.einsum('bhqk,bkhd->bqhd', pd.astype(v.dtype), v)

    out = lax.map(block, (qb, jnp.arange(nb)))
    return out.transpose(1, 0, 2, 3, 4).reshape(B, S, DA_HEADS, DA_V_DIM)

def retention(q, k, v):
    B, S = q.shape[0], q.shape[1]
    C = RET_CHUNK
    n = S // C
    log_gamma = jnp.log1p(-jnp.exp2(-5.0 - jnp.arange(RET_HEADS, dtype=jnp.float32)))
    k = k * (RET_QK_DIM ** -0.5)
    qc = q.reshape(B, n, C, RET_HEADS, RET_QK_DIM)
    kc = k.reshape(B, n, C, RET_HEADS, RET_QK_DIM)
    vc = v.reshape(B, n, C, RET_HEADS, RET_V_DIM)
    idx = jnp.arange(C, dtype=jnp.float32)
    rel = idx[:, None] - idx[None, :]
    decay = jnp.where(rel[None] >= 0,
                      jnp.exp(log_gamma[:, None, None] * jnp.maximum(rel, 0.0)[None]), 0.0)
    inner = jnp.einsum('bnqhd,bnkhd->bnhqk', qc, kc,
                       preferred_element_type=jnp.float32) * decay
    o_inner = jnp.einsum('bnhqk,bnkhe->bnqhe', inner, vc.astype(jnp.float32))
    k_dec = jnp.exp(log_gamma[None, :] * (C - 1.0 - idx)[:, None])
    kv = jnp.einsum('bnkhd,kh,bnkhe->nbhde', kc.astype(jnp.float32), k_dec,
                    vc.astype(jnp.float32))
    chunk_decay = jnp.exp(log_gamma * C)[None, :, None, None]

    def step(R, kv_i):
        return R * chunk_decay + kv_i, R

    R0 = jnp.zeros((B, RET_HEADS, RET_QK_DIM, RET_V_DIM), jnp.float32)
    _, R_prev = lax.scan(step, R0, kv)
    q_dec = jnp.exp(log_gamma[None, :] * (idx + 1.0)[:, None])
    o_cross = jnp.einsum('bnqhd,qh,nbhde->bnqhe', qc.astype(jnp.float32), q_dec, R_prev)
    return (o_inner + o_cross).reshape(B, S, RET_HEADS, RET_V_DIM)

def token_mixers(hn, pos, layer, w_in, da_q_norm, da_k_norm, lam_q1, lam_k1, lam_q2, lam_k2,
                 da_subln, w_proj_da, w_proj_ret, w_out):
    B, S, _ = hn.shape
    z = hn @ w_in
    offs = np.cumsum([DA_Q_W, DA_K_W, DA_V_W, RET_Q_W, RET_K_W, RET_V_W, RET_G_W, D_MODEL])
    qa, ka, va, qr, kr, vr, gr, ga, gb = jnp.split(z, [int(o) for o in offs], axis=-1)

    qa = rope(rms_norm(qa.reshape(B, S, 2 * DA_HEADS, DA_HEAD_DIM), da_q_norm), pos,
              ROPE_ROT_DIM, ROPE_THETA).reshape(B, S, DA_HEADS, 2, DA_HEAD_DIM)
    ka = rope(rms_norm(ka.reshape(B, S, 2 * DA_HEADS, DA_HEAD_DIM), da_k_norm), pos,
              ROPE_ROT_DIM, ROPE_THETA).reshape(B, S, DA_HEADS, 2, DA_HEAD_DIM)
    va = va.reshape(B, S, DA_HEADS, DA_V_DIM)
    lambda_init = 0.8 - 0.6 * math.exp(-0.3 * layer)
    lam = (jnp.exp(jnp.sum(lam_q1.astype(jnp.float32) * lam_k1.astype(jnp.float32)))
           - jnp.exp(jnp.sum(lam_q2.astype(jnp.float32) * lam_k2.astype(jnp.float32)))
           + lambda_init)
    oa = diff_attention(qa, ka, va, lam)
    ya = (rms_norm(oa, da_subln) * (1.0 - lambda_init)).reshape(B, S, DA_V_W)

    qr = rope(qr.reshape(B, S, RET_HEADS, RET_QK_DIM), pos, RET_QK_DIM, RET_ROPE_THETA)
    kr = rope(kr.reshape(B, S, RET_HEADS, RET_QK_DIM), pos, RET_QK_DIM, RET_ROPE_THETA)
    orr = retention(qr, kr, vr.reshape(B, S, RET_HEADS, RET_V_DIM))
    yr = (group_norm(orr).reshape(B, S, RET_V_W)
          * jax.nn.silu(gr.astype(jnp.float32))).astype(hn.dtype)

    merged = jax.nn.sigmoid(ga) * (ya @ w_proj_da) + jax.nn.sigmoid(gb) * (yr @ w_proj_ret)
    return merged @ w_out

def swiglu(x, w1, w3, w2):
    return (jax.nn.silu(x @ w1) * (x @ w3)) @ w2

def moe(hn, w_router, w1, w3, w2):
    B, S, D = hn.shape
    t = hn.reshape(B * S, D)
    logits = (t @ w_router).astype(jnp.float32)
    top_v, top_i = lax.top_k(logits, TOP_K)
    top_w = jax.nn.softmax(top_v, axis=-1)
    combine = jnp.sum(jax.nn.one_hot(top_i, N_EXPERTS, dtype=jnp.float32) * top_w[..., None], axis=1)
    out = jnp.zeros_like(t)
    for e in range(N_EXPERTS):
        out = out + combine[:, e:e + 1].astype(t.dtype) * swiglu(t, w1[e], w3[e], w2[e])
    return out.reshape(B, S, D)

def setup_inputs(seed: int = 0) -> dict:
    key = jax.random.key(seed)
    ks = jax.random.split(key, 24)
    f32 = jnp.float32

    def nrm(k, shape, fan_in):
        return jax.random.normal(k, shape, f32) * (fan_in ** -0.5)

    def gain(k, shape):
        return 1.0 + 0.05 * jax.random.normal(k, shape, f32)

    x = jax.random.normal(ks[0], (BATCH, SEQ, D_MODEL), f32)
    positions = jnp.broadcast_to(jnp.arange(SEQ, dtype=jnp.int32)[None, :], (BATCH, SEQ))
    return {
        "x": x,
        "positions": positions,
        "attn_norm": gain(ks[1], (DEPTH, D_MODEL)),
        "w_in": nrm(ks[2], (DEPTH, D_MODEL, IN_W), D_MODEL),
        "da_q_norm": gain(ks[3], (DEPTH, DA_HEAD_DIM)),
        "da_k_norm": gain(ks[4], (DEPTH, DA_HEAD_DIM)),
        "lam_q1": 0.1 * jax.random.normal(ks[5], (DEPTH, DA_HEAD_DIM), f32),
        "lam_k1": 0.1 * jax.random.normal(ks[6], (DEPTH, DA_HEAD_DIM), f32),
        "lam_q2": 0.1 * jax.random.normal(ks[7], (DEPTH, DA_HEAD_DIM), f32),
        "lam_k2": 0.1 * jax.random.normal(ks[8], (DEPTH, DA_HEAD_DIM), f32),
        "da_subln": gain(ks[9], (DEPTH, DA_V_DIM)),
        "w_proj_da": nrm(ks[10], (DEPTH, DA_V_W, D_MODEL), DA_V_W),
        "w_proj_ret": nrm(ks[11], (DEPTH, RET_V_W, D_MODEL), RET_V_W),
        "w_out": nrm(ks[12], (DEPTH, D_MODEL, D_MODEL), D_MODEL),
        "ffn_norm": gain(ks[13], (DEPTH, D_MODEL)),
        "dense_w1": nrm(ks[14], (N_DENSE, D_MODEL, D_FF), D_MODEL),
        "dense_w3": nrm(ks[15], (N_DENSE, D_MODEL, D_FF), D_MODEL),
        "dense_w2": nrm(ks[16], (N_DENSE, D_FF, D_MODEL), D_FF),
        "w_router": nrm(ks[17], (N_MOE, D_MODEL, N_EXPERTS), D_MODEL),
        "moe_w1": nrm(ks[18], (N_MOE, N_EXPERTS, D_MODEL, D_FF), D_MODEL),
        "moe_w3": nrm(ks[19], (N_MOE, N_EXPERTS, D_MODEL, D_FF), D_MODEL),
        "moe_w2": nrm(ks[20], (N_MOE, N_EXPERTS, D_FF, D_MODEL), D_FF),
    }

def reference(x, positions, attn_norm, w_in, da_q_norm, da_k_norm, lam_q1, lam_k1, lam_q2, lam_k2,
              da_subln, w_proj_da, w_proj_ret, w_out, ffn_norm, dense_w1, dense_w3, dense_w2,
              w_router, moe_w1, moe_w3, moe_w2):
    h = x
    for layer in range(DEPTH):
        hn = rms_norm(h, attn_norm[layer])
        h = h + token_mixers(hn, positions, layer, w_in[layer], da_q_norm[layer], da_k_norm[layer],
                             lam_q1[layer], lam_k1[layer], lam_q2[layer], lam_k2[layer],
                             da_subln[layer], w_proj_da[layer], w_proj_ret[layer], w_out[layer])
        hn = rms_norm(h, ffn_norm[layer])
        j = layer // 2
        if layer % 2 == 0:
            h = h + swiglu(hn, dense_w1[j], dense_w3[j], dense_w2[j])
        else:
            h = h + moe(hn, w_router[j], moe_w1[j], moe_w3[j], moe_w2[j])
    return h


_drawn_inputs = setup_inputs


def setup_inputs(seed=0):
    import zlib

    import numpy as np

    out = dict(_drawn_inputs(seed))
    spreads = {}
    factors = {}
    for name, (base, spread) in spreads.items():
        noise = np.random.default_rng([zlib.crc32(name.encode()), seed]).standard_normal(out[name].shape)
        drawn = base * np.exp(spread * noise) if base else spread * noise
        out[name] = __import__('jax').numpy.asarray(drawn.astype(out[name].dtype))
    for name, factor in factors.items():
        out[name] = (out[name] * factor).astype(out[name].dtype)
    return out
```

```python
import math
from contextlib import ExitStack

import numpy as np

import concourse.bass as bass
from concourse import mybir

F32 = mybir.dt.float32
F32R = mybir.dt.float32r
I32 = mybir.dt.int32
U32 = mybir.dt.uint32
ALU = mybir.AluOpType
ACT = mybir.ActivationFunctionType
AX = mybir.AxisListType

P = 128
SEQ = 256
TT = SEQ // P
D = 1024
KC = D // P
DEPTH = 2
HEADS = 4
HD = 64
VD = 128
AW = HEADS * VD
IN_W = 5120
FF = 2816
FC = FF // P
E = 8
EPS = 1e-6
DA_SCALE = HD ** -0.5
DA_THETA, RET_THETA = 500000.0, 10000.0
DA_HALF, RET_HALF = HD // 8, HD // 2
NF = DA_HALF + RET_HALF
MASKED = -1.0e30

UNIT = 2048
RAW, SPLIT = 6, 3
SLICES = FF // 256
IN_GROUPS = IN_W // 512
MIX_UNITS = 2 * IN_GROUPS + 4 + 4
FFN_UNITS = 2 * SLICES + FC // 2
MIX_BASE = [0, MIX_UNITS + FFN_UNITS]
DENSE_BASE = MIX_UNITS
MOE_BASE = MIX_BASE[1] + MIX_UNITS
OVER_BASE = MOE_BASE + E * FFN_UNITS
AHEAD = 2

ZQK, ZV, ZR, ZRV, ZG = 0, 2048, 3072, 4096, 5120
SGA, SGB = 6144, 8192
QKT, RETT = 10240, 12288
RIN = 13312
MIX_WORDS = RIN + HEADS * 384


def constants():
    i = np.arange(P)
    c = {}
    c["ident"] = np.eye(P, dtype=np.float32)
    c["mask"] = np.where(i[None, :] <= i[:, None], 0.0, MASKED).astype(np.float32)
    lg = np.log1p(-np.exp2(-5.0 - np.arange(HEADS)))
    rel = np.arange(SEQ)[None, :] - i[:, None]
    dec = np.where(rel[:, None] >= 0, np.exp(lg[None, :, None] * np.maximum(rel, 0)[:, None]), 0.0)
    c["decay"] = (dec * HD ** -0.5).astype(np.float32).reshape(P, HEADS * SEQ)
    f = np.concatenate([1.0 / np.power(np.float32(th), np.arange(n, dtype=np.float32) / np.float32(n))
                        for th, n in ((DA_THETA, DA_HALF), (RET_THETA, RET_HALF))]).astype(np.float32)
    c["freq"] = np.broadcast_to(f, (P, NF)).copy()
    c["iota"] = np.broadcast_to(i.astype(np.float32), (P, P)).copy()
    c["before"] = (i[:, None] < i[None, :]).astype(np.float32)
    return c


def build(nc, x, positions, attn_norm, w_in, da_q_norm, da_k_norm, lam_q1, lam_k1, lam_q2, lam_k2,
          da_subln, w_proj_da, w_proj_ret, w_out, ffn_norm, dense_w1, dense_w3, dense_w2, w_router,
          moe_w1, moe_w3, moe_w2, ident_d, mask_d, decay_d, freq_d, iota_d, before_d, out):
    ctx = ExitStack()
    with ctx:
        def sb(name, shape, dt=F32):
            return ctx.enter_context(nc.sbuf_tensor(name, shape, dt))

        def sem(name):
            return ctx.enter_context(nc.semaphore(name))

        arena_at = (nc.sbuf_base + 31) // 32 * 32
        mix = sb("mix", [P, MIX_WORDS])
        place = [arena_at]

        def over(name, words, dt=F32):
            t = nc.alloc_sbuf_tensor_at(name, [P, words], dt, offset=place[0])
            place[0] += 4 * words
            return t
        gT_h = over("gT_h", FC * SEQ, F32R)
        gT_l = over("gT_l", FC * SEQ, F32R)
        sgm = over("sgm", 2 * 512)
        gbuf = over("gbuf", 2 * 512)
        assert place[0] <= arena_at + 4 * MIX_WORDS
        place[0] = arena_at + 4 * (2 * FC * P)
        hn_h = over("hn_h", TT * D, F32R)
        hn_l = over("hn_l", TT * D, F32R)
        place[0] = arena_at + 4 * (2 * FC * P + 2 * TT * D)
        moe_gT_h = nc.alloc_sbuf_tensor_at("moe_gT_h", [P, FC * P], F32R, offset=arena_at)
        moe_gT_l = nc.alloc_sbuf_tensor_at("moe_gT_l", [P, FC * P], F32R, offset=arena_at + 4 * FC * P)
        moe_sgm = over("moe_sgm", 2 * 256)
        moe_gbuf = over("moe_gbuf", 2 * 256)
        sel_r = over("sel_r", 2 * TT * P, F32R)
        sel_f = over("sel_f", 2 * TT * P)
        selT = over("selT", 2 * TT * P)
        assert place[0] <= arena_at + 4 * MIX_WORDS

        raw = sb("raw", [P, RAW, UNIT])
        wh = sb("wh", [P, SPLIT, UNIT], F32R)
        wl = sb("wl", [P, SPLIT, UNIT], F32R)
        XT_h = sb("XT_h", [P, KC, SEQ], F32R)
        XT_l = sb("XT_l", [P, KC, SEQ], F32R)
        h = sb("h", [P, TT, D])
        xs = sb("xs", [P, TT * D])
        ident = sb("ident", [P, P])
        mask = sb("mask", [P, P])
        decay = sb("decay", [P, HEADS, SEQ])
        iota = sb("iota", [P, P])
        before = sb("before", [P, P])
        ones = sb("ones", [P, P])
        freq = sb("freq", [P, NF])
        pos_i = sb("pos_i", [P, TT], I32)
        pos_f = sb("pos_f", [P, TT])
        cos = sb("cos", [P, TT, NF])
        sin = sb("sin", [P, TT, NF])
        ang = sb("ang", [P, 3, TT, NF])
        g_attn = sb("g_attn", [P, DEPTH, KC])
        g_ffn = sb("g_ffn", [P, DEPTH, KC])
        g_moe = sb("g_moe", [P, D])
        g_qk = sb("g_qk", [P, DEPTH, 2, HD])
        g_sub = sb("g_sub", [P, DEPTH])
        g_subs = sb("g_subs", [P, DEPTH])
        lamv = sb("lamv", [P, 4, DEPTH, HD])
        lamp = sb("lamp", [P, 2, DEPTH, HD])
        lams = sb("lams", [P, 2, DEPTH])
        lame = sb("lame", [P, 2, DEPTH])
        lamn = sb("lamn", [P, DEPTH])
        wr = sb("wr", [P, KC, E])
        wr_h = sb("wr_h", [P, KC, E], F32R)
        wr_l = sb("wr_l", [P, KC, E], F32R)
        nhalf = sb("nhalf", [P, 32])
        ssq = sb("ssq", [P, 32])
        rst = sb("rst", [P, 32])
        mxs = sb("mxs", [P, 2, 8])
        nbs = sb("nbs", [P, 2, 8])
        sms = sb("sms", [P, 2, 8])
        rcs = sb("rcs", [P, 2, 8])
        mu = sb("mu", [P, 8])
        lg = sb("lg", [P, TT, E])
        top = sb("top", [P, TT, 8])
        tidx = sb("tidx", [P, TT, 8], U32)
        tif = sb("tif", [P, TT, 8])
        tdf = sb("tdf", [P, TT])
        te = sb("te", [P, TT])
        tw = sb("tw", [P, 3, TT])
        oh = sb("oh", [P, 2, TT, E])
        comb = sb("comb", [P, TT, E])
        routed = sb("routed", [P, TT, E])
        rank1 = sb("rank1", [P, TT, E])
        rank = sb("rank", [P, TT, E])
        rank2 = sb("rank2", [P, TT, E])
        okey = sb("okey", [P, 3, E])
        nover = sb("nover", [P, 1])
        otab = sb("otab", [P, 16], I32)

        ps = ctx.enter_context(nc.psum_tensor("ps", [P, 8, 512], F32))

        consts_in = sem("consts_in")
        x_in = sem("x_in")
        landed = [sem(f"landed{s}") for s in range(RAW)]
        hi_ready = sem("hi_ready")
        lo_ready = sem("lo_ready")
        unit_used = sem("unit_used")
        dchain = sem("dchain")
        sin_ready = sem("sin_ready")
        ang_ready = sem("ang_ready")
        lam_sum = sem("lam_sum")
        lam_exp = sem("lam_exp")
        pool_const = sem("pool_const")
        ms_ready = sem("ms_ready")
        rs_ready = sem("rs_ready")
        sq_done = sem("sq_done")
        xs_ready = sem("xs_ready")
        xt_tr = sem("xt_tr")
        xt_hi = sem("xt_hi")
        xt_lo = sem("xt_lo")
        in_evac = sem("in_evac")
        zqk_ready = sem("zqk_ready")
        zr_ready = sem("zr_ready")
        silu_ready = sem("silu_ready")
        zt_tr = sem("zt_tr")
        zt_cp = sem("zt_cp")
        ret_s = sem("ret_s")
        ret_w = sem("ret_w")
        ret_o = sem("ret_o")
        da_s = sem("da_s")
        nb_ready = sem("nb_ready")
        exp_done = sem("exp_done")
        pd_ready = sem("pd_ready")
        pd_tr = sem("pd_tr")
        pd_cp = sem("pd_cp")
        da_o = sem("da_o")
        osq = sem("osq")
        yr_ready = sem("yr_ready")
        ya_ready = sem("ya_ready")
        yt_tr = sem("yt_tr")
        yt_hi = sem("yt_hi")
        yt_lo = sem("yt_lo")
        proj_evac = sem("proj_evac")
        m_ready = sem("m_ready")
        mt_tr = sem("mt_tr")
        mt_hi = sem("mt_hi")
        mt_lo = sem("mt_lo")
        h_ready = sem("h_ready")
        sig_done = sem("sig_done")
        g_half = sem("g_half")
        g_ready = sem("g_ready")
        g_tr = sem("g_tr")
        g_hi = sem("g_hi")
        g_lo = sem("g_lo")
        wr_hi = sem("wr_hi")
        wr_lo = sem("wr_lo")
        hn_full = sem("hn_full")
        hn_hi = sem("hn_hi")
        hn_lo = sem("hn_lo")
        logit = sem("logit")
        te_in = sem("te_in")
        te_out = sem("te_out")
        routed_ready = sem("routed_ready")
        ranked = sem("ranked")
        table_ready = sem("table_ready")
        sel_ready = sem("sel_ready")
        gat = sem("gat")
        gat_hi = sem("gat_hi")
        gat_lo = sem("gat_lo")
        st_tr = sem("st_tr")
        st_cp = sem("st_cp")
        y_cp = sem("y_cp")
        sc_done = sem("sc_done")
        h_add = sem("h_add")
        stored = sem("stored")

        w_in_v = [w_in[l].rearrange("(c p) n -> p c n", p=P) for l in range(DEPTH)]
        pr_v = [w_proj_ret[l].rearrange("(c p) n -> p c n", p=P) for l in range(DEPTH)]
        pd_v = [w_proj_da[l].rearrange("(c p) n -> p c n", p=P) for l in range(DEPTH)]
        wo_v = [w_out[l].rearrange("(c p) n -> p c n", p=P) for l in range(DEPTH)]
        dn_v = [w[0].rearrange("(c p) n -> p c n", p=P) for w in (dense_w1, dense_w3, dense_w2)]
        me_v = [w[0].rearrange("e (c p) n -> e p c n", p=P) for w in (moe_w1, moe_w3, moe_w2)]

        def mixer_unit(l, u):
            if u < 2 * IN_GROUPS:
                g, half = divmod(u, 2)
                return [w_in_v[l][:, half * 4 + 2 * a:half * 4 + 2 * a + 2, g * 512:(g + 1) * 512] for a in (0, 1)]
            u -= 2 * IN_GROUPS
            if u < 4:
                v = (pr_v if u < 2 else pd_v)[l]
                n = u % 2
                return [v[:, 2 * a:2 * a + 2, n * 512:(n + 1) * 512] for a in (0, 1)]
            n, half = divmod(u - 4, 2)
            return [wo_v[l][:, half * 4 + 2 * a:half * 4 + 2 * a + 2, n * 512:(n + 1) * 512] for a in (0, 1)]

        def ffn_unit(w1, w3, w2, slot, u):
            if u < 2 * SLICES:
                j, half = divmod(u, 2)
                to = raw[:, slot, :].rearrange("p (c w n) -> p c w n", c=4, w=2)
                return [(to[:, :, a, :], w[:, half * 4:half * 4 + 4, j * 256:(j + 1) * 256])
                        for a, w in ((0, w1), (1, w3))]
            c = 2 * (u - 2 * SLICES)
            return [(raw[:, slot, a * D:(a + 1) * D], w2[:, c + a, :]) for a in (0, 1)]

        class Units:
            def __init__(self, base, i=None, per=0, raw_slots=RAW):
                self.base, self.i, self.per, self.raw_slots = base, i, per, raw_slots
                assert i is None or (per % raw_slots == 0 and per % SPLIT == 0)

            def at(self, const, per):
                return const if self.i is None else const + self.i * per

            def count(self, j):
                return self.at(self.base + j + 1, self.per)

            def before(self, j, n):
                c = self.base + j + 1 - n
                return None if self.i is None and c < 1 else self.at(c, self.per)

            def split_slot(self, j):
                return (self.base + j) % SPLIT

            def raw_slot(self, j):
                return (self.base + j) % self.raw_slots

            def landed(self, j):
                n, s = self.base + j, self.raw_slot(j)
                if self.raw_slots == RAW:
                    c = n // RAW + 1
                else:
                    c = len([m for m in range(OVER_BASE) if m % RAW == s])
                    c += len([m for m in range(OVER_BASE, n + 1) if m % SPLIT == s])
                return self.at(32 * c, 32 * (self.per // self.raw_slots))

        def load_unit(eng, U, j, pairs):
            v = U.before(j, U.raw_slots)
            if v is not None:
                eng.wait_ge(lo_ready, v)
            for to, of in pairs:
                eng.dma_start(to, of).then_inc(landed[U.raw_slot(j)], 16)

        def split_hi(act, U, j):
            act.wait_ge(landed[U.raw_slot(j)], U.landed(j))
            v = U.before(j, SPLIT)
            if v is not None:
                act.wait_ge(unit_used, v)
            nc.scalar.activation(wh[:, U.split_slot(j), :], raw[:, U.raw_slot(j), :], ACT.Copy).then_inc(hi_ready, 1)

        def split_lo(dve, U, j):
            dve.wait_ge(hi_ready, U.count(j))
            v = U.before(j, SPLIT)
            if v is not None:
                dve.wait_ge(unit_used, v)
            s = U.split_slot(j)
            nc.vector.tensor_tensor(wl[:, s, :], raw[:, U.raw_slot(j), :], wh[:, s, :].bitcast(F32),
                                    ALU.subtract).then_inc(lo_ready, 1)

        def product(o, xh, xl, bh, bl, start, stop):
            nc.tensor.matmul(o, xh, bh, start=start, stop=False)
            nc.tensor.matmul(o, xh, bl, start=False, stop=False)
            return nc.tensor.matmul(o, xl, bh, start=False, stop=stop)

        def gemm_unit(pe, U, j, outs, xT, chunks, start, stop):
            pe.wait_ge(lo_ready, U.count(j))
            s = U.split_slot(j)
            for a, c in enumerate(chunks):
                for o, cols in outs:
                    last = product(o, xT[0][:, c, cols], xT[1][:, c, cols],
                                   wh[:, s, a * 512:(a + 1) * 512], wl[:, s, a * 512:(a + 1) * 512],
                                   start and a == 0, stop and a == len(chunks) - 1)
            last.then_inc(unit_used, 1)

        tok = [slice(t * P, (t + 1) * P) for t in range(TT)]
        gT3 = [g[:, :].rearrange("p (c n) -> p c n", c=FC) for g in (gT_h, gT_l)]
        moe_gT3 = [g[:, :].rearrange("p (c n) -> p c n", c=FC) for g in (moe_gT_h, moe_gT_l)]
        xs3 = xs[:, :].rearrange("p (t n) -> p t n", t=TT)

        def mx(off, words):
            return mix[:, off:off + words]

        block = ctx.enter_context(nc.Block())

        @block.sync
        def _(sp):
            sp.dma_start(h[:, :, :], x[0].rearrange("(t p) d -> p t d", p=P)).then_inc(x_in, 16)
            for l in range(DEPTH):
                U = Units(MIX_BASE[l])
                for u in range(MIX_UNITS):
                    to = raw[:, U.raw_slot(u), :].rearrange("p (a c n) -> p a c n", a=2, c=2)
                    load_unit(sp, U, u, [(to[:, a], s) for a, s in enumerate(mixer_unit(l, u))])
                if l == 0:
                    U = Units(DENSE_BASE)
                    for u in range(FFN_UNITS):
                        load_unit(sp, U, u, ffn_unit(*dn_v, U.raw_slot(u), u))
            with sp.Fori(0, E // 2) as i:
                U = Units(MOE_BASE, i, 2 * FFN_UNITS)
                for half in range(2):
                    w = [v[2 * i + half] for v in me_v]
                    for u in range(FFN_UNITS):
                        j = half * FFN_UNITS + u
                        load_unit(sp, U, j, ffn_unit(*w, U.raw_slot(j), u))
            sp.wait_ge(table_ready, 1)
            n_over = sp.value_load(otab[0:1, 0:1], min_val=0, max_val=3)
            with sp.If(n_over > 0):
                with sp.Fori(0, n_over) as k:
                    e = sp.value_load(otab[0:1, bass.ds(k + 8, 1)], min_val=0, max_val=E - 1)
                    U = Units(OVER_BASE, k, FFN_UNITS, SPLIT)
                    w = [v[e] for v in me_v]
                    for u in range(FFN_UNITS):
                        load_unit(sp, U, u, ffn_unit(*w, U.raw_slot(u), u))
            sp.wait_ge(h_add, n_over * 4 + 4 * E)
            sp.dma_start(out[0].rearrange("(t p) d -> p t d", p=P), h[:, :, :]).then_inc(stored, 16)
            sp.wait_ge(stored, 16)

        @block.gpsimd
        def _(pool):
            nc.gpsimd.memset(nhalf[:, :], -0.5).then_inc(pool_const, 1)
            nc.gpsimd.memset(ones[:, :], 1.0).then_inc(pool_const, 1)
            pool.wait_ge(pool_const, 2)
            widths = [2, 32, 8, 4, 4, 2] * DEPTH
            for n, w in enumerate(widths):
                pool.wait_ge(ms_ready, n + 1)
                nc.gpsimd.tensor_tensor(rst[:, 0:w], ssq[:, 0:w], nhalf[:, 0:w], ALU.pow).then_inc(rs_ready, 1)

        @block.scalar
        def _(act):
            loads = [(pos_i[:, :], positions[0].rearrange("(t p) -> p t", p=P)),
                     (freq[:, :], freq_d), (ident[:, :], ident_d),
                     (g_attn[:, :, :], attn_norm.rearrange("l (c p) -> p l c", p=P)),
                     (mask[:, :], mask_d), (decay[:, :, :], decay_d.rearrange("p (h q) -> p h q", h=HEADS)),
                     (iota[:, :], iota_d), (before[:, :], before_d),
                     (g_ffn[:, :, :], ffn_norm.rearrange("l (c p) -> p l c", p=P)),
                     (g_moe[:, :], ffn_norm[1:2, :].to_broadcast([P, D])),
                     (g_sub[:, :], da_subln.rearrange("l p -> p l")),
                     (wr[:, :, :], w_router[0].rearrange("(c p) e -> p c e", p=P))]
            for l in range(DEPTH):
                loads += [(g_qk[:, l, 0, :], da_q_norm[l:l + 1, :].to_broadcast([P, HD])),
                          (g_qk[:, l, 1, :], da_k_norm[l:l + 1, :].to_broadcast([P, HD]))]
                loads += [(lamv[:, a, l, :], v[l:l + 1, :].to_broadcast([P, HD]))
                          for a, v in enumerate((lam_q1, lam_k1, lam_q2, lam_k2))]
            with nc.allow_non_contiguous_dma("small gains"):
                for to, of in loads:
                    act.dma_start(to, of).then_inc(consts_in, 16)
            assert len(loads) == NLOADS
            act.wait_ge(consts_in, 16 * NLOADS)
            act.wait_ge(ang_ready, 1)
            nc.scalar.activation(sin[:, :, :], ang[:, 0], ACT.Sin)
            nc.scalar.activation(cos[:, :, :], ang[:, 1], ACT.Sin).then_inc(sin_ready, 1)
            act.wait_ge(lam_sum, 1)
            nc.scalar.activation(lame[:, :, :], lams[:, :, :], ACT.Exp).then_inc(lam_exp, 1)
            nc.scalar.activation(wr_h[:, :, :], wr[:, :, :], ACT.Copy).then_inc(wr_hi, 1)

            split_to = [0]

            def split_until(U, j):
                while split_to[0] <= U.base + j:
                    split_hi(act, Units(0), split_to[0])
                    split_to[0] += 1

            def norm_stage(n, gain):
                if n == 0:
                    act.wait_ge(x_in, 16)
                else:
                    act.wait_ge(h_ready, n)
                for t in range(TT):
                    nc.scalar.activation(xs3[:, t, :], h[:, t, :], ACT.Square, accum_out=ssq[:, t:t + 1])\
                        .then_inc(sq_done, 1)
                for r in range(4):
                    act.wait_ge(xt_tr, 4 * n + r + 1)
                    for a in range(2):
                        c = 2 * r + a
                        ins = nc.scalar.activation(XT_h[:, c, :], ps[:, 4 + r, a * SEQ:(a + 1) * SEQ], ACT.Copy,
                                                   scale=gain[:, c:c + 1])
                    ins.then_inc(xt_hi, 1)

            def mixers(l):
                U = Units(MIX_BASE[l])
                split_until(U, AHEAD - 1)
                norm_stage(2 * l, g_attn[:, l, :])

                def evac(g):
                    act.wait_ge(unit_used, U.count(2 * g + 1))
                    acc = ps[:, 2 * (g % 2):2 * (g % 2) + 2, :]
                    if g < 2:
                        to = mx(ZQK, 2048).rearrange("p (t n) -> p t n", t=TT)[:, :, g * 512:(g + 1) * 512]
                    elif g < 6:
                        to = mx((ZV, ZR, ZRV, ZG)[g - 2], 1024).rearrange("p (t n) -> p t n", t=TT)
                    else:
                        a = (g - 6) % 2
                        to = mx((SGA, SGB)[(g - 6) // 2], 2048)\
                            .rearrange("p (t n) -> p t n", t=TT)[:, :, a * 512:(a + 1) * 512]
                    if g == 5:
                        nc.scalar.activation(mx(RIN, 1024).rearrange("p (t n) -> p t n", t=TT), acc, ACT.Sigmoid)
                    nc.scalar.activation(to, acc, ACT.Copy if g < 6 else ACT.Sigmoid).then_inc(in_evac, 1)

                qkT = mx(QKT, 2048).rearrange("p (r n) -> p r n", r=4)
                retT = mx(RETT, 1024).rearrange("p (r n) -> p r n", r=2)
                for g in range(IN_GROUPS):
                    if g > 0:
                        evac(g - 1)
                    if g == 9:
                        for r in range(6):
                            act.wait_ge(zt_tr, 6 * l + r + 1)
                            nc.scalar.activation(qkT[:, r] if r < 4 else retT[:, r - 4], ps[:, 4 + r % 4, :],
                                                 ACT.Copy).then_inc(zt_cp, 1)
                    split_until(U, 2 * g + 1 + AHEAD)
                evac(IN_GROUPS - 1)
                e0 = mx(ZR, 1024).rearrange("p (a n) -> p a n", a=8)
                e1 = mx(ZQK, 2048).rearrange("p (a n) -> p a n", a=8)
                s0 = ps[:, 0:2, :].rearrange("p b (h n) -> p (b h) n", h=4)
                s1 = ps[:, 2:6, :].rearrange("p b (h n) -> p (b h) n", h=2)
                for t, (e, s) in enumerate(((e0, s0), (e1, s1))):
                    act.wait_ge(nb_ready, 2 * l + t + 1)
                    for a in range(8):
                        ins = nc.scalar.activation(e[:, a], s[:, a], ACT.Exp, bias=nbs[:, t, a:a + 1],
                                                   scale=DA_SCALE, accum_out=sms[:, t, a:a + 1])
                        ins.then_inc(exp_done, 1)
                pdT = mx(QKT, 1536).rearrange("p (r n) -> p r n", r=3)
                for r in range(3):
                    act.wait_ge(pd_tr, 3 * l + r + 1)
                    nc.scalar.activation(pdT[:, r], ps[:, (0, 2, 3)[r], :], ACT.Copy).then_inc(pd_cp, 1)
                for t in range(TT):
                    act.wait_ge(da_o, 2 * l + t + 1)
                    if t == 0:
                        act.wait_ge(yr_ready, l + 1)
                    nc.scalar.activation(mx(RIN + 512 * t, 512), ps[:, (1, 4)[t], :], ACT.Square).then_inc(osq, 1)
                for r in range(4):
                    act.wait_ge(yt_tr, 4 * l + r + 1)
                    c, bank = ((4, 6), (6, 7), (0, 4), (2, 5))[r]
                    src = ps[:, bank, :].rearrange("p (a n) -> p a n", a=2)
                    nc.scalar.activation(XT_h[:, c:c + 2, :], src, ACT.Copy,
                                         scale=1.0 if r < 2 else g_subs[:, l:l + 1]).then_inc(yt_hi, 1)
                for u in range(4):
                    split_until(U, 2 * IN_GROUPS + u + AHEAD)
                for r in range(4):
                    act.wait_ge(mt_tr, 4 * l + r + 1)
                    nc.scalar.activation(XT_h[:, 2 * r:2 * r + 2, :],
                                         ps[:, 4 + r, :].rearrange("p (a n) -> p a n", a=2), ACT.Copy)\
                        .then_inc(mt_hi, 1)
                split_until(U, MIX_UNITS - 1)

            def sigmoid_slice(products, bank, buf):
                act.wait_ge(unit_used, products)
                nc.scalar.activation(buf, bank, ACT.Sigmoid).then_inc(sig_done, 1)

            def dense():
                split_until(Units(DENSE_BASE), AHEAD - 1)
                norm_stage(1, g_ffn[:, 0, :])

                def sigm(j):
                    b = 2 * (j % 2)
                    sigmoid_slice(Units(DENSE_BASE).count(2 * j + 1), ps[:, b:b + 2, 0:256],
                                  sgm[:, (j % 2) * 512:(j % 2 + 1) * 512].rearrange("p (t n) -> p t n", t=TT))

                def hi(j):
                    act.wait_ge(g_tr, j + 1)
                    nc.scalar.activation(gT3[0][:, 2 * j:2 * j + 2, :],
                                         ps[:, 4 + j % 2, :].rearrange("p (a n) -> p a n", a=2), ACT.Copy)\
                        .then_inc(g_hi, 1)
                for j in range(SLICES):
                    if j >= 1:
                        sigm(j - 1)
                    if j >= 2:
                        hi(j - 2)
                    split_until(Units(DENSE_BASE), 2 * j + 1 + AHEAD)
                for u in range(SLICES):
                    if u == 0:
                        sigm(SLICES - 1)
                        hi(SLICES - 2)
                    if u == 1:
                        hi(SLICES - 1)
                    split_until(Units(DENSE_BASE), 2 * SLICES + u + AHEAD)

            mixers(0)
            dense()
            mixers(1)
            split_until(Units(MOE_BASE), -1)
            norm_stage(3, g_ffn[:, 1, :])
            act.wait_ge(hn_full, 1)
            nc.scalar.activation(hn_h[:, :], xs[:, :], ACT.Copy).then_inc(hn_hi, 1)
            act.wait_ge(te_in, 1)
            nc.scalar.activation(te[:, :], tdf[:, :], ACT.Exp).then_inc(te_out, 1)

            def gather_hi(p, b):
                act.wait_ge(st_tr, p + 1)
                nc.scalar.activation(selT[:, b * SEQ:(b + 1) * SEQ], ps[:, 4, 0:SEQ], ACT.Copy).then_inc(st_cp, 1)
                for r in range(2):
                    act.wait_ge(gat, p * 4 + r + 1)
                    nc.scalar.activation(XT_h[:, 4 * r:4 * r + 4, tok[b]],
                                         ps[:, 6 + r, :].rearrange("p (c n) -> p c n", c=4), ACT.Copy)\
                        .then_inc(gat_hi, 1)

            def sigm(U, j0, j):
                sigmoid_slice(U.count(j0 + 2 * j + 1), ps[:, j % 2, 0:256], moe_sgm[:, (j % 2) * 256:(j % 2 + 1) * 256])

            def hi(q, j):
                act.wait_ge(g_tr, q * SLICES + j + 1)
                nc.scalar.activation(moe_gT3[0][:, 2 * j:2 * j + 2, :],
                                     ps[:, 4 + j % 2, 0:256].rearrange("p (a n) -> p a n", a=2), ACT.Copy)\
                    .then_inc(g_hi, 1)

            def expert(p, b, U, j0, first, last_split, gather_next):
                if first:
                    gather_hi(p, b)
                    for j in range(AHEAD):
                        split_hi(act, U, j0 + j)
                for j in range(SLICES):
                    if j >= 1:
                        sigm(U, j0, j - 1)
                    if j >= 2:
                        hi(p + 1, j - 2)
                    for a in range(2):
                        split_hi(act, U, j0 + 2 * j + AHEAD + a)
                for u in range(SLICES):
                    if u == 0:
                        sigm(U, j0, SLICES - 1)
                        hi(p + 1, SLICES - 2)
                        if gather_next:
                            gather_hi(p + 1, 1 - b)
                    if u == 1:
                        hi(p + 1, SLICES - 1)
                    if 2 * SLICES + u + AHEAD <= last_split:
                        split_hi(act, U, j0 + 2 * SLICES + u + AHEAD)
                act.wait_ge(unit_used, U.count(j0 + FFN_UNITS - 1))
                nc.scalar.activation(xs3[:, b, :].rearrange("p (a n) -> p a n", a=2), ps[:, 2:4, :], ACT.Copy)\
                    .then_inc(y_cp, 1)

            with act.Fori(0, E // 2) as i:
                U = Units(MOE_BASE, i, 2 * FFN_UNITS)
                expert(2 * i, 0, U, 0, True, FFN_UNITS + 1, True)
                expert(2 * i + 1, 1, U, FFN_UNITS, False, FFN_UNITS - 1, False)
            act.wait_ge(table_ready, 1)
            n_over = act.value_load(otab[0:1, 0:1], min_val=0, max_val=3)
            with act.If(n_over > 0):
                with act.Fori(0, n_over) as k:
                    expert(k + E, 0, Units(OVER_BASE, k, FFN_UNITS, SPLIT), 0, True, FFN_UNITS - 1, False)

        @block.tensor
        def _(pe):
            pe.wait_ge(consts_in, 16 * NLOADS)

            def transpose(o, i):
                return nc.tensor.transpose(o, i, ident[:, :])

            def norm_stage(n):
                pe.wait_ge(xs_ready, n + 1)
                for r in range(4):
                    for a in range(2):
                        for t in range(TT):
                            c = 2 * r + a
                            last = transpose(ps[:, 4 + r, a * SEQ + t * P:a * SEQ + (t + 1) * P],
                                             xs3[:, t, c * P:(c + 1) * P])
                    last.then_inc(xt_tr, 1)

            def mixers(l):
                U = Units(MIX_BASE[l])
                norm_stage(2 * l)
                zqk = mx(ZQK, 2048).rearrange("p (t n) -> p t n", t=TT)
                zr = mx(ZR, 1024).rearrange("p (t n) -> p t n", t=TT)
                for g in range(IN_GROUPS):
                    if g == 0:
                        pe.wait_ge(xt_lo, 8 * l + 4)
                    if g >= 2:
                        pe.wait_ge(in_evac, IN_GROUPS * l + g - 1)
                    outs = [(ps[:, 2 * (g % 2) + t, :], tok[t]) for t in range(TT)]
                    for half in range(2):
                        gemm_unit(pe, U, 2 * g + half, outs, (XT_h, XT_l), range(4 * half, 4 * half + 4),
                                         half == 0, half == 1)
                    if g == 8:
                        pe.wait_ge(zqk_ready, l + 1)
                        for r in range(6):
                            if r == 4:
                                pe.wait_ge(zr_ready, l + 1)
                            if r >= 4:
                                pe.wait_ge(zt_cp, 6 * l + r - 3)
                            for a in range(2):
                                for t in range(TT):
                                    src = zqk[:, t, (2 * r + a) * P:(2 * r + a + 1) * P] if r < 4 else \
                                        zr[:, t, (2 * (r - 4) + a) * P:(2 * (r - 4) + a + 1) * P]
                                    last = transpose(ps[:, 4 + r % 4, (a * 2 + t) * P:(a * 2 + t + 1) * P], src)
                            last.then_inc(zt_tr, 1)
                qkT = mx(QKT, 2048).rearrange("p (b n) -> p b n", b=8)
                retT = mx(RETT, 1024).rearrange("p (b n) -> p b n", b=4)
                pe.wait_ge(zt_cp, 6 * l + 6)
                for hd in range(HEADS):
                    rows = slice((hd % 2) * HD, (hd % 2 + 1) * HD)
                    q, k = retT[rows, hd // 2], retT[rows, 2 + hd // 2]
                    nc.tensor.matmul(ps[:, 4 + hd, 0:SEQ], k[:, 0:P], q, start=True, stop=True)
                    nc.tensor.matmul(ps[:, 4 + hd, SEQ:SEQ + P], k[:, P:SEQ], q[:, P:SEQ], start=True, stop=True)\
                        .then_inc(ret_s, 1)
                for t in range(TT):
                    n = P * (t + 1)
                    if t == 0:
                        pe.wait_ge(in_evac, IN_GROUPS * l + 9)
                    else:
                        pe.wait_ge(in_evac, IN_GROUPS * l + 10)
                        pe.wait_ge(ret_w, 4 * l + 2)
                    for hd in range(HEADS):
                        for c in range(2):
                            rows = slice(c * HD, (c + 1) * HD)
                            if t == 0:
                                o = ps[:, c, hd * P:(hd + 1) * P]
                            else:
                                o = ps[:, 2 + 2 * c + hd // 2, (hd % 2) * SEQ:(hd % 2 + 1) * SEQ]
                            last = nc.tensor.matmul(o, qkT[rows, hd, tok[t]], qkT[rows, 4 + hd, 0:n],
                                                    start=True, stop=True)
                            if hd == HEADS - 1:
                                last.then_inc(da_s, 1)
                pe.wait_ge(ret_w, 4 * l + 4)
                rin = mx(RIN, HEADS * 384).rearrange("p (h n) -> p h n", h=HEADS)
                rv = mx(ZRV, 1024).rearrange("p (t n) -> p t n", t=TT)
                va = mx(ZV, 1024).rearrange("p (t n) -> p t n", t=TT)
                for hd in range(HEADS):
                    cols = slice(hd * VD, (hd + 1) * VD)
                    nc.tensor.matmul(ps[:, 6, cols], rin[:, hd, 0:P], rv[:, 0, cols], start=True, stop=True)
                    nc.tensor.matmul(ps[:, 7, cols], rin[:, hd, P:SEQ], rv[:, 0, cols], start=True, stop=False)
                    last = nc.tensor.matmul(ps[:, 7, cols], rin[:, hd, SEQ:SEQ + P], rv[:, 1, cols],
                                            start=False, stop=True)
                last.then_inc(ret_o, 1)
                pd0 = mx(ZR, 512).rearrange("p (h n) -> p h n", h=4)
                pd1 = mx(ZQK, 1024).rearrange("p (h n) -> p h n", h=4)
                pdT = mx(QKT, 1536).rearrange("p (b n) -> p b n", b=12)
                pe.wait_ge(pd_ready, 2 * l + 1)
                for hd in range(HEADS):
                    last = transpose(ps[:, 0, hd * P:(hd + 1) * P], pd0[:, hd])
                last.then_inc(pd_tr, 1)
                pe.wait_ge(pd_ready, 2 * l + 2)
                for r in range(2):
                    for a in range(4):
                        last = transpose(ps[:, 2 + r, a * P:(a + 1) * P], pd1[:, 2 * r + a // 2, tok[a % 2]])
                    last.then_inc(pd_tr, 1)
                pe.wait_ge(pd_cp, 3 * l + 1)
                for hd in range(HEADS):
                    cols = slice(hd * VD, (hd + 1) * VD)
                    last = nc.tensor.matmul(ps[:, 1, cols], pdT[:, hd], va[:, 0, cols], start=True, stop=True)
                last.then_inc(da_o, 1)
                pe.wait_ge(pd_cp, 3 * l + 3)
                for hd in range(HEADS):
                    cols = slice(hd * VD, (hd + 1) * VD)
                    nc.tensor.matmul(ps[:, 4, cols], pdT[:, 4 + 2 * hd], va[:, 0, cols], start=True, stop=False)
                    last = nc.tensor.matmul(ps[:, 4, cols], pdT[:, 5 + 2 * hd], va[:, 1, cols],
                                            start=False, stop=True)
                last.then_inc(da_o, 1)
                yv = xs[:, :].rearrange("p (m t n) -> p m t n", m=2, t=TT)
                for r in range(4):
                    m = 1 if r < 2 else 0
                    if r % 2 == 0:
                        pe.wait_ge(yr_ready if m else ya_ready, l + 1)
                    for a in range(2):
                        for t in range(TT):
                            c = 2 * (r % 2) + a
                            last = transpose(ps[:, (6, 7, 4, 5)[r], (a * 2 + t) * P:(a * 2 + t + 1) * P],
                                             yv[:, m, t, c * P:(c + 1) * P])
                    last.then_inc(yt_tr, 1)
                for u in range(4):
                    if u == 0:
                        pe.wait_ge(yt_lo, 4 * l + 2)
                    if u == 2:
                        pe.wait_ge(yt_lo, 4 * l + 4)
                    if u >= 2:
                        pe.wait_ge(proj_evac, 2 * l + u - 1)
                    outs = [(ps[:, 2 * (u % 2) + t, :], tok[t]) for t in range(TT)]
                    c0 = 4 if u < 2 else 0
                    gemm_unit(pe, U, 2 * IN_GROUPS + u, outs, (XT_h, XT_l), range(c0, c0 + 4), True, True)
                pe.wait_ge(m_ready, l + 1)
                mg = mx(SGA, 2048).rearrange("p (t n) -> p t n", t=TT)
                for r in range(4):
                    for a in range(2):
                        for t in range(TT):
                            c = 2 * r + a
                            last = transpose(ps[:, 4 + r, (a * 2 + t) * P:(a * 2 + t + 1) * P],
                                             mg[:, t, c * P:(c + 1) * P])
                    last.then_inc(mt_tr, 1)
                pe.wait_ge(mt_lo, 4 * l + 4)
                for n in range(2):
                    outs = [(ps[:, 2 * n + t, :], tok[t]) for t in range(TT)]
                    for half in range(2):
                        gemm_unit(pe, U, 2 * IN_GROUPS + 4 + 2 * n + half, outs, (XT_h, XT_l),
                                         range(4 * half, 4 * half + 4), half == 0, half == 1)

            def dense():
                U = Units(DENSE_BASE)
                norm_stage(1)
                pe.wait_ge(xt_lo, 8)

                def g_transposes(j):
                    pe.wait_ge(g_ready, j + 1)
                    if j >= 2:
                        pe.wait_ge(g_lo, j - 1)
                    gv = gbuf[:, (j % 2) * 512:(j % 2 + 1) * 512].rearrange("p (t n) -> p t n", t=TT)
                    for a in range(2):
                        for t in range(TT):
                            last = transpose(ps[:, 4 + j % 2, (a * 2 + t) * P:(a * 2 + t + 1) * P],
                                             gv[:, t, a * P:(a + 1) * P])
                    last.then_inc(g_tr, 1)
                for j in range(SLICES):
                    if j >= 2:
                        pe.wait_ge(g_ready, j - 1)
                    outs = [(ps[:, 2 * (j % 2) + t, :], tok[t]) for t in range(TT)]
                    for half in range(2):
                        gemm_unit(pe, U, 2 * j + half, outs, (XT_h, XT_l), range(4 * half, 4 * half + 4),
                                         half == 0, half == 1)
                    if j >= 1:
                        g_transposes(j - 1)
                for u in range(SLICES):
                    pe.wait_ge(g_lo, u + 1)
                    down_unit(pe, U, 2 * SLICES + u, [((6, 7), tok[0]), ((2, 3), tok[1])], gT3, u)
                    if u == 0:
                        g_transposes(SLICES - 1)

            def down_unit(pe, U, j, outs, gT, u):
                pe.wait_ge(lo_ready, U.count(j))
                s = U.split_slot(j)
                for a in range(2):
                    for banks, cols in outs:
                        for n in range(2):
                            b = slice(a * D + n * 512, a * D + (n + 1) * 512)
                            last = product(ps[:, banks[n], :], gT[0][:, 2 * u + a, cols], gT[1][:, 2 * u + a, cols],
                                           wh[:, s, b], wl[:, s, b], u == 0 and a == 0, u == SLICES - 1 and a == 1)
                last.then_inc(unit_used, 1)

            mixers(0)
            dense()
            mixers(1)
            norm_stage(3)
            pe.wait_ge(xt_lo, 16)
            pe.wait_ge(wr_lo, 1)
            for t in range(TT):
                o = ps[:, 0, t * E:(t + 1) * E]
                for c in range(KC):
                    product(o, XT_h[:, c, tok[t]], XT_l[:, c, tok[t]], wr_h[:, c, :], wr_l[:, c, :], c == 0, False)
                    last = nc.tensor.matmul(o, XT_l[:, c, tok[t]], wr_l[:, c, :], start=False, stop=c == KC - 1)
            last.then_inc(logit, 1)
            pe.wait_ge(routed_ready, 1)
            pe.wait_ge(pool_const, 2)
            nc.tensor.matmul(ps[:, 1, 0:E], before[:, :], routed[:, 0, :], start=True, stop=True)
            nc.tensor.matmul(ps[:, 1, E:2 * E], before[:, :], routed[:, 1, :], start=True, stop=False)
            nc.tensor.matmul(ps[:, 1, E:2 * E], ones[:, :], routed[:, 0, :], start=False, stop=True)
            nc.tensor.matmul(ps[:, 1, 2 * E:3 * E], ones[:, :], routed[:, 0, :], start=True, stop=False)
            nc.tensor.matmul(ps[:, 1, 2 * E:3 * E], ones[:, :], routed[:, 1, :], start=False, stop=True)\
                .then_inc(ranked, 1)
            pe.wait_ge(hn_lo, 1)

            def gather(p, b):
                pe.wait_ge(sel_ready, p + 1)
                for t in range(TT):
                    last = transpose(ps[:, 4, tok[t]], sel_f[:, (2 * b + t) * P:(2 * b + t + 1) * P])
                last.then_inc(st_tr, 1)
                for r in range(4):
                    if r >= 2:
                        pe.wait_ge(gat_hi, p * 2 + r - 1)
                    hn = (hn_h, hn_l)[r // 2][:, :].rearrange("p (t n) -> p t n", t=TT)
                    for a in range(4):
                        c = 4 * (r % 2) + a
                        for t in range(TT):
                            last = nc.tensor.matmul(ps[:, 6 + r % 2, a * P:(a + 1) * P], hn[:, t, c * P:(c + 1) * P],
                                                    sel_r[:, (2 * b + t) * P:(2 * b + t + 1) * P],
                                                    start=t == 0, stop=t == TT - 1)
                    last.then_inc(gat, 1)

            def g_transposes(p, j, gathered=False):
                if gathered:
                    pe.wait_ge(st_cp, p + 2)
                pe.wait_ge(g_ready, (p + 1) * SLICES + j + 1)
                if j >= 2:
                    pe.wait_ge(g_lo, (p + 1) * SLICES + j - 1)
                if j == 0:
                    pe.wait_ge(st_cp, p + 1)
                for a in range(2):
                    last = transpose(ps[:, 4 + j % 2, a * P:(a + 1) * P],
                                     moe_gbuf[:, (j % 2) * 256 + a * P:(j % 2) * 256 + (a + 1) * P])
                last.then_inc(g_tr, 1)

            def scatter(p, b):
                pe.wait_ge(y_cp, p + 1)
                for r in range(4):
                    t, n = divmod(r, 2)
                    if r >= 2:
                        pe.wait_ge(h_add, p * 4 + r - 1)
                    nc.tensor.matmul(ps[:, 6 + r % 2, :], selT[:, b * SEQ + t * P:b * SEQ + (t + 1) * P],
                                     xs3[:, b, n * 512:(n + 1) * 512], start=True, stop=True).then_inc(sc_done, 1)

            def expert(p, b, U, j0, first, scatter_prev, gather_next, scatter_here):
                if first:
                    gather(p, b)
                pe.wait_ge(gat_lo, p * 2 + 2)
                for j in range(SLICES):
                    if j >= 2:
                        pe.wait_ge(g_ready, (p + 1) * SLICES + j - 1)
                    for half in range(2):
                        gemm_unit(pe, U, j0 + 2 * j + half, [(ps[:, j % 2, :], tok[b])], (XT_h, XT_l),
                                         range(4 * half, 4 * half + 4), half == 0, half == 1)
                    if j >= 1:
                        g_transposes(p, j - 1)
                    if j == 1 and scatter_prev:
                        scatter(p - 1, 1 - b)
                if gather_next:
                    if scatter_prev:
                        pe.wait_ge(h_add, p * 4)
                    pe.wait_ge(g_lo, (p + 1) * SLICES + SLICES - 2)
                    gather(p + 1, 1 - b)
                for u in range(SLICES):
                    pe.wait_ge(g_lo, (p + 1) * SLICES + u + 1)
                    if u == 0 and scatter_prev:
                        pe.wait_ge(y_cp, p)
                    down_unit(pe, U, j0 + 2 * SLICES + u, [((2, 3), slice(0, P))], moe_gT3, u)
                    if u == 0:
                        g_transposes(p, SLICES - 1, gather_next)
                if scatter_here:
                    scatter(p, b)
                    pe.wait_ge(h_add, p * 4 + 4)

            with pe.Fori(0, E // 2) as i:
                U = Units(MOE_BASE, i, 2 * FFN_UNITS)
                expert(2 * i, 0, U, 0, True, False, True, False)
                expert(2 * i + 1, 1, U, FFN_UNITS, False, True, False, True)
            pe.wait_ge(table_ready, 1)
            n_over = pe.value_load(otab[0:1, 0:1], min_val=0, max_val=3)
            with pe.If(n_over > 0):
                with pe.Fori(0, n_over) as k:
                    expert(k + E, 0, Units(OVER_BASE, k, FFN_UNITS, SPLIT), 0, True, False, False, True)

        @block.vector
        def _(dve):
            chain = [0]

            def link(ins):
                chain[0] += 1
                ins.then_inc(dchain, 1)
                dve.wait_ge(dchain, chain[0])

            tt, ts, stt = nc.vector.tensor_tensor, nc.vector.tensor_scalar, nc.vector.scalar_tensor_tensor
            copy, reduce = nc.vector.tensor_copy, nc.vector.tensor_reduce
            roots = [0]

            def inverse_root(width, scale):
                ts(ssq[:, 0:width], ssq[:, 0:width], scale, EPS, ALU.mult, ALU.add).then_inc(ms_ready, 1)
                roots[0] += 1
                dve.wait_ge(rs_ready, roots[0])

            dve.wait_ge(consts_in, 16 * NLOADS)
            link(copy(pos_f[:, :], pos_i[:, :]))
            for t in range(TT):
                ins = ts(ang[:, 2, t, :], freq[:, :], pos_f[:, t:t + 1], None, ALU.mult)
            link(ins)
            magic = 1.5 * 2 ** 23
            turn = 2 * math.pi
            c1 = 6.28125
            c2 = float((np.array([turn - c1], np.float32).view(np.uint32) & np.uint32(0xFFFFF000)).view(np.float32)[0])
            c3 = turn - c1 - c2
            for a, k in ((0, sin), (1, cos)):
                k, r = k[:, :, :], ang[:, a]
                if a:
                    link(ts(k, ang[:, 2], 1 / turn, 0.25, ALU.mult, ALU.add))
                    link(ts(k, k, magic, magic, ALU.add, ALU.subtract))
                else:
                    link(ts(k, ang[:, 2], 1 / turn, magic, ALU.mult, ALU.add))
                    link(ts(k, k, magic, None, ALU.subtract))
                link(stt(r, k, -c1, ang[:, 2], ALU.mult, ALU.add))
                link(stt(r, k, -c2, r, ALU.mult, ALU.add))
                link(stt(r, k, -c3, r, ALU.mult, ALU.add))
                if a:
                    link(ts(r, r, math.pi / 2, None, ALU.add))
                pi = 3.1415925
                ins = ts(r, r, pi, -pi, ALU.min, ALU.max)
            ins.then_inc(ang_ready, 1)
            link(tt(lamp[:, :, :, :], lamv[:, 0::2], lamv[:, 1::2], ALU.mult))
            reduce(lams[:, :, :], lamp[:, :, :, :], AX.X, ALU.add).then_inc(lam_sum, 1)
            for l in range(DEPTH):
                ts(g_subs[:, l:l + 1], g_sub[:, l:l + 1], 1.0 - lambda_init(l), None, ALU.mult)
            dve.wait_ge(lam_exp, 1)
            link(tt(lamn[:, :], lame[:, 1], lame[:, 0], ALU.subtract))
            for l in range(DEPTH):
                ins = ts(lamn[:, l:l + 1], lamn[:, l:l + 1], -lambda_init(l), None, ALU.add)
            link(ins)
            dve.wait_ge(wr_hi, 1)
            tt(wr_l[:, :, :], wr[:, :, :], wr_h[:, :, :].bitcast(F32), ALU.subtract).then_inc(wr_lo, 1)
            dve.wait_ge(sin_ready, 1)

            split_to = [0]

            def split_until(U, j):
                while split_to[0] <= U.base + j:
                    split_lo(dve, Units(0), split_to[0])
                    split_to[0] += 1

            def norm_stage(n, gain):
                dve.wait_ge(sq_done, 2 * n + 2)
                inverse_root(TT, 1.0 / D)
                for t in range(TT):
                    ins = ts(xs3[:, t, :], h[:, t, :], rst[:, t:t + 1], None, ALU.mult)
                ins.then_inc(xs_ready, 1)
                for r in range(4):
                    dve.wait_ge(xt_hi, 4 * n + r + 1)
                    for a in range(2):
                        c = 2 * r + a
                        ins = stt(XT_l[:, c, :], ps[:, 4 + r, a * SEQ:(a + 1) * SEQ], gain[:, c:c + 1],
                                  XT_h[:, c, :].bitcast(F32), ALU.mult, ALU.subtract)
                    ins.then_inc(xt_lo, 1)

            def rotate(x1, x2, cs, sn, tmp):
                tt(tmp[0], x1, cs, ALU.mult)
                tt(tmp[1], x2, sn, ALU.mult)
                tt(tmp[2], x1, sn, ALU.mult)
                link(tt(tmp[3], x2, cs, ALU.mult))
                tt(x1, tmp[0], tmp[1], ALU.subtract)
                return tt(x2, tmp[2], tmp[3], ALU.add)

            def mixers(l):
                U = Units(MIX_BASE[l])
                split_until(U, AHEAD - 1)
                norm_stage(2 * l, g_attn[:, l, :])
                zq = mx(ZQK, 2048)
                zq32 = zq.rearrange("p (g d) -> p g d", d=HD)
                for g in range(IN_GROUPS):
                    if g == 3:
                        dve.wait_ge(in_evac, IN_GROUPS * l + 2)
                        dve.wait_ge(xt_tr, 8 * l + 4)
                        link(tt(xs[:, :], zq, zq, ALU.mult))
                        link(reduce(ssq[:, 0:32], xs[:, :].rearrange("p (g d) -> p g d", d=HD), AX.X, ALU.add))
                        inverse_root(32, 1.0 / HD)
                        link(tt(zq32, zq32, rst[:, 0:32].unsqueeze(2).to_broadcast([P, 32, HD]), ALU.mult))
                    if g == 4:
                        for t in range(TT):
                            for a in range(2):
                                v = zq.rearrange("p (t a g d) -> p t a g d", t=TT, a=2, d=HD)[:, t, a]
                                ins = tt(v, v, g_qk[:, l, a, :].unsqueeze(1).to_broadcast([P, 8, HD]), ALU.mult)
                        link(ins)
                    if g == 5:
                        v = zq.rearrange("p (t g d) -> p t g d", t=TT, d=HD)
                        shape = [P, TT, 16, DA_HALF]
                        tmp = [xs[:, a * 256:(a + 1) * 256].rearrange("p (t g d) -> p t g d", t=TT, d=DA_HALF)
                               for a in range(4)]
                        rotate(v[:, :, :, 0:DA_HALF], v[:, :, :, DA_HALF:2 * DA_HALF],
                               cos[:, :, 0:DA_HALF].unsqueeze(2).to_broadcast(shape),
                               sin[:, :, 0:DA_HALF].unsqueeze(2).to_broadcast(shape), tmp).then_inc(zqk_ready, 1)
                    if g == 6:
                        dve.wait_ge(zqk_ready, l + 1)
                        dve.wait_ge(in_evac, IN_GROUPS * l + 4)
                        v = mx(ZR, 1024).rearrange("p (t g d) -> p t g d", t=TT, d=HD)
                        shape = [P, TT, 8, RET_HALF]
                        tmp = [xs[:, a * 512:(a + 1) * 512].rearrange("p (t g d) -> p t g d", t=TT, d=RET_HALF)
                               for a in range(4)]
                        rotate(v[:, :, :, 0:RET_HALF], v[:, :, :, RET_HALF:HD],
                               cos[:, :, DA_HALF:NF].unsqueeze(2).to_broadcast(shape),
                               sin[:, :, DA_HALF:NF].unsqueeze(2).to_broadcast(shape), tmp).then_inc(zr_ready, 1)
                    if g == 8:
                        dve.wait_ge(in_evac, IN_GROUPS * l + 6)
                        link(tt(mx(ZG, 1024), mx(ZG, 1024), mx(RIN, 1024), ALU.mult))
                    split_until(U, 2 * g + 1 + AHEAD)
                rin = mx(RIN, HEADS * 384).rearrange("p (h n) -> p h n", h=HEADS)
                for hd in range(HEADS):
                    dve.wait_ge(ret_s, 4 * l + hd + 1)
                    tt(rin[:, hd, 0:SEQ], ps[:, 4 + hd, 0:SEQ], decay[:, hd, :], ALU.mult)
                    tt(rin[:, hd, SEQ:384], ps[:, 4 + hd, SEQ:384], decay[:, hd, 0:P], ALU.mult).then_inc(ret_w, 1)
                s0 = ps[:, 0:2, :].rearrange("p b (h n) -> p (b h) n", h=4)
                s1 = ps[:, 2:6, :].rearrange("p b (h n) -> p (b h) n", h=2)
                mask8 = mask[:, :].unsqueeze(1).to_broadcast([P, 8, P])
                for t, (s, diag) in enumerate(((s0, s0), (s1, s1[:, :, P:SEQ]))):
                    dve.wait_ge(da_s, 4 * l + 2 * t + 2)
                    link(tt(diag, diag, mask8, ALU.add))
                    link(reduce(mxs[:, t, :], s, AX.X, ALU.max))
                    ts(nbs[:, t, :], mxs[:, t, :], -DA_SCALE, None, ALU.mult).then_inc(nb_ready, 1)
                ya = xs[:, 0:1024].rearrange("p (t h n) -> p t h n", t=TT, h=HEADS)
                yr = xs[:, 1024:2048].rearrange("p (g n) -> p g n", g=8)
                ro = ps[:, 6:8, :].rearrange("p b (h n) -> p (b h) n", h=HEADS)
                dve.wait_ge(ret_o, l + 1)
                link(reduce(mu[:, :], ro, AX.X, ALU.add))
                link(ts(mu[:, :], mu[:, :], -1.0 / VD, None, ALU.mult))
                link(tt(yr, ro, mu[:, :].unsqueeze(2).to_broadcast([P, 8, VD]), ALU.add))
                sq = mx(RIN, 1024).rearrange("p (g n) -> p g n", g=8)
                link(tt(sq, yr, yr, ALU.mult))
                link(reduce(ssq[:, 0:8], sq, AX.X, ALU.add))
                inverse_root(8, 1.0 / VD)
                link(tt(yr, yr, rst[:, 0:8].unsqueeze(2).to_broadcast([P, 8, VD]), ALU.mult))
                tt(xs[:, 1024:2048], xs[:, 1024:2048], mx(ZG, 1024), ALU.mult).then_inc(yr_ready, 1)
                for t, (e, n) in enumerate(((mx(ZR, 1024), P), (mx(ZQK, 2048), SEQ))):
                    e = e.rearrange("p (a n) -> p a n", a=8)
                    dve.wait_ge(exp_done, 16 * l + 8 * t + 8)
                    link(nc.vector.reciprocal(rcs[:, t, :], sms[:, t, :]))
                    link(ts(rcs[:, t, 4:8], rcs[:, t, 4:8], lamn[:, l:l + 1], None, ALU.mult))
                    link(tt(e, e, rcs[:, t, :].unsqueeze(2).to_broadcast([P, 8, n]), ALU.mult))
                    tt(e[:, 0:4], e[:, 0:4], e[:, 4:8], ALU.add).then_inc(pd_ready, 1)
                for t in range(TT):
                    dve.wait_ge(osq, 2 * l + t + 1)
                    o = ps[:, (1, 4)[t], :].rearrange("p (h n) -> p h n", h=HEADS)
                    link(reduce(ssq[:, 0:4], mx(RIN + 512 * t, 512).rearrange("p (h n) -> p h n", h=HEADS),
                                AX.X, ALU.add))
                    inverse_root(4, 1.0 / VD)
                    ins = tt(ya[:, t], o, rst[:, 0:4].unsqueeze(2).to_broadcast([P, HEADS, VD]), ALU.mult)
                ins.then_inc(ya_ready, 1)
                for r in range(4):
                    dve.wait_ge(yt_hi, 4 * l + r + 1)
                    c, bank = ((4, 6), (6, 7), (0, 4), (2, 5))[r]
                    v = ps[:, bank, :].rearrange("p (a n) -> p a n", a=2)
                    stt(XT_l[:, c:c + 2, :], v, 1.0 if r < 2 else g_subs[:, l:l + 1],
                        XT_h[:, c:c + 2, :].bitcast(F32), ALU.mult, ALU.subtract).then_inc(yt_lo, 1)
                for u in range(4):
                    n = u % 2
                    gate = mx(SGB if u < 2 else SGA, 2048)
                    gate = gate.rearrange("p (t n) -> p t n", t=TT)[:, :, n * 512:(n + 1) * 512]
                    split_until(U, 2 * IN_GROUPS + u + AHEAD)
                    dve.wait_ge(unit_used, U.count(2 * IN_GROUPS + u))
                    ins = tt(gate, gate, ps[:, 2 * n:2 * n + 2, :], ALU.mult)
                    if u < 2:
                        ins.then_inc(proj_evac, 1)
                    else:
                        link(ins)
                        if u == 2:
                            dve.wait_ge(proj_evac, 2 * l + 2)
                        other = mx(SGB, 2048).rearrange("p (t n) -> p t n", t=TT)[:, :, n * 512:(n + 1) * 512]
                        ins = tt(gate, gate, other, ALU.add)
                        if u == 3:
                            ins.then_inc(m_ready, 1)
                for r in range(4):
                    dve.wait_ge(mt_hi, 4 * l + r + 1)
                    v = ps[:, 4 + r, :].rearrange("p (a n) -> p a n", a=2)
                    tt(XT_l[:, 2 * r:2 * r + 2, :], v, XT_h[:, 2 * r:2 * r + 2, :].bitcast(F32), ALU.subtract)\
                        .then_inc(mt_lo, 1)
                split_until(U, MIX_UNITS - 1)
                for n in range(2):
                    dve.wait_ge(unit_used, U.count(2 * IN_GROUPS + 4 + 2 * n + 1))
                    v = h[:, :, n * 512:(n + 1) * 512]
                    ins = tt(v, ps[:, 2 * n:2 * n + 2, :], v, ALU.add)
                ins.then_inc(h_ready, 1)

            def dense():
                U = Units(DENSE_BASE)
                split_until(U, AHEAD - 1)
                norm_stage(1, g_ffn[:, 0, :])

                def g(j):
                    dve.wait_ge(sig_done, j + 1)
                    b = 2 * (j % 2)
                    cols = slice((j % 2) * 512, (j % 2 + 1) * 512)
                    s = sgm[:, cols].rearrange("p (t n) -> p t n", t=TT)
                    o = gbuf[:, cols].rearrange("p (t n) -> p t n", t=TT)
                    tt(o, ps[:, b:b + 2, 0:256], s, ALU.mult).then_inc(g_half, 1)
                    dve.wait_ge(g_half, j + 1)
                    tt(o, ps[:, b:b + 2, 256:512], o, ALU.mult).then_inc(g_ready, 1)

                def lo(j):
                    dve.wait_ge(g_hi, j + 1)
                    tt(gT3[1][:, 2 * j:2 * j + 2, :], ps[:, 4 + j % 2, :].rearrange("p (a n) -> p a n", a=2),
                       gT3[0][:, 2 * j:2 * j + 2, :].bitcast(F32), ALU.subtract).then_inc(g_lo, 1)
                for j in range(SLICES):
                    if j >= 1:
                        g(j - 1)
                    if j >= 2:
                        lo(j - 2)
                    split_until(U, 2 * j + 1 + AHEAD)
                for u in range(SLICES):
                    if u == 0:
                        g(SLICES - 1)
                        lo(SLICES - 2)
                    if u == 1:
                        lo(SLICES - 1)
                    split_until(U, 2 * SLICES + u + AHEAD)
                dve.wait_ge(unit_used, U.count(FFN_UNITS - 1))
                for t, b in ((0, 6), (1, 2)):
                    v = h[:, t, :].rearrange("p (n c) -> p n c", n=2)
                    ins = tt(v, ps[:, b:b + 2, :], v, ALU.add)
                ins.then_inc(h_ready, 1)

            mixers(0)
            dense()
            mixers(1)
            norm_stage(3, g_ffn[:, 1, :])
            for t in range(TT):
                ins = tt(xs3[:, t, :], xs3[:, t, :], g_moe[:, :], ALU.mult)
            ins.then_inc(hn_full, 1)
            dve.wait_ge(hn_hi, 1)
            tt(hn_l[:, :], xs[:, :], hn_h[:, :].bitcast(F32), ALU.subtract).then_inc(hn_lo, 1)
            dve.wait_ge(logit, 1)
            link(copy(lg[:, :, :], ps[:, 0, 0:TT * E].rearrange("p (t e) -> p t e", t=TT)))
            for t in range(TT):
                link(nc.vector.max(top[:, t, :], lg[:, t, :]))
                link(nc.vector.max_index(tidx[:, t, :], top[:, t, :], lg[:, t, :]))
            link(copy(tif[:, :, :], tidx[:, :, :]))
            tt(tdf[:, :], top[:, :, 1], top[:, :, 0], ALU.subtract).then_inc(te_in, 1)
            dve.wait_ge(te_out, 1)
            link(ts(tw[:, 0, :], te[:, :], 1.0, None, ALU.add))
            link(nc.vector.reciprocal(tw[:, 1, :], tw[:, 0, :]))
            link(tt(tw[:, 2, :], te[:, :], tw[:, 1, :], ALU.mult))
            for t in range(TT):
                for a in range(2):
                    link(ts(oh[:, a, t, :], iota[:, 0:E], tif[:, t, a:a + 1], None, ALU.is_equal))
                link(ts(comb[:, t, :], oh[:, 0, t, :], tw[:, 1, t:t + 1], None, ALU.mult))
                link(stt(comb[:, t, :], oh[:, 1, t, :], tw[:, 2, t:t + 1], comb[:, t, :], ALU.mult, ALU.add))
            tt(routed[:, :, :], oh[:, 0], oh[:, 1], ALU.add).then_inc(routed_ready, 1)
            dve.wait_ge(routed_ready, 1)
            dve.wait_ge(ranked, 1)
            link(stt(rank1[:, :, :], ps[:, 1, 0:TT * E].rearrange("p (t e) -> p t e", t=TT), 1.0, routed[:, :, :],
                     ALU.add, ALU.mult))
            ts(rank[:, :, :], rank1[:, :, :], -1.0, None, ALU.add)
            ts(rank2[:, :, :], rank1[:, :, :], -1.0 - P, None, ALU.add)
            link(ts(okey[:, 0, :], ps[:, 1, TT * E:(TT + 1) * E], float(P), None, ALU.is_gt))
            reduce(nover[:, :], okey[:, 0, :], AX.X, ALU.add)
            link(ts(okey[:, 1, :], iota[:, 0:E], -1.0, float(E), ALU.mult, ALU.add))
            link(tt(okey[:, 1, :], okey[:, 1, :], okey[:, 0, :], ALU.mult))
            link(nc.vector.max(okey[:, 2, :], okey[:, 1, :]))
            link(ts(okey[:, 2, :], okey[:, 2, :], -1.0, float(E), ALU.mult, ALU.add))
            ts(otab[:, 8:16], okey[:, 2, :], float(E - 1), None, ALU.min)
            copy(otab[:, 0:1], nover[:, :]).then_inc(table_ready, 1)

            def select(b, e, places):
                for t in range(TT):
                    r = places[:, t, bass.ds(e, 1)]
                    cols = slice((2 * b + t) * P, (2 * b + t + 1) * P)
                    ts(sel_f[:, cols], iota[:, :], r, None, ALU.is_equal)
                    ins = ts(sel_r[:, cols], iota[:, :], r, None, ALU.is_equal)
                ins.then_inc(sel_ready, 1)

            def gather_lo(p, b):
                for r in range(2):
                    dve.wait_ge(gat, p * 4 + 2 + r + 1)
                    copy(XT_l[:, 4 * r:4 * r + 4, tok[b]], ps[:, 6 + r, :].rearrange("p (c n) -> p c n", c=4))\
                        .then_inc(gat_lo, 1)

            def g(p, U, j0, j):
                dve.wait_ge(sig_done, (p + 1) * SLICES + j + 1)
                cols = slice((j % 2) * 256, (j % 2 + 1) * 256)
                tt(moe_gbuf[:, cols], ps[:, j % 2, 0:256], moe_sgm[:, cols], ALU.mult).then_inc(g_half, 1)
                dve.wait_ge(g_half, (p + 1) * SLICES + j + 1)
                tt(moe_gbuf[:, cols], ps[:, j % 2, 256:512], moe_gbuf[:, cols], ALU.mult).then_inc(g_ready, 1)

            def lo(p, j):
                dve.wait_ge(g_hi, (p + 1) * SLICES + j + 1)
                tt(moe_gT3[1][:, 2 * j:2 * j + 2, :], ps[:, 4 + j % 2, 0:256].rearrange("p (a n) -> p a n", a=2),
                   moe_gT3[0][:, 2 * j:2 * j + 2, :].bitcast(F32), ALU.subtract).then_inc(g_lo, 1)

            def add_back(p, e, r):
                t, n = divmod(r, 2)
                dve.wait_ge(sc_done, p * 4 + r + 1)
                v = h[:, t, n * 512:(n + 1) * 512]
                stt(v, ps[:, 6 + r % 2, :], comb[:, t, bass.ds(e, 1)], v, ALU.mult, ALU.add).then_inc(h_add, 1)

            def expert(p, b, U, j0, e, places, first, last_split, scatter_prev, e_next, scatter_here):
                if first:
                    select(b, e, places)
                    gather_lo(p, b)
                    for j in range(AHEAD):
                        split_lo(dve, U, j0 + j)
                for j in range(SLICES):
                    if j >= 1:
                        g(p, U, j0, j - 1)
                    if j >= 2:
                        lo(p, j - 2)
                    if j in (2, 3) and scatter_prev is not None:
                        for r in (0, 1) if j == 2 else (2, 3):
                            add_back(p - 1, scatter_prev, r)
                    if j == 7 and e_next is not None:
                        select(1 - b, e_next, places)
                    for a in range(2):
                        split_lo(dve, U, j0 + 2 * j + AHEAD + a)
                for u in range(SLICES):
                    if u == 0:
                        g(p, U, j0, SLICES - 1)
                        lo(p, SLICES - 2)
                        if e_next is not None:
                            gather_lo(p + 1, 1 - b)
                    if u == 1:
                        lo(p, SLICES - 1)
                    if 2 * SLICES + u + AHEAD <= last_split:
                        split_lo(dve, U, j0 + 2 * SLICES + u + AHEAD)
                if scatter_here:
                    for r in range(4):
                        add_back(p, e, r)

            with dve.Fori(0, E // 2) as i:
                U = Units(MOE_BASE, i, 2 * FFN_UNITS)
                expert(2 * i, 0, U, 0, 2 * i, rank, True, FFN_UNITS + 1, None, 2 * i + 1, False)
                expert(2 * i + 1, 1, U, FFN_UNITS, 2 * i + 1, rank, False, FFN_UNITS - 1, 2 * i, None, True)
            dve.wait_ge(table_ready, 1)
            n_over = dve.value_load(otab[0:1, 0:1], min_val=0, max_val=3)
            with dve.If(n_over > 0):
                with dve.Fori(0, n_over) as k:
                    e = dve.value_load(otab[0:1, bass.ds(k + 8, 1)], min_val=0, max_val=E - 1)
                    expert(k + E, 0, Units(OVER_BASE, k, FFN_UNITS, SPLIT), 0, e, rank2, True, FFN_UNITS - 1,
                           None, None, True)


NLOADS = 12 + 6 * DEPTH


def lambda_init(layer):
    return 0.8 - 0.6 * math.exp(-0.3 * layer)


INPUTS = ["x", "positions", "attn_norm", "w_in", "da_q_norm", "da_k_norm", "lam_q1", "lam_k1", "lam_q2",
          "lam_k2", "da_subln", "w_proj_da", "w_proj_ret", "w_out", "ffn_norm", "dense_w1", "dense_w3",
          "dense_w2", "w_router", "moe_w1", "moe_w3", "moe_w2"]


def kernel(**inputs):
    import concourse.bacc as bacc
    from concourse.bass_utils import run_bass_kernel_spmd

    nc = bacc.Bacc("TRN2", target_bir_lowering=False, num_devices=1)
    arrays, args = {}, []
    tensors = [(n, np.ascontiguousarray(inputs[n])) for n in INPUTS] + list(constants().items())
    for name, a in tensors:
        arrays[f"in_{name}"] = a
        args.append(nc.dram_tensor(f"in_{name}", a.shape, mybir.dt.from_np(a.dtype), kind="ExternalInput").ap())
    args.append(nc.dram_tensor("out", (1, SEQ, D), F32, kind="ExternalOutput").ap())
    build(nc, *args)
    r = run_bass_kernel_spmd(nc, [arrays], core_ids=[0])
    return r.results[0]["out"]
```

```python
import math
from contextlib import ExitStack

import numpy as np

import concourse.bass as bass
from concourse import mybir

F32 = mybir.dt.float32
F32R = mybir.dt.float32r
I32 = mybir.dt.int32
U32 = mybir.dt.uint32
ALU = mybir.AluOpType
ACT = mybir.ActivationFunctionType
AX = mybir.AxisListType

P = 128
SEQ = 256
TT = SEQ // P
D = 1024
KC = D // P
DEPTH = 2
HEADS = 4
HD = 64
VD = 128
AW = HEADS * VD
IN_W = 5120
FF = 2816
FC = FF // P
E = 8
EPS = 1e-6
DA_SCALE = HD ** -0.5
DA_THETA, RET_THETA = 500000.0, 10000.0
DA_HALF, RET_HALF = HD // 8, HD // 2
NF = DA_HALF + RET_HALF
MASKED = -1.0e30

UNIT = 2048
RAW, SPLIT = 6, 3
SLICES = FF // 256
IN_GROUPS = IN_W // 512
MIX_UNITS = 2 * IN_GROUPS + 4 + 4
FFN_UNITS = 2 * SLICES + FC // 2
MIX_BASE = [0, MIX_UNITS + FFN_UNITS]
DENSE_BASE = MIX_UNITS
MOE_BASE = MIX_BASE[1] + MIX_UNITS
OVER_BASE = MOE_BASE + E * FFN_UNITS
IN_ORDER = [0, 1, 3, 4, 5, 2, 6, 7, 8, 9]
ROOTS = 5
PROJ_BANK = [0, 2, 6, 2]
AHEAD = 2

ZQK, ZV, ZR, ZRV, ZG = 0, 2048, 3072, 4096, 5120
SGA, SGB = 6144, 8192
QKT, RETT = 10240, 12288
RIN = 13312
MIX_WORDS = RIN + HEADS * 384


def _columns(widths):
    at, out = 0, {}
    for name, w in widths:
        out[name] = (at, w)
        at += w
    return out, at


COLS, COLS_W = _columns([("ident", P), ("g_attn", DEPTH * KC), ("g_ffn", DEPTH * KC), ("g_sub", DEPTH),
                         ("freq", NF), ("mask", P), ("iota", P), ("before", P), ("wr", KC * E),
                         ("decay", HEADS * SEQ), ("stack", E)])
COLS_FIRST = P + 2 * DEPTH * KC
ROWS, ROWS_W = _columns([("g_qk", 2 * DEPTH * HD), ("lam", 4 * DEPTH * HD), ("g_moe", D)])


def tables():
    i = np.arange(P)
    c = {}
    c["ident"] = np.eye(P)
    c["mask"] = np.where(i[None, :] <= i[:, None], 0.0, MASKED)
    lg = np.log1p(-np.exp2(-5.0 - np.arange(HEADS)))
    rel = np.arange(SEQ)[None, :] - i[:, None]
    dec = np.where(rel[:, None] >= 0, np.exp(lg[None, :, None] * np.maximum(rel, 0)[:, None]), 0.0)
    c["decay"] = (dec * HD ** -0.5).reshape(P, HEADS * SEQ)
    f = np.concatenate([1.0 / np.power(np.float32(th), np.arange(n, dtype=np.float32) / np.float32(n))
                        for th, n in ((DA_THETA, DA_HALF), (RET_THETA, RET_HALF))])
    c["freq"] = np.broadcast_to(f, (P, NF))
    c["iota"] = np.broadcast_to(i, (P, P))
    c["stack"] = (i[:, None] < 2 * E) & (i[:, None] % E == np.arange(E)[None, :])
    c["before"] = i[:, None] < i[None, :]
    return {k: v.astype(np.float32) for k, v in c.items()}


def build(nc, x, positions, w_in, w_proj_da, w_proj_ret, w_out, dense_w1, dense_w3, dense_w2,
          moe_w1, moe_w3, moe_w2, cols_d, rows_d, out):
    ctx = ExitStack()
    with ctx:
        def sb(name, shape, dt=F32):
            return ctx.enter_context(nc.sbuf_tensor(name, shape, dt))

        def sem(name):
            return ctx.enter_context(nc.semaphore(name))

        arena_at = (nc.sbuf_base + 31) // 32 * 32
        mix = sb("mix", [P, MIX_WORDS])
        place = [arena_at]

        def over(name, words, dt=F32):
            t = nc.alloc_sbuf_tensor_at(name, [P, words], dt, offset=place[0])
            place[0] += 4 * words
            return t
        gT_h = over("gT_h", FC * SEQ, F32R)
        gT_l = over("gT_l", FC * SEQ, F32R)
        sgm = over("sgm", 2 * 512)
        gbuf = over("gbuf", 2 * 512)
        assert place[0] <= arena_at + 4 * MIX_WORDS
        place[0] = arena_at + 4 * (2 * FC * P)
        hn_h = over("hn_h", TT * D, F32R)
        hn_l = over("hn_l", TT * D, F32R)
        place[0] = arena_at + 4 * (2 * FC * P + 2 * TT * D)
        moe_gT_h = nc.alloc_sbuf_tensor_at("moe_gT_h", [P, FC * P], F32R, offset=arena_at)
        moe_gT_l = nc.alloc_sbuf_tensor_at("moe_gT_l", [P, FC * P], F32R, offset=arena_at + 4 * FC * P)
        YR_h = nc.alloc_sbuf_tensor_at("YR_h", [P, HEADS, SEQ], F32R, offset=arena_at + 4 * ZQK)
        YR_l = nc.alloc_sbuf_tensor_at("YR_l", [P, HEADS, SEQ], F32R, offset=arena_at + 4 * (ZQK + HEADS * SEQ))
        MT_h = nc.alloc_sbuf_tensor_at("MT_h", [P, KC, SEQ], F32R, offset=arena_at + 4 * QKT)
        MT_l = nc.alloc_sbuf_tensor_at("MT_l", [P, KC, SEQ], F32R, offset=arena_at + 4 * (QKT + KC * SEQ))
        assert QKT + 2 * KC * SEQ <= MIX_WORDS
        moe_sgm = over("moe_sgm", 2 * 256)
        moe_gbuf = over("moe_gbuf", 2 * 256)
        sel_r = over("sel_r", 2 * TT * P, F32R)
        selT = over("selT", 2 * TT * P)
        assert place[0] <= arena_at + 4 * MIX_WORDS

        raw = sb("raw", [P, RAW, UNIT])
        wh = sb("wh", [P, SPLIT, UNIT], F32R)
        wl = sb("wl", [P, SPLIT, UNIT], F32R)
        XT_h = sb("XT_h", [P, KC, SEQ], F32R)
        XT_l = sb("XT_l", [P, KC, SEQ], F32R)
        h = sb("h", [P, TT, D])
        xs = sb("xs", [P, TT * D])
        cols = sb("cols", [P, COLS_W])
        rows = sb("rows", [P, ROWS_W])
        ones = sb("ones", [P, P])

        def col(name):
            return cols[:, COLS[name][0]:COLS[name][0] + COLS[name][1]]

        def row(name):
            return rows[:, ROWS[name][0]:ROWS[name][0] + ROWS[name][1]]
        ident, mask, iota, before, freq, g_sub, stack = (col(n) for n in ("ident", "mask", "iota", "before", "freq", "g_sub",
                                                                          "stack"))
        decay = col("decay").rearrange("p (h q) -> p h q", h=HEADS)
        g_attn = col("g_attn").rearrange("p (l c) -> p l c", l=DEPTH)
        g_ffn = col("g_ffn").rearrange("p (l c) -> p l c", l=DEPTH)
        wr = col("wr").rearrange("p (c e) -> p c e", c=KC)
        g_moe = row("g_moe")
        g_qk = row("g_qk").rearrange("p (l a d) -> p l a d", l=DEPTH, a=2)
        lamv = row("lam").rearrange("p (a l d) -> p a l d", a=4, l=DEPTH)
        pos_i = sb("pos_i", [P, TT], I32)
        pos_f = sb("pos_f", [P, TT])
        cos = sb("cos", [P, TT, NF])
        sin = sb("sin", [P, TT, NF])
        ang = sb("ang", [P, 3, TT, NF])
        g_subs = sb("g_subs", [P, DEPTH])
        lamp = sb("lamp", [P, 2, DEPTH, HD])
        lams = sb("lams", [P, 2, DEPTH])
        lame = sb("lame", [P, 2, DEPTH])
        lamn = sb("lamn", [P, DEPTH])
        wr_hl = sb("wr_hl", [P, KC, 2 * E], F32R)
        lgT = sb("lgT", [2 * E, SEQ])
        nhalf = sb("nhalf", [P, 32])
        ssq = sb("ssq", [P, 32])
        rst = sb("rst", [P, 32])
        rn = sb("rn", [P, TT])
        mxs = sb("mxs", [P, 2, 8])
        nbs = sb("nbs", [P, 2, 8])
        sms = sb("sms", [P, 2, 8])
        rcs = sb("rcs", [P, 2, 8])
        mu = sb("mu", [P, 8])
        mur = sb("mur", [P, 8])
        yaf = sb("yaf", [P, 8])
        lg = sb("lg", [P, TT, E])
        top = sb("top", [P, TT, 8])
        tidx = sb("tidx", [P, TT, 8], U32)
        tif = sb("tif", [P, TT, 8])
        tdf = sb("tdf", [P, TT])
        te = sb("te", [P, TT])
        tw = sb("tw", [P, 3, TT])
        oh = sb("oh", [P, 2, TT, E])
        comb = sb("comb", [P, TT, E])
        routed = sb("routed", [P, TT, E])
        rank1 = sb("rank1", [P, TT, E])
        rank = sb("rank", [P, TT, E])
        rank2 = sb("rank2", [P, TT, E])
        okey = sb("okey", [P, 3, E])
        nover = sb("nover", [P, 1])
        otab = sb("otab", [P, 16], I32)

        ps = ctx.enter_context(nc.psum_tensor("ps", [P, 8, 512], F32))

        first_in = sem("first_in")
        consts_in = sem("consts_in")
        x_in = [sem(f"x_in{n}") for n in range(2)]
        landed = [sem(f"landed{s}") for s in range(RAW)]
        hi_ready = sem("hi_ready")
        lo_ready = sem("lo_ready")
        unit_used = sem("unit_used")
        dchain = sem("dchain")
        sin_ready = sem("sin_ready")
        ang_ready = sem("ang_ready")
        lam_sum = sem("lam_sum")
        lam_exp = sem("lam_exp")
        pool_const = sem("pool_const")
        ms_ready = sem("ms_ready")
        rs_ready = sem("rs_ready")
        sq_done = sem("sq_done")
        xt_tr = sem("xt_tr")
        xt_hi = sem("xt_hi")
        xt_lo = sem("xt_lo")
        in_evac = sem("in_evac")
        zqk_ready = sem("zqk_ready")
        zr_ready = sem("zr_ready")
        silu_ready = sem("silu_ready")
        zt_tr = sem("zt_tr")
        zt_cp = sem("zt_cp")
        ret_s = sem("ret_s")
        ret_w = sem("ret_w")
        ret_o = sem("ret_o")
        da_s = sem("da_s")
        nb_ready = sem("nb_ready")
        exp_done = sem("exp_done")
        pd_ready = sem("pd_ready")
        pd_tr = sem("pd_tr")
        pd_cp = sem("pd_cp")
        da_o = sem("da_o")
        pchain = sem("pchain")
        mu_ready = sem("mu_ready")
        gn_sq = sem("gn_sq")
        mur_ready = sem("mur_ready")
        gn_out = sem("gn_out")
        osq = sem("osq")
        down_half = sem("down_half")
        yr_ready = sem("yr_ready")
        ya_ready = sem("ya_ready")
        yt_tr = sem("yt_tr")
        yt_hi = sem("yt_hi")
        yt_lo = sem("yt_lo")
        proj_evac = sem("proj_evac")
        m_ready = sem("m_ready")
        mt_tr = sem("mt_tr")
        mt_hi = sem("mt_hi")
        mt_lo = sem("mt_lo")
        h_half = sem("h_half")
        sig_done = sem("sig_done")
        g_half = sem("g_half")
        g_ready = sem("g_ready")
        g_tr = sem("g_tr")
        g_hi = sem("g_hi")
        g_lo = sem("g_lo")
        wr_hi = sem("wr_hi")
        wr_lo = sem("wr_lo")
        hn_hi = sem("hn_hi")
        hn_lo = sem("hn_lo")
        hg_ready = sem("hg_ready")
        logit = sem("logit")
        lgt_cp = sem("lgt_cp")
        te_in = sem("te_in")
        te_out = sem("te_out")
        routed_ready = sem("routed_ready")
        ranked = sem("ranked")
        table_ready = sem("table_ready")
        sel_ready = sem("sel_ready")
        gat = sem("gat")
        gat_cp = sem("gat_cp")
        st_tr = sem("st_tr")
        st_cp = sem("st_cp")
        y_cp = sem("y_cp")
        sc_done = sem("sc_done")
        h_add = sem("h_add")
        stored = sem("stored")

        w_in_v = [w_in[l].rearrange("(c p) n -> p c n", p=P) for l in range(DEPTH)]
        pr_v = [w_proj_ret[l].rearrange("(c p) n -> p c n", p=P) for l in range(DEPTH)]
        pd_v = [w_proj_da[l].rearrange("(c p) n -> p c n", p=P) for l in range(DEPTH)]
        wo_v = [w_out[l].rearrange("(c p) n -> p c n", p=P) for l in range(DEPTH)]
        dn_v = [w[0].rearrange("(c p) n -> p c n", p=P) for w in (dense_w1, dense_w3, dense_w2)]
        me_v = [w[0].rearrange("e (c p) n -> e p c n", p=P) for w in (moe_w1, moe_w3, moe_w2)]

        def mixer_unit(l, u):
            if u < 2 * IN_GROUPS:
                g, half = divmod(u, 2)
                b = IN_ORDER[g]
                return [w_in_v[l][:, half * 4 + 2 * a:half * 4 + 2 * a + 2, b * 512:(b + 1) * 512] for a in (0, 1)]
            u -= 2 * IN_GROUPS
            if u < 4:
                v = (pr_v, pd_v)[u % 2][l]
                n = u // 2
                return [v[:, 2 * a:2 * a + 2, n * 512:(n + 1) * 512] for a in (0, 1)]
            n, half = divmod(u - 4, 2)
            return [wo_v[l][:, half * 4 + 2 * a:half * 4 + 2 * a + 2, n * 512:(n + 1) * 512] for a in (0, 1)]

        def ffn_unit(w1, w3, w2, slot, u):
            if u < 2 * SLICES:
                j, half = divmod(u, 2)
                to = raw[:, slot, :].rearrange("p (c w n) -> p c w n", c=4, w=2)
                return [(to[:, :, a, :], w[:, half * 4:half * 4 + 4, j * 256:(j + 1) * 256])
                        for a, w in ((0, w1), (1, w3))]
            c = 2 * (u - 2 * SLICES)
            return [(raw[:, slot, a * D:(a + 1) * D], w2[:, c + a, :]) for a in (0, 1)]

        class Units:
            def __init__(self, base, i=None, per=0, raw_slots=RAW):
                self.base, self.i, self.per, self.raw_slots = base, i, per, raw_slots
                assert i is None or (per % raw_slots == 0 and per % SPLIT == 0)

            def at(self, const, per):
                return const if self.i is None else const + self.i * per

            def count(self, j):
                return self.at(self.base + j + 1, self.per)

            def before(self, j, n):
                c = self.base + j + 1 - n
                return None if self.i is None and c < 1 else self.at(c, self.per)

            def split_slot(self, j):
                return (self.base + j) % SPLIT

            def raw_slot(self, j):
                return (self.base + j) % self.raw_slots

            def landed(self, j):
                n, s = self.base + j, self.raw_slot(j)
                if self.raw_slots == RAW:
                    c = n // RAW + 1
                else:
                    c = len([m for m in range(OVER_BASE) if m % RAW == s])
                    c += len([m for m in range(OVER_BASE, n + 1) if m % SPLIT == s])
                return self.at(32 * c, 32 * (self.per // self.raw_slots))

        def load_unit(eng, U, j, pairs):
            v = U.before(j, U.raw_slots)
            if v is not None:
                eng.wait_ge(lo_ready, v)
            for to, of in pairs:
                eng.dma_start(to, of).then_inc(landed[U.raw_slot(j)], 16)

        def split_hi(act, U, j):
            act.wait_ge(landed[U.raw_slot(j)], U.landed(j))
            v = U.before(j, SPLIT)
            if v is not None:
                act.wait_ge(unit_used, v)
            nc.scalar.activation(wh[:, U.split_slot(j), :], raw[:, U.raw_slot(j), :], ACT.Copy).then_inc(hi_ready, 1)

        def split_lo(dve, U, j):
            dve.wait_ge(hi_ready, U.count(j))
            v = U.before(j, SPLIT)
            if v is not None:
                dve.wait_ge(unit_used, v)
            s = U.split_slot(j)
            nc.vector.tensor_tensor(wl[:, s, :], raw[:, U.raw_slot(j), :], wh[:, s, :].bitcast(F32),
                                    ALU.subtract).then_inc(lo_ready, 1)

        def product(o, xh, xl, bh, bl, start, stop):
            nc.tensor.matmul(o, xh, bh, start=start, stop=False)
            nc.tensor.matmul(o, xh, bl, start=False, stop=False)
            return nc.tensor.matmul(o, xl, bh, start=False, stop=stop)

        def gemm_unit(pe, U, j, outs, xT, chunks, start, stop, between=None):
            pe.wait_ge(lo_ready, U.count(j))
            s = U.split_slot(j)
            for a, c in enumerate(chunks):
                if a == 2 and between is not None:
                    between()
                for o, cols in outs:
                    last = product(o, xT[0][:, c, cols], xT[1][:, c, cols],
                                   wh[:, s, a * 512:(a + 1) * 512], wl[:, s, a * 512:(a + 1) * 512],
                                   start and a == 0, stop and a == len(chunks) - 1)
            last.then_inc(unit_used, 1)

        tok = [slice(t * P, (t + 1) * P) for t in range(TT)]
        gT3 = [g[:, :].rearrange("p (c n) -> p c n", c=FC) for g in (gT_h, gT_l)]
        moe_gT3 = [g[:, :].rearrange("p (c n) -> p c n", c=FC) for g in (moe_gT_h, moe_gT_l)]
        xs3 = xs[:, :].rearrange("p (t n) -> p t n", t=TT)

        def mx(off, words):
            return mix[:, off:off + words]

        block = ctx.enter_context(nc.Block())

        @block.sync
        def _(sp):
            xv = x[0].rearrange("(t p) d -> p t d", p=P)
            for n in range(2):
                sp.dma_start(h[:, :, n * 512:(n + 1) * 512], xv[:, :, n * 512:(n + 1) * 512]).then_inc(x_in[n], 16)
            for l in range(DEPTH):
                U = Units(MIX_BASE[l])
                for u in range(MIX_UNITS):
                    to = raw[:, U.raw_slot(u), :].rearrange("p (a c n) -> p a c n", a=2, c=2)
                    load_unit(sp, U, u, [(to[:, a], s) for a, s in enumerate(mixer_unit(l, u))])
                if l == 0:
                    U = Units(DENSE_BASE)
                    for u in range(FFN_UNITS):
                        load_unit(sp, U, u, ffn_unit(*dn_v, U.raw_slot(u), u))
            with sp.Fori(0, E // 2) as i:
                U = Units(MOE_BASE, i, 2 * FFN_UNITS)
                for half in range(2):
                    w = [v[2 * i + half] for v in me_v]
                    for u in range(FFN_UNITS):
                        j = half * FFN_UNITS + u
                        load_unit(sp, U, j, ffn_unit(*w, U.raw_slot(j), u))
            sp.wait_ge(table_ready, 1)
            n_over = sp.value_load(otab[0:1, 0:1], min_val=0, max_val=3)
            with sp.If(n_over > 0):
                with sp.Fori(0, n_over) as k:
                    e = sp.value_load(otab[0:1, bass.ds(k + 8, 1)], min_val=0, max_val=E - 1)
                    U = Units(OVER_BASE, k, FFN_UNITS, SPLIT)
                    w = [v[e] for v in me_v]
                    for u in range(FFN_UNITS):
                        load_unit(sp, U, u, ffn_unit(*w, U.raw_slot(u), u))
            sp.wait_ge(h_add, n_over * 4 + 4 * E)
            sp.dma_start(out[0].rearrange("(t p) d -> p t d", p=P), h[:, :, :]).then_inc(stored, 16)
            sp.wait_ge(stored, 16)

        @block.gpsimd
        def _(pool):
            nc.gpsimd.memset(nhalf[:, :], -0.5).then_inc(pool_const, 1)
            nc.gpsimd.memset(ones[:, :], 1.0).then_inc(pool_const, 1)
            pool.wait_ge(pool_const, 2)
            n_roots, chain = [0], [0]

            def root(to, of):
                n_roots[0] += 1
                pool.wait_ge(ms_ready, n_roots[0])
                nc.gpsimd.tensor_tensor(to, of, nhalf[:, 0:of.shape[-1]], ALU.pow).then_inc(rs_ready, 1)

            for l in range(DEPTH):
                root(rn[:, :], ssq[:, 0:TT])
                root(rst[:, :], ssq[:, :])
                pool.wait_ge(sin_ready, 1)
                pool.wait_ge(in_evac, IN_GROUPS * l + 3)
                zr4 = mx(ZR, 1024).rearrange("p (t g d) -> p t g d", t=TT, d=HD)
                x1, x2 = zr4[:, :, :, 0:RET_HALF], zr4[:, :, :, RET_HALF:HD]
                cs, sn = (v[:, :, DA_HALF:NF].unsqueeze(2).to_broadcast([P, TT, 8, RET_HALF]) for v in (cos, sin))
                tmp = [mx(SGB + a * 512, 512).rearrange("p (t g d) -> p t g d", t=TT, d=RET_HALF) for a in range(4)]
                tt = nc.gpsimd.tensor_tensor
                tt(tmp[0], x1, cs, ALU.mult)
                tt(tmp[1], x2, sn, ALU.mult)
                tt(tmp[2], x1, sn, ALU.mult)
                tt(tmp[3], x2, cs, ALU.mult).then_inc(pchain, 1)
                pool.wait_ge(pchain, l + 1)
                tt(x1, tmp[0], tmp[1], ALU.subtract)
                tt(x2, tmp[2], tmp[3], ALU.add).then_inc(zr_ready, 1)
                pool.wait_ge(in_evac, IN_GROUPS * l + 5)
                tt(mx(ZG, 1024), mx(ZG, 1024), mx(SGA, 1024), ALU.mult).then_inc(silu_ready, 1)
                root(rst[:, 0:8], ssq[:, 0:8])
                root(rst[:, 8:16], ssq[:, 8:16])
                root(rn[:, :], ssq[:, 0:TT])

        @block.scalar
        def _(act):
            act.dma_start(cols[:, 0:COLS_FIRST], cols_d[:, 0:COLS_FIRST]).then_inc(first_in, 16)
            act.dma_start(pos_i[:, :], positions).then_inc(consts_in, 16)
            act.dma_start(cols[:, COLS_FIRST:], cols_d[:, COLS_FIRST:]).then_inc(consts_in, 16)
            act.dma_start(rows[:, :], rows_d.to_broadcast([P, ROWS_W])).then_inc(consts_in, 16)
            act.wait_ge(first_in, 16)

            split_to = [0]

            def split_until(U, j):
                while split_to[0] <= U.base + j:
                    split_hi(act, Units(0), split_to[0])
                    split_to[0] += 1

            def norm_hi(n, half, gain):
                for r in (2 * half, 2 * half + 1):
                    act.wait_ge(xt_tr, 4 * n + r + 1)
                    for a in range(2):
                        c = 2 * r + a
                        ins = nc.scalar.activation(XT_h[:, c, :], ps[:, 4 + r, a * SEQ:(a + 1) * SEQ], ACT.Copy,
                                                   scale=gain[:, c:c + 1])
                    ins.then_inc(xt_hi, 1)

            def squares(n, to=xs3):
                if n == 0:
                    for s in x_in:
                        act.wait_ge(s, 16)
                else:
                    act.wait_ge(h_half, 2 * n)
                for t in range(TT):
                    nc.scalar.activation(to[:, t, :], h[:, t, :], ACT.Square, accum_out=ssq[:, t:t + 1])\
                        .then_inc(sq_done, 1)

            def small_tables():
                act.wait_ge(ang_ready, 1)
                nc.scalar.activation(sin[:, :, :], ang[:, 0], ACT.Sin)
                nc.scalar.activation(cos[:, :, :], ang[:, 1], ACT.Sin).then_inc(sin_ready, 1)
                act.wait_ge(lam_sum, 1)
                nc.scalar.activation(lame[:, :, :], lams[:, :, :], ACT.Exp).then_inc(lam_exp, 1)
                nc.scalar.activation(wr_hl[:, :, 0:E], wr, ACT.Copy).then_inc(wr_hi, 1)

            def mixers(l):
                U = Units(MIX_BASE[l])
                gain = g_attn[:, l, :]
                if l == 0:
                    norm_hi(0, 0, gain)
                    split_until(U, 0)
                    norm_hi(0, 1, gain)
                    split_until(U, 1)
                qkT = mx(QKT, 2048).rearrange("p (r n) -> p r n", r=4)
                retT = mx(RETT, 1024).rearrange("p (r n) -> p r n", r=2)
                e0 = mx(ZR, 1024).rearrange("p (c h n) -> p c h n", c=2, h=HEADS)
                e1 = mx(ZQK, 2048).rearrange("p (c h n) -> p c h n", c=2, h=HEADS)

                def evac(g):
                    act.wait_ge(unit_used, U.count(2 * g + 1))
                    if g == 0:
                        act.wait_ge(rs_ready, ROOTS * l + 1)
                    for t in range(TT):
                        acc = ps[:, 2 * (g % 2) + t, :]
                        if g < 2:
                            to = mx(ZQK + t * 1024 + g * 512, 512)
                        elif g < 6:
                            to = mx((ZR, ZRV, ZG, ZV)[g - 2] + t * 512, 512)
                        else:
                            to = mx((SGA, SGB)[(g - 6) // 2] + t * 1024 + (g % 2) * 512, 512)
                        if g < 2:
                            at = t * 1024 + g * 512
                            nc.scalar.activation(xs[:, at:at + 512], acc, ACT.Square, scale=rn[:, t:t + 1])
                        if g == 4:
                            nc.scalar.activation(mx(SGA + t * 512, 512), acc, ACT.Sigmoid, scale=rn[:, t:t + 1])
                        ins = nc.scalar.activation(to, acc, ACT.Copy if g < 6 else ACT.Sigmoid, scale=rn[:, t:t + 1])
                    ins.then_inc(in_evac, 1)

                def zt_copy(r):
                    act.wait_ge(zt_tr, 6 * l + r + 1)
                    nc.scalar.activation(qkT[:, r] if r < 4 else retT[:, r - 4], ps[:, 4 + r % 4, :], ACT.Copy)\
                        .then_inc(zt_cp, 1)

                def exps(k):
                    act.wait_ge(nb_ready, 3 * l + k + 1)
                    for c in range(2):
                        for hd in ((0, 1), (2, 3), (0, 1, 2, 3))[k]:
                            t, n = (1, SEQ) if k < 2 else (0, P)
                            bank = (6, 6, 4)[k] + c
                            a = hd % 2 if k < 2 else hd
                            ins = nc.scalar.activation((e0 if t == 0 else e1)[:, c, hd],
                                                       ps[:, bank, a * n:(a + 1) * n], ACT.Exp,
                                                       bias=nbs[:, t, 4 * c + hd:4 * c + hd + 1], scale=DA_SCALE,
                                                       accum_out=sms[:, t, 4 * c + hd:4 * c + hd + 1])
                    ins.then_inc(exp_done, 1)

                pdT = mx(QKT, 1536).rearrange("p (r n) -> p r n", r=3)

                def pd_copy(r):
                    act.wait_ge(pd_tr, 3 * l + r + 1)
                    nc.scalar.activation(pdT[:, r], ps[:, (4, 5, 5)[r], :], ACT.Copy).then_inc(pd_cp, 1)

                def group_squares():
                    act.wait_ge(mu_ready, l + 1)
                    for g in range(8):
                        ins = nc.scalar.activation(mx(RIN + g * VD, VD), ps[:, 6 + g // 4, (g % 4) * VD:(g % 4 + 1) * VD],
                                                   ACT.Square, bias=mu[:, g:g + 1], accum_out=ssq[:, g:g + 1])
                    ins.then_inc(gn_sq, 1)

                def group_norm():
                    act.wait_ge(mur_ready, l + 1)
                    for g in range(8):
                        ins = nc.scalar.activation(xs[:, 1024 + g * VD:1024 + (g + 1) * VD],
                                                   ps[:, 6 + g // 4, (g % 4) * VD:(g % 4 + 1) * VD], ACT.Identity,
                                                   scale=rst[:, g:g + 1], bias=mur[:, g:g + 1])
                    ins.then_inc(gn_out, 1)

                def out_squares(t):
                    act.wait_ge(da_o, 2 * l + 2 - t)
                    for hd in range(HEADS):
                        ins = nc.scalar.activation(mx(RETT + t * 512 + hd * VD, VD),
                                                   ps[:, 5 - t, hd * VD:(hd + 1) * VD], ACT.Square,
                                                   scale=rcs[:, t, hd:hd + 1],
                                                   accum_out=ssq[:, 8 + 4 * t + hd:9 + 4 * t + hd])
                    ins.then_inc(osq, 1)

                for n in range(2 * IN_GROUPS):
                    if n == 0:
                        if l > 0:
                            norm_hi(2 * l, 1, gain)
                        squares(2 * l)
                    if n == 1 and l == 0:
                        small_tables()
                    if n == 10:
                        for r in range(4):
                            zt_copy(r)
                    if n in (13, 15, 16):
                        exps((13, 15, 16).index(n))
                    if n == 14:
                        act.wait_ge(silu_ready, l + 1)
                    if n == 17:
                        pd_copy(0)
                        pd_copy(1)
                        group_squares()
                    if n % 2 == 0 and n > 0:
                        evac(n // 2 - 1)
                    if n == 11:
                        zt_copy(4)
                        zt_copy(5)
                    if n == 18:
                        pd_copy(2)
                        group_norm()
                        out_squares(1)
                    if n == 19:
                        out_squares(0)
                    split_until(U, n + AHEAD)

                def yt(r):
                    act.wait_ge(yt_tr, 4 * l + r + 1)
                    c = 2 * (r % 2)
                    nc.scalar.activation((YR_h if r < 2 else XT_h)[:, c:c + 2, :],
                                         ps[:, (6, 7, 4, 5)[r], :].rearrange("p (a n) -> p a n", a=2),
                                         ACT.Copy, scale=1.0 if r < 2 else g_subs[:, l:l + 1]).then_inc(yt_hi, 1)

                yt(0)
                yt(1)
                evac(IN_GROUPS - 1)
                split_until(U, 22)
                yt(2)
                yt(3)
                split_until(U, 24)

                def mt(half):
                    for r in (2 * half, 2 * half + 1):
                        act.wait_ge(mt_tr, 4 * l + r + 1)
                        nc.scalar.activation(MT_h[:, 2 * r:2 * r + 2, :],
                                             ps[:, 4 + r, :].rearrange("p (a n) -> p a n", a=2), ACT.Copy)\
                            .then_inc(mt_hi, 1)
                mt(0)
                split_until(U, 26)
                mt(1)
                split_until(U, 28)
                norm_hi(2 * l + 1, 0, g_ffn[:, l, :])
                split_until(U, 29)

            def sigmoid_slice(products, bank, buf):
                act.wait_ge(unit_used, products)
                nc.scalar.activation(buf, bank, ACT.Sigmoid).then_inc(sig_done, 1)

            def dense():
                def sigm(j):
                    act.wait_ge(unit_used, Units(DENSE_BASE).count(2 * j + 1))
                    if j == 0:
                        act.wait_ge(rs_ready, ROOTS)
                    for t in range(TT):
                        ins = nc.scalar.activation(sgm[:, (2 * (j % 2) + t) * 256:(2 * (j % 2) + t + 1) * 256],
                                                   ps[:, 2 * (j % 2) + t, 0:256], ACT.Sigmoid, scale=rn[:, t:t + 1])
                    ins.then_inc(sig_done, 1)

                def hi(j):
                    act.wait_ge(g_tr, j + 1)
                    nc.scalar.activation(gT3[0][:, 2 * j:2 * j + 2, :],
                                         ps[:, 4 + j % 2, :].rearrange("p (a n) -> p a n", a=2), ACT.Copy)\
                        .then_inc(g_hi, 1)
                for j in range(SLICES):
                    if j == 0:
                        norm_hi(1, 1, g_ffn[:, 0, :])
                        squares(1)
                    if j >= 1:
                        sigm(j - 1)
                    if j >= 2:
                        hi(j - 2)
                    split_until(Units(DENSE_BASE), 2 * j + 1 + AHEAD)
                for u in range(SLICES):
                    if u == 0:
                        sigm(SLICES - 1)
                        hi(SLICES - 2)
                    if u == 1:
                        hi(SLICES - 1)
                    if u == SLICES - 1:
                        norm_hi(2, 0, g_attn[:, 1, :])
                    split_until(Units(DENSE_BASE), 2 * SLICES + u + AHEAD)

            mixers(0)
            dense()
            mixers(1)
            norm_hi(3, 1, g_ffn[:, 1, :])
            squares(3, mx(ZQK, 2048).rearrange("p (t n) -> p t n", t=TT))
            act.wait_ge(logit, 1)
            nc.scalar.activation(lgT[:, :], ps[0:2 * E, 0, 0:SEQ], ACT.Copy).then_inc(lgt_cp, 1)
            act.wait_ge(hg_ready, 1)
            act.wait_ge(rs_ready, 2 * ROOTS)
            for t in range(TT):
                ins = nc.scalar.activation(hn_h[:, t * D:(t + 1) * D], xs3[:, t, :], ACT.Copy, scale=rn[:, t:t + 1])
            ins.then_inc(hn_hi, 1)
            act.wait_ge(te_in, 1)
            nc.scalar.activation(te[:, :], tdf[:, :], ACT.Exp).then_inc(te_out, 1)

            def gather_copy(p, b):
                act.wait_ge(st_tr, p + 1)
                nc.scalar.activation(selT[:, b * SEQ:(b + 1) * SEQ], ps[:, 4, 0:SEQ], ACT.Copy).then_inc(st_cp, 1)
                for r in range(4):
                    act.wait_ge(gat, p * 4 + r + 1)
                    nc.scalar.activation((XT_h, XT_l)[r // 2][:, 4 * (r % 2):4 * (r % 2) + 4, tok[b]],
                                         ps[:, 6 + r % 2, :].rearrange("p (c n) -> p c n", c=4), ACT.Copy)\
                        .then_inc(gat_cp, 1)

            def sigm(U, j0, j):
                sigmoid_slice(U.count(j0 + 2 * j + 1), ps[:, j % 2, 0:256], moe_sgm[:, (j % 2) * 256:(j % 2 + 1) * 256])

            def hi(q, j):
                act.wait_ge(g_tr, q * SLICES + j + 1)
                nc.scalar.activation(moe_gT3[0][:, 2 * j:2 * j + 2, :],
                                     ps[:, 4 + j % 2, 0:256].rearrange("p (a n) -> p a n", a=2), ACT.Copy)\
                    .then_inc(g_hi, 1)

            def expert(p, b, U, j0, last_split, gather_next, first=False, split_first=False):
                if first:
                    gather_copy(p, b)
                    if split_first:
                        for j in range(AHEAD):
                            split_hi(act, U, j0 + j)
                for j in range(SLICES):
                    if j >= 1:
                        sigm(U, j0, j - 1)
                    if j >= 2:
                        hi(p + 1, j - 2)
                    for a in range(2):
                        split_hi(act, U, j0 + 2 * j + AHEAD + a)
                for u in range(SLICES):
                    if u == 0:
                        sigm(U, j0, SLICES - 1)
                        hi(p + 1, SLICES - 2)
                        if gather_next:
                            gather_copy(p + 1, 1 - b)
                    if u == 1:
                        hi(p + 1, SLICES - 1)
                    if 2 * SLICES + u + AHEAD <= last_split:
                        split_hi(act, U, j0 + 2 * SLICES + u + AHEAD)
                act.wait_ge(unit_used, U.count(j0 + FFN_UNITS - 1))
                nc.scalar.activation(xs3[:, b, :].rearrange("p (a n) -> p a n", a=2), ps[:, 2:4, :], ACT.Copy)\
                    .then_inc(y_cp, 1)

            gather_copy(0, 0)
            expert(0, 0, Units(MOE_BASE), 0, FFN_UNITS + 1, True)
            with act.Fori(0, E // 2 - 1) as i:
                U = Units(MOE_BASE + FFN_UNITS, i, 2 * FFN_UNITS)
                expert(2 * i + 1, 1, U, 0, FFN_UNITS + 1, True)
                expert(2 * i + 2, 0, U, FFN_UNITS, FFN_UNITS + 1, True)
            U = Units(MOE_BASE)
            expert(E - 1, 1, U, (E - 1) * FFN_UNITS, FFN_UNITS - 1, False)
            act.wait_ge(table_ready, 1)
            n_over = act.value_load(otab[0:1, 0:1], min_val=0, max_val=3)
            with act.If(n_over > 0):
                with act.Fori(0, n_over) as k:
                    expert(k + E, 0, Units(OVER_BASE, k, FFN_UNITS, SPLIT), 0, FFN_UNITS - 1, False, True, True)

        @block.tensor
        def _(pe):
            pe.wait_ge(first_in, 16)

            def transpose(o, i):
                return nc.tensor.transpose(o, i, ident)

            def norm_T(n, half):
                if n == 0:
                    pe.wait_ge(x_in[half], 16)
                else:
                    pe.wait_ge(h_half, 2 * (n - 1) + half + 1)
                for r in (2 * half, 2 * half + 1):
                    for a in range(2):
                        for t in range(TT):
                            c = 2 * r + a
                            last = transpose(ps[:, 4 + r, a * SEQ + t * P:a * SEQ + (t + 1) * P],
                                             h[:, t, c * P:(c + 1) * P])
                    last.then_inc(xt_tr, 1)

            def mixers(l):
                U = Units(MIX_BASE[l])
                if l == 0:
                    norm_T(0, 0)
                    norm_T(0, 1)
                zqk = mx(ZQK, 2048).rearrange("p (t n) -> p t n", t=TT)
                zr = mx(ZR, 1024).rearrange("p (t n) -> p t n", t=TT)
                qkT = mx(QKT, 2048).rearrange("p (b n) -> p b n", b=8)
                retT = mx(RETT, 1024).rearrange("p (b n) -> p b n", b=4)
                rin = mx(RIN, HEADS * 384).rearrange("p (h n) -> p h n", h=HEADS)
                rv = mx(ZRV, 1024).rearrange("p (t n) -> p t n", t=TT)
                va = mx(ZV, 1024).rearrange("p (t n) -> p t n", t=TT)
                pd0 = mx(ZR, 512).rearrange("p (h n) -> p h n", h=4)
                pd1 = mx(ZQK, 1024).rearrange("p (h n) -> p h n", h=4)
                pdT = mx(QKT, 1536).rearrange("p (b n) -> p b n", b=12)

                def zt(r):
                    for a in range(2):
                        for t in range(TT):
                            src = zqk[:, t, (2 * r + a) * P:(2 * r + a + 1) * P] if r < 4 else \
                                zr[:, t, (2 * (r - 4) + a) * P:(2 * (r - 4) + a + 1) * P]
                            last = transpose(ps[:, 4 + r % 4, (a * 2 + t) * P:(a * 2 + t + 1) * P], src)
                    last.then_inc(zt_tr, 1)

                def ret_scores(hd):
                    part = slice((hd % 2) * HD, (hd % 2 + 1) * HD)
                    q, k = retT[part, hd // 2], retT[part, 2 + hd // 2]
                    bank = 4 + hd % 2
                    nc.tensor.matmul(ps[:, bank, 0:SEQ], k[:, 0:P], q, start=True, stop=True)
                    nc.tensor.matmul(ps[:, bank, SEQ:SEQ + P], k[:, P:SEQ], q[:, P:SEQ], start=True, stop=True)\
                        .then_inc(ret_s, 1)

                def da_scores(k):
                    t = 1 if k < 2 else 0
                    n = P * (t + 1)
                    for hd in ((0, 1), (2, 3), (0, 1, 2, 3))[k]:
                        a = hd % 2 if k < 2 else hd
                        for c in range(2):
                            part = slice(c * HD, (c + 1) * HD)
                            last = nc.tensor.matmul(ps[:, (6, 6, 4)[k] + c, a * n:(a + 1) * n],
                                                    qkT[part, hd, tok[t]], qkT[part, 4 + hd, 0:n],
                                                    start=True, stop=True)
                    last.then_inc(da_s, 1)

                def ret_out():
                    for hd in range(HEADS):
                        cs = slice(hd * VD, (hd + 1) * VD)
                        nc.tensor.matmul(ps[:, 6, cs], rin[:, hd, 0:P], rv[:, 0, cs], start=True, stop=True)
                        nc.tensor.matmul(ps[:, 7, cs], rin[:, hd, P:SEQ], rv[:, 0, cs], start=True, stop=False)
                        last = nc.tensor.matmul(ps[:, 7, cs], rin[:, hd, SEQ:SEQ + P], rv[:, 1, cs],
                                                start=False, stop=True)
                    last.then_inc(ret_o, 1)

                def da_out(t):
                    for hd in range(HEADS):
                        cs = slice(hd * VD, (hd + 1) * VD)
                        if t == 1:
                            nc.tensor.matmul(ps[:, 4, cs], pdT[:, 2 * hd], va[:, 0, cs], start=True, stop=False)
                            last = nc.tensor.matmul(ps[:, 4, cs], pdT[:, 1 + 2 * hd], va[:, 1, cs],
                                                    start=False, stop=True)
                        else:
                            last = nc.tensor.matmul(ps[:, 5, cs], pdT[:, 8 + hd], va[:, 0, cs], start=True, stop=True)
                    last.then_inc(da_o, 1)

                yv = xs[:, :].rearrange("p (m t n) -> p m t n", m=2, t=TT)

                def yt(m):
                    pe.wait_ge(yr_ready if m else ya_ready, l + 1)
                    for r in range(2):
                        for a in range(2):
                            for t in range(TT):
                                c = 2 * r + a
                                last = transpose(ps[:, (4, 6)[m] + r, (a * 2 + t) * P:(a * 2 + t + 1) * P],
                                                 yv[:, m, t, c * P:(c + 1) * P])
                        last.then_inc(yt_tr, 1)

                for n in range(2 * IN_GROUPS):
                    g, half = divmod(n, 2)
                    if n < 2:
                        pe.wait_ge(xt_lo, 8 * l + 2 * n + 2)
                    if half == 0 and g >= 2:
                        pe.wait_ge(in_evac, IN_GROUPS * l + g - 1)
                    outs = [(ps[:, 2 * (g % 2) + t, :], tok[t]) for t in range(TT)]
                    late = (lambda: norm_T(2 * l, 1)) if n == 0 and l > 0 else (lambda: yt(1)) if n == 19 else None
                    gemm_unit(pe, U, n, outs, (XT_h, XT_l), range(4 * half, 4 * half + 4), half == 0, half == 1,
                              late)
                    if n == 9:
                        pe.wait_ge(zqk_ready, l + 1)
                        for r in range(4):
                            zt(r)
                    if n == 10:
                        pe.wait_ge(zr_ready, l + 1)
                        pe.wait_ge(zt_cp, 6 * l + 2)
                        zt(4)
                        zt(5)
                    if n == 11:
                        pe.wait_ge(zt_cp, 6 * l + 4)
                        da_scores(0)
                        pe.wait_ge(zt_cp, 6 * l + 6)
                        ret_scores(0)
                        ret_scores(1)
                    if n == 12:
                        pe.wait_ge(ret_w, 4 * l + 2)
                        ret_scores(2)
                        ret_scores(3)
                    if n == 13:
                        pe.wait_ge(exp_done, 3 * l + 1)
                        da_scores(1)
                    if n == 14:
                        pe.wait_ge(ret_w, 4 * l + 4)
                        da_scores(2)
                    if n == 15:
                        pe.wait_ge(exp_done, 3 * l + 2)
                        ret_out()
                    if n == 16:
                        pe.wait_ge(exp_done, 3 * l + 3)
                        pe.wait_ge(pd_ready, 2 * l + 1)
                        for r in range(2):
                            for a in range(4):
                                last = transpose(ps[:, 4 + r, a * P:(a + 1) * P], pd1[:, 2 * r + a // 2, tok[a % 2]])
                            last.then_inc(pd_tr, 1)
                    if n == 17:
                        pe.wait_ge(pd_cp, 3 * l + 2)
                        da_out(1)
                        pe.wait_ge(pd_ready, 2 * l + 2)
                        for hd in range(HEADS):
                            last = transpose(ps[:, 5, hd * P:(hd + 1) * P], pd0[:, hd])
                        last.then_inc(pd_tr, 1)
                    if n == 18:
                        pe.wait_ge(pd_cp, 3 * l + 3)
                        da_out(0)
                mg = mx(SGA, 2048).rearrange("p (t n) -> p t n", t=TT)

                def mt(half):
                    pe.wait_ge(m_ready, 2 * l + half + 1)
                    for r in (2 * half, 2 * half + 1):
                        for a in range(2):
                            for t in range(TT):
                                c = 2 * r + a
                                last = transpose(ps[:, 4 + r, (a * 2 + t) * P:(a * 2 + t + 1) * P],
                                                 mg[:, t, c * P:(c + 1) * P])
                        last.then_inc(mt_tr, 1)

                for u in range(4):
                    if u == 0:
                        pe.wait_ge(yt_lo, 4 * l + 2)
                        pe.wait_ge(in_evac, IN_GROUPS * l + 9)
                    if u == 1:
                        pe.wait_ge(yt_lo, 4 * l + 4)
                        pe.wait_ge(in_evac, IN_GROUPS * l + 10)
                    b = PROJ_BANK[u]
                    between = (lambda: yt(0)) if u == 0 else None
                    gemm_unit(pe, U, 2 * IN_GROUPS + u, [(ps[:, b + t, :], tok[t]) for t in range(TT)],
                              (XT_h, XT_l) if u % 2 else (YR_h, YR_l), range(4), True, True, between)
                    if u == 2:
                        mt(0)
                for u in range(4):
                    n, half = divmod(u, 2)
                    if u < 2:
                        pe.wait_ge(mt_lo, 4 * l + 2 * u + 2)
                    outs = [(ps[:, 2 * n + t, :], tok[t]) for t in range(TT)]
                    between = {0: lambda: mt(1), 2: lambda: norm_T(2 * l + 1, 0)}.get(u)
                    gemm_unit(pe, U, 2 * IN_GROUPS + 4 + u, outs, (MT_h, MT_l), range(4 * half, 4 * half + 4),
                              half == 0, half == 1, between)

            def dense():
                U = Units(DENSE_BASE)

                def g_transposes(j):
                    pe.wait_ge(g_ready, j + 1)
                    if j >= 2:
                        pe.wait_ge(g_lo, j - 1)
                    gv = gbuf[:, (j % 2) * 512:(j % 2 + 1) * 512].rearrange("p (t n) -> p t n", t=TT)
                    for a in range(2):
                        for t in range(TT):
                            last = transpose(ps[:, 4 + j % 2, (a * 2 + t) * P:(a * 2 + t + 1) * P],
                                             gv[:, t, a * P:(a + 1) * P])
                    last.then_inc(g_tr, 1)
                for j in range(SLICES):
                    if j >= 2:
                        pe.wait_ge(g_ready, j - 1)
                    outs = [(ps[:, 2 * (j % 2) + t, :], tok[t]) for t in range(TT)]
                    for half in range(2):
                        if j == 0:
                            pe.wait_ge(xt_lo, 4 + 2 * half + 2)
                            pe.wait_ge(h_half, 1)
                        late = (lambda: norm_T(1, 1)) if j == 0 and half == 0 else None
                        gemm_unit(pe, U, 2 * j + half, outs, (XT_h, XT_l), range(4 * half, 4 * half + 4),
                                  half == 0, half == 1, late)
                    if j >= 1:
                        g_transposes(j - 1)
                down_outs = [((2, 3), tok[0]), ((6, 7), tok[1])]
                for u in range(SLICES - 2):
                    pe.wait_ge(g_lo, u + 1)
                    down_unit(pe, U, 2 * SLICES + u, down_outs, gT3, u)
                    if u == 0:
                        g_transposes(SLICES - 1)
                pe.wait_ge(g_lo, SLICES)
                pe.wait_ge(lo_ready, U.count(FFN_UNITS - 1))
                for n in range(2):
                    for u in (SLICES - 2, SLICES - 1):
                        s = U.split_slot(2 * SLICES + u)
                        for a in range(2):
                            b = slice(a * D + n * 512, a * D + (n + 1) * 512)
                            for banks, cols in down_outs:
                                last = product(ps[:, banks[n], :], gT3[0][:, 2 * u + a, cols], gT3[1][:, 2 * u + a, cols],
                                               wh[:, s, b], wl[:, s, b], False, u == SLICES - 1 and a == 1)
                            if n == 1 and u == SLICES - 2 and a == 0:
                                norm_T(2, 0)
                        if n == 1:
                            last.then_inc(unit_used, 1)
                    if n == 0:
                        last.then_inc(down_half, 1)

            def down_unit(pe, U, j, outs, gT, u):
                pe.wait_ge(lo_ready, U.count(j))
                s = U.split_slot(j)
                for a in range(2):
                    for banks, cols in outs:
                        for n in range(2):
                            b = slice(a * D + n * 512, a * D + (n + 1) * 512)
                            last = product(ps[:, banks[n], :], gT[0][:, 2 * u + a, cols], gT[1][:, 2 * u + a, cols],
                                           wh[:, s, b], wl[:, s, b], u == 0 and a == 0, u == SLICES - 1 and a == 1)
                last.then_inc(unit_used, 1)

            mixers(0)
            dense()
            mixers(1)
            norm_T(3, 1)
            pe.wait_ge(xt_lo, 16)
            pe.wait_ge(h_half, 6)
            pe.wait_ge(wr_lo, 1)
            for c in range(KC):
                for a, xT in enumerate((XT_h, XT_l)):
                    last = nc.tensor.matmul(ps[0:2 * E, 0, 0:SEQ], wr_hl[:, c, :], xT[:, c, :],
                                            start=c == 0 and a == 0, stop=c == KC - 1 and a == 1)
            last.then_inc(logit, 1)
            pe.wait_ge(consts_in, 48)
            pe.wait_ge(lgt_cp, 1)
            for t in range(TT):
                last = nc.tensor.matmul(ps[:, 2, t * E:(t + 1) * E], lgT[:, tok[t]], stack[0:2 * E, :],
                                        start=True, stop=True)
            last.then_inc(logit, 1)
            pe.wait_ge(routed_ready, 1)
            pe.wait_ge(pool_const, 2)
            nc.tensor.matmul(ps[:, 1, 0:E], before, routed[:, 0, :], start=True, stop=True)
            nc.tensor.matmul(ps[:, 1, E:2 * E], before, routed[:, 1, :], start=True, stop=False)
            nc.tensor.matmul(ps[:, 1, E:2 * E], ones[:, :], routed[:, 0, :], start=False, stop=True)
            nc.tensor.matmul(ps[:, 1, 2 * E:3 * E], ones[:, :], routed[:, 0, :], start=True, stop=False)
            nc.tensor.matmul(ps[:, 1, 2 * E:3 * E], ones[:, :], routed[:, 1, :], start=False, stop=True)\
                .then_inc(ranked, 1)

            def gather(p, b):
                pe.wait_ge(sel_ready, p + 1)
                for t in range(TT):
                    last = transpose(ps[:, 4, tok[t]], sel_r[:, (2 * b + t) * P:(2 * b + t + 1) * P].bitcast(F32))
                last.then_inc(st_tr, 1)
                pe.wait_ge(hn_hi, 1)
                for r in range(4):
                    if r >= 2:
                        pe.wait_ge(hn_lo, 1)
                        pe.wait_ge(gat_cp, p * 4 + r - 1)
                    hn = (hn_h, hn_l)[r // 2][:, :].rearrange("p (t n) -> p t n", t=TT)
                    for a in range(4):
                        c = 4 * (r % 2) + a
                        for t in range(TT):
                            last = nc.tensor.matmul(ps[:, 6 + r % 2, a * P:(a + 1) * P], hn[:, t, c * P:(c + 1) * P],
                                                    sel_r[:, (2 * b + t) * P:(2 * b + t + 1) * P],
                                                    start=t == 0, stop=t == TT - 1)
                    last.then_inc(gat, 1)

            def g_transposes(p, j, gathered=False):
                if gathered:
                    pe.wait_ge(st_cp, p + 2)
                pe.wait_ge(g_ready, (p + 1) * SLICES + j + 1)
                if j >= 2:
                    pe.wait_ge(g_lo, (p + 1) * SLICES + j - 1)
                if j == 0:
                    pe.wait_ge(st_cp, p + 1)
                for a in range(2):
                    last = transpose(ps[:, 4 + j % 2, a * P:(a + 1) * P],
                                     moe_gbuf[:, (j % 2) * 256 + a * P:(j % 2) * 256 + (a + 1) * P])
                last.then_inc(g_tr, 1)

            def scatter(p, b, r):
                t, n = divmod(r, 2)
                if r == 0:
                    pe.wait_ge(y_cp, p + 1)
                if r >= 2:
                    pe.wait_ge(h_add, p * 4 + r - 1)
                nc.tensor.matmul(ps[:, 6 + r % 2, :], selT[:, b * SEQ + t * P:b * SEQ + (t + 1) * P],
                                 xs3[:, b, n * 512:(n + 1) * 512], start=True, stop=True).then_inc(sc_done, 1)

            def expert(p, b, U, j0, first, scatter_prev, gather_next, scatter_here):
                if first:
                    gather(p, b)
                pe.wait_ge(gat_cp, p * 4 + 4)
                for j in range(SLICES):
                    if j >= 2:
                        pe.wait_ge(g_ready, (p + 1) * SLICES + j - 1)
                    for half in range(2):
                        gemm_unit(pe, U, j0 + 2 * j + half, [(ps[:, j % 2, :], tok[b])], (XT_h, XT_l),
                                         range(4 * half, 4 * half + 4), half == 0, half == 1)
                    if j >= 1:
                        g_transposes(p, j - 1)
                    if 1 <= j <= 4 and scatter_prev:
                        scatter(p - 1, 1 - b, j - 1)
                if gather_next:
                    if scatter_prev:
                        pe.wait_ge(h_add, p * 4)
                    pe.wait_ge(g_lo, (p + 1) * SLICES + SLICES - 2)
                    gather(p + 1, 1 - b)
                for u in range(SLICES):
                    pe.wait_ge(g_lo, (p + 1) * SLICES + u + 1)
                    down_unit(pe, U, j0 + 2 * SLICES + u, [((2, 3), slice(0, P))], moe_gT3, u)
                    if u == 0:
                        g_transposes(p, SLICES - 1, gather_next)
                if scatter_here:
                    if scatter_prev:
                        pe.wait_ge(h_add, p * 4)
                    for r in range(4):
                        scatter(p, b, r)
                    pe.wait_ge(h_add, p * 4 + 4)

            gather(0, 0)
            expert(0, 0, Units(MOE_BASE), 0, False, False, True, False)
            with pe.Fori(0, E // 2 - 1) as i:
                U = Units(MOE_BASE + FFN_UNITS, i, 2 * FFN_UNITS)
                expert(2 * i + 1, 1, U, 0, False, True, True, False)
                expert(2 * i + 2, 0, U, FFN_UNITS, False, True, True, False)
            U = Units(MOE_BASE)
            expert(E - 1, 1, U, (E - 1) * FFN_UNITS, False, True, False, True)
            pe.wait_ge(table_ready, 1)
            n_over = pe.value_load(otab[0:1, 0:1], min_val=0, max_val=3)
            with pe.If(n_over > 0):
                with pe.Fori(0, n_over) as k:
                    expert(k + E, 0, Units(OVER_BASE, k, FFN_UNITS, SPLIT), 0, True, False, False, True)

        @block.vector
        def _(dve):
            chain = [0]

            def link(ins):
                chain[0] += 1
                ins.then_inc(dchain, 1)
                dve.wait_ge(dchain, chain[0])

            tt, ts, stt = nc.vector.tensor_tensor, nc.vector.tensor_scalar, nc.vector.scalar_tensor_tensor
            copy, reduce = nc.vector.tensor_copy, nc.vector.tensor_reduce
            roots = [0]

            def ask_root(cols, scale):
                ts(ssq[:, cols], ssq[:, cols], scale, EPS, ALU.mult, ALU.add).then_inc(ms_ready, 1)
                roots[0] += 1

            def wait_root():
                dve.wait_ge(rs_ready, roots[0])

            def small_tables():
                dve.wait_ge(consts_in, 48)
                link(copy(pos_f[:, :], pos_i[:, :]))
                for t in range(TT):
                    ins = ts(ang[:, 2, t, :], freq, pos_f[:, t:t + 1], None, ALU.mult)
                link(ins)
                magic = 1.5 * 2 ** 23
                turn = 2 * math.pi
                c1 = 6.28125
                c2 = float((np.array([turn - c1], np.float32).view(np.uint32) & np.uint32(0xFFFFF000)).view(np.float32)[0])
                c3 = turn - c1 - c2
                for a, k in ((0, sin), (1, cos)):
                    k, r = k[:, :, :], ang[:, a]
                    if a:
                        link(ts(k, ang[:, 2], 1 / turn, 0.25, ALU.mult, ALU.add))
                        link(ts(k, k, magic, magic, ALU.add, ALU.subtract))
                    else:
                        link(ts(k, ang[:, 2], 1 / turn, magic, ALU.mult, ALU.add))
                        link(ts(k, k, magic, None, ALU.subtract))
                    link(stt(r, k, -c1, ang[:, 2], ALU.mult, ALU.add))
                    link(stt(r, k, -c2, r, ALU.mult, ALU.add))
                    link(stt(r, k, -c3, r, ALU.mult, ALU.add))
                    if a:
                        link(ts(r, r, math.pi / 2, None, ALU.add))
                    pi = 3.1415925
                    ins = ts(r, r, pi, -pi, ALU.min, ALU.max)
                ins.then_inc(ang_ready, 1)
                link(tt(lamp[:, :, :, :], lamv[:, 0::2], lamv[:, 1::2], ALU.mult))
                reduce(lams[:, :, :], lamp[:, :, :, :], AX.X, ALU.add).then_inc(lam_sum, 1)
                for l in range(DEPTH):
                    ts(g_subs[:, l:l + 1], g_sub[:, l:l + 1], 1.0 - lambda_init(l), None, ALU.mult)

            def small_tables_end():
                dve.wait_ge(lam_exp, 1)
                link(tt(lamn[:, :], lame[:, 1], lame[:, 0], ALU.subtract))
                for l in range(DEPTH):
                    ins = ts(lamn[:, l:l + 1], lamn[:, l:l + 1], -lambda_init(l), None, ALU.add)
                link(ins)
                dve.wait_ge(wr_hi, 1)
                tt(wr_hl[:, :, E:2 * E], wr, wr_hl[:, :, 0:E].bitcast(F32), ALU.subtract).then_inc(wr_lo, 1)
                dve.wait_ge(sin_ready, 1)

            split_to = [0]

            def split_until(U, j):
                while split_to[0] <= U.base + j:
                    split_lo(dve, Units(0), split_to[0])
                    split_to[0] += 1

            def norm_lo(n, half, gain):
                for r in (2 * half, 2 * half + 1):
                    dve.wait_ge(xt_hi, 4 * n + r + 1)
                    for a in range(2):
                        c = 2 * r + a
                        ins = stt(XT_l[:, c, :], ps[:, 4 + r, a * SEQ:(a + 1) * SEQ], gain[:, c:c + 1],
                                  XT_h[:, c, :].bitcast(F32), ALU.mult, ALU.subtract)
                    ins.then_inc(xt_lo, 1)

            def norm_factors(n):
                dve.wait_ge(sq_done, 2 * n + 2)
                ts(ssq[:, 0:TT], ssq[:, 0:TT], 1.0 / D, EPS, ALU.mult, ALU.add).then_inc(ms_ready, 1)
                roots[0] += 1

            def rotate(x1, x2, cs, sn, tmp):
                tt(tmp[0], x1, cs, ALU.mult)
                tt(tmp[1], x2, sn, ALU.mult)
                tt(tmp[2], x1, sn, ALU.mult)
                link(tt(tmp[3], x2, cs, ALU.mult))
                tt(x1, tmp[0], tmp[1], ALU.subtract)
                return tt(x2, tmp[2], tmp[3], ALU.add)

            def mixers(l):
                U = Units(MIX_BASE[l])
                gain = g_attn[:, l, :]
                if l == 0:
                    norm_lo(0, 0, gain)
                    split_until(U, 0)
                    norm_lo(0, 1, gain)
                    split_until(U, 1)
                zq = mx(ZQK, 2048)
                zq32 = zq.rearrange("p (g d) -> p g d", d=HD)
                zq4 = zq.rearrange("p (t g d) -> p t g d", t=TT, d=HD)
                rin = mx(RIN, HEADS * 384).rearrange("p (h n) -> p h n", h=HEADS)
                ya = xs[:, 0:1024].rearrange("p (t h n) -> p t h n", t=TT, h=HEADS)
                ro = ps[:, 6:8, :].rearrange("p b (h n) -> p (b h) n", h=HEADS)

                def decay_scores(hd):
                    dve.wait_ge(ret_s, 4 * l + hd + 1)
                    bank = 4 + hd % 2
                    tt(rin[:, hd, 0:SEQ], ps[:, bank, 0:SEQ], decay[:, hd, :], ALU.mult)
                    tt(rin[:, hd, SEQ:384], ps[:, bank, SEQ:384], decay[:, hd, 0:P], ALU.mult).then_inc(ret_w, 1)

                def maxima(k):
                    dve.wait_ge(da_s, 3 * l + k + 1)
                    b, m = (6, 6, 4)[k], (2, 2, 4)[k]
                    for c in range(2):
                        sc = ps[:, b + c, :].rearrange("p (h n) -> p h n", h=m)
                        diag = sc[:, :, P:SEQ] if k < 2 else sc
                        ins = tt(diag, diag, mask.unsqueeze(1).to_broadcast([P, m, P]), ALU.add)
                    link(ins)
                    t = 1 if k < 2 else 0
                    cols = slice(2 * k, 2 * k + 2) if k < 2 else slice(0, 4)
                    mv = mxs[:, t, :].rearrange("p (c h) -> p c h", c=2)[:, :, cols]
                    nv = nbs[:, t, :].rearrange("p (c h) -> p c h", c=2)[:, :, cols]
                    link(reduce(mv, ps[:, b:b + 2, :].rearrange("p c (h n) -> p c h n", h=m), AX.X, ALU.max))
                    ts(nv, mv, -DA_SCALE, None, ALU.mult).then_inc(nb_ready, 1)

                def probabilities(t):
                    e, n = ((mx(ZR, 1024), P), (mx(ZQK, 2048), SEQ))[t]
                    e = e.rearrange("p (a n) -> p a n", a=8)
                    dve.wait_ge(exp_done, 3 * l + (3, 2)[t])
                    link(nc.vector.reciprocal(rcs[:, t, :], sms[:, t, :]))
                    link(stt(rcs[:, t, 4:8], rcs[:, t, 4:8], lamn[:, l:l + 1], sms[:, t, 0:4], ALU.mult, ALU.mult))
                    for hd in range(HEADS):
                        ins = stt(e[:, hd], e[:, 4 + hd], rcs[:, t, 4 + hd:5 + hd], e[:, hd], ALU.mult, ALU.add)
                    ins.then_inc(pd_ready, 1)

                def retention_means():
                    dve.wait_ge(ret_o, l + 1)
                    link(reduce(mu[:, :], ro, AX.X, ALU.add))
                    ts(mu[:, :], mu[:, :], -1.0 / VD, None, ALU.mult).then_inc(mu_ready, 1)

                def group_root():
                    dve.wait_ge(gn_sq, l + 1)
                    ask_root(slice(0, 8), 1.0 / VD)

                def group_offsets():
                    wait_root()
                    dve.wait_ge(mu_ready, l + 1)
                    tt(mur[:, :], mu[:, :], rst[:, 0:8], ALU.mult).then_inc(mur_ready, 1)

                for n in range(2 * IN_GROUPS):
                    if n == 0:
                        if l > 0:
                            norm_lo(2 * l, 1, gain)
                        norm_factors(2 * l)
                    if l == 0 and n == 1:
                        small_tables()
                    if l == 0 and n == 2:
                        small_tables_end()
                    if n == 5:
                        dve.wait_ge(in_evac, IN_GROUPS * l + 2)
                        link(reduce(ssq[:, 0:32], xs[:, :].rearrange("p (g d) -> p g d", d=HD), AX.X, ALU.add))
                        ask_root(slice(0, 32), 1.0 / HD)
                    if n == 6:
                        wait_root()
                        link(tt(zq32, zq32, rst[:, 0:32].unsqueeze(2).to_broadcast([P, 32, HD]), ALU.mult))
                    if n == 7:
                        for t in range(TT):
                            for a in range(2):
                                v = zq4[:, t, 8 * a:8 * a + 8]
                                ins = tt(v, v, g_qk[:, l, a, :].unsqueeze(1).to_broadcast([P, 8, HD]), ALU.mult)
                        link(ins)
                    if n == 8:
                        shape = [P, TT, 16, DA_HALF]
                        tmp = [xs[:, a * 256:(a + 1) * 256].rearrange("p (t g d) -> p t g d", t=TT, d=DA_HALF)
                               for a in range(4)]
                        rotate(zq4[:, :, :, 0:DA_HALF], zq4[:, :, :, DA_HALF:2 * DA_HALF],
                               cos[:, :, 0:DA_HALF].unsqueeze(2).to_broadcast(shape),
                               sin[:, :, 0:DA_HALF].unsqueeze(2).to_broadcast(shape), tmp).then_inc(zqk_ready, 1)
                    if n == 12:
                        maxima(0)
                        decay_scores(0)
                        decay_scores(1)
                    if n == 13:
                        decay_scores(2)
                        decay_scores(3)
                    if n == 14:
                        maxima(1)
                    if n == 15:
                        maxima(2)
                    if n == 16:
                        probabilities(1)
                        retention_means()
                    if n == 17:
                        probabilities(0)
                    if n == 18:
                        group_offsets()
                    if n == 19:
                        dve.wait_ge(gn_out, l + 1)
                        dve.wait_ge(silu_ready, l + 1)
                        tt(xs[:, 1024:2048], xs[:, 1024:2048], mx(ZG, 1024), ALU.mult).then_inc(yr_ready, 1)
                    split_until(U, n + AHEAD)
                    if n == 17:
                        group_root()
                dve.wait_ge(osq, 2 * l + 2)
                ask_root(slice(8, 16), 1.0 / VD)

                def yt(r):
                    dve.wait_ge(yt_hi, 4 * l + r + 1)
                    c = slice(2 * (r % 2), 2 * (r % 2) + 2)
                    hi, lo = (YR_h, YR_l) if r < 2 else (XT_h, XT_l)
                    stt(lo[:, c, :], ps[:, (6, 7, 4, 5)[r], :].rearrange("p (a n) -> p a n", a=2),
                        1.0 if r < 2 else g_subs[:, l:l + 1], hi[:, c, :].bitcast(F32),
                        ALU.mult, ALU.subtract).then_inc(yt_lo, 1)

                yt(0)
                yt(1)
                wait_root()
                link(tt(yaf[:, :].rearrange("p (t h) -> p t h", t=TT), rst[:, 8:16].rearrange("p (t h) -> p t h", t=TT),
                        rcs[:, :, 0:HEADS], ALU.mult))
                for t in range(TT):
                    o = ps[:, 5 - t, :].rearrange("p (h n) -> p h n", h=HEADS)
                    ins = tt(ya[:, t], o, yaf[:, 4 * t:4 * t + 4].unsqueeze(2).to_broadcast([P, HEADS, VD]), ALU.mult)
                ins.then_inc(ya_ready, 1)
                split_until(U, 22)
                yt(2)
                yt(3)

                def gate_proj(u):
                    n = u // 2
                    gate = mx(SGA if u % 2 else SGB, 2048)
                    gate = gate.rearrange("p (t n) -> p t n", t=TT)[:, :, n * 512:(n + 1) * 512]
                    dve.wait_ge(unit_used, U.count(2 * IN_GROUPS + u))
                    ins = tt(gate, gate, ps[:, PROJ_BANK[u]:PROJ_BANK[u] + 2, :], ALU.mult)
                    if u % 2 == 0:
                        ins.then_inc(proj_evac, 1)
                    else:
                        link(ins)
                        dve.wait_ge(proj_evac, 2 * l + n + 1)
                        other = mx(SGB, 2048).rearrange("p (t n) -> p t n", t=TT)[:, :, n * 512:(n + 1) * 512]
                        tt(gate, gate, other, ALU.add).then_inc(m_ready, 1)

                def mt(half):
                    for r in (2 * half, 2 * half + 1):
                        dve.wait_ge(mt_hi, 4 * l + r + 1)
                        v = ps[:, 4 + r, :].rearrange("p (a n) -> p a n", a=2)
                        tt(MT_l[:, 2 * r:2 * r + 2, :], v, MT_h[:, 2 * r:2 * r + 2, :].bitcast(F32), ALU.subtract)\
                            .then_inc(mt_lo, 1)

                def add_h(n):
                    dve.wait_ge(unit_used, U.count(2 * IN_GROUPS + 4 + 2 * n + 1))
                    v = h[:, :, n * 512:(n + 1) * 512]
                    tt(v, ps[:, 2 * n:2 * n + 2, :], v, ALU.add).then_inc(h_half, 1)

                gate_proj(0)
                split_until(U, 23)
                gate_proj(1)
                split_until(U, 24)
                gate_proj(2)
                mt(0)
                split_until(U, 25)
                gate_proj(3)
                mt(1)
                split_until(U, 27)
                add_h(0)
                split_until(U, 28)
                norm_lo(2 * l + 1, 0, g_ffn[:, l, :])
                split_until(U, 29)
                add_h(1)

            def dense():
                U = Units(DENSE_BASE)

                def g(j):
                    dve.wait_ge(sig_done, j + 1)
                    if j == 0:
                        dve.wait_ge(rs_ready, ROOTS)
                    b = 2 * (j % 2)
                    at = [slice((b + t) * 256, (b + t + 1) * 256) for t in range(TT)]
                    for t in range(TT):
                        ins = stt(gbuf[:, at[t]], ps[:, b + t, 0:256], rn[:, t:t + 1], sgm[:, at[t]], ALU.mult, ALU.mult)
                    ins.then_inc(g_half, 1)
                    dve.wait_ge(g_half, j + 1)
                    for t in range(TT):
                        ins = stt(gbuf[:, at[t]], ps[:, b + t, 256:512], rn[:, t:t + 1], gbuf[:, at[t]],
                                  ALU.mult, ALU.mult)
                    ins.then_inc(g_ready, 1)

                def lo(j):
                    dve.wait_ge(g_hi, j + 1)
                    tt(gT3[1][:, 2 * j:2 * j + 2, :], ps[:, 4 + j % 2, :].rearrange("p (a n) -> p a n", a=2),
                       gT3[0][:, 2 * j:2 * j + 2, :].bitcast(F32), ALU.subtract).then_inc(g_lo, 1)
                for j in range(SLICES):
                    if j == 0:
                        norm_lo(1, 1, g_ffn[:, 0, :])
                        norm_factors(1)
                    if j >= 1:
                        g(j - 1)
                    if j >= 2:
                        lo(j - 2)
                    split_until(U, 2 * j + 1 + AHEAD)
                for u in range(SLICES):
                    if u == 0:
                        g(SLICES - 1)
                        lo(SLICES - 2)
                    if u == 1:
                        lo(SLICES - 1)
                    if u < SLICES - 1:
                        split_until(U, 2 * SLICES + u + AHEAD)
                for n in range(2):
                    if n == 0:
                        dve.wait_ge(down_half, 1)
                    else:
                        dve.wait_ge(unit_used, U.count(FFN_UNITS - 1))
                    for t in range(TT):
                        v = h[:, t, n * 512:(n + 1) * 512]
                        ins = tt(v, ps[:, (2, 6)[t] + n, :], v, ALU.add)
                    ins.then_inc(h_half, 1)
                    if n == 0:
                        norm_lo(2, 0, g_attn[:, 1, :])
                split_until(U, FFN_UNITS + 1)

            mixers(0)
            dense()
            mixers(1)
            def select(b, e, places):
                for t in range(TT):
                    r = places[:, t, bass.ds(e, 1)]
                    ins = ts(sel_r[:, (2 * b + t) * P:(2 * b + t + 1) * P], iota, r, None, ALU.is_equal)
                ins.then_inc(sel_ready, 1)

            norm_lo(3, 1, g_ffn[:, 1, :])
            dve.wait_ge(h_half, 6)
            tt(xs3, h[:, :, :], g_moe.unsqueeze(1).to_broadcast([P, TT, D]), ALU.mult).then_inc(hg_ready, 1)
            norm_factors(3)
            dve.wait_ge(rs_ready, 2 * ROOTS)
            dve.wait_ge(logit, 2)
            for t in range(TT):
                ins = ts(lg[:, t, :], ps[:, 2, t * E:(t + 1) * E], rn[:, t:t + 1], None, ALU.mult)
            link(ins)
            for t in range(TT):
                ins = nc.vector.max(top[:, t, :], lg[:, t, :])
            link(ins)
            for t in range(TT):
                ins = nc.vector.max_index(tidx[:, t, :], top[:, t, :], lg[:, t, :])
            link(ins)
            tt(tdf[:, :], top[:, :, 1], top[:, :, 0], ALU.subtract).then_inc(te_in, 1)
            link(copy(tif[:, :, :], tidx[:, :, :]))
            for t in range(TT):
                for a in range(2):
                    ins = ts(oh[:, a, t, :], iota[:, 0:E], tif[:, t, a:a + 1], None, ALU.is_equal)
            link(ins)
            tt(routed[:, :, :], oh[:, 0], oh[:, 1], ALU.add).then_inc(routed_ready, 1)
            dve.wait_ge(routed_ready, 1)
            dve.wait_ge(ranked, 1)
            link(stt(rank1[:, :, :], ps[:, 1, 0:TT * E].rearrange("p (t e) -> p t e", t=TT), 1.0, routed[:, :, :],
                     ALU.add, ALU.mult))
            link(ts(rank[:, :, :], rank1[:, :, :], -1.0, None, ALU.add))
            select(0, 0, rank)
            dve.wait_ge(hg_ready, 1)
            dve.wait_ge(hn_hi, 1)
            for t in range(TT):
                ins = stt(hn_l[:, t * D:(t + 1) * D], xs3[:, t, :], rn[:, t:t + 1],
                          hn_h[:, t * D:(t + 1) * D].bitcast(F32), ALU.mult, ALU.subtract)
            ins.then_inc(hn_lo, 1)
            ts(rank2[:, :, :], rank1[:, :, :], -1.0 - P, None, ALU.add)
            dve.wait_ge(te_out, 1)
            link(ts(tw[:, 0, :], te[:, :], 1.0, None, ALU.add))
            link(nc.vector.reciprocal(tw[:, 1, :], tw[:, 0, :]))
            link(tt(tw[:, 2, :], te[:, :], tw[:, 1, :], ALU.mult))
            for t in range(TT):
                ins = ts(comb[:, t, :], oh[:, 0, t, :], tw[:, 1, t:t + 1], None, ALU.mult)
            link(ins)
            for t in range(TT):
                ins = stt(comb[:, t, :], oh[:, 1, t, :], tw[:, 2, t:t + 1], comb[:, t, :], ALU.mult, ALU.add)
            link(ins)
            link(ts(okey[:, 0, :], ps[:, 1, TT * E:(TT + 1) * E], float(P), None, ALU.is_gt))
            reduce(nover[:, :], okey[:, 0, :], AX.X, ALU.add)
            link(ts(okey[:, 1, :], iota[:, 0:E], -1.0, float(E), ALU.mult, ALU.add))
            link(tt(okey[:, 1, :], okey[:, 1, :], okey[:, 0, :], ALU.mult))
            link(nc.vector.max(okey[:, 2, :], okey[:, 1, :]))
            link(ts(okey[:, 2, :], okey[:, 2, :], -1.0, float(E), ALU.mult, ALU.add))
            ts(otab[:, 8:16], okey[:, 2, :], float(E - 1), None, ALU.min)
            copy(otab[:, 0:1], nover[:, :]).then_inc(table_ready, 1)

            def g(p, U, j0, j):
                dve.wait_ge(sig_done, (p + 1) * SLICES + j + 1)
                cols = slice((j % 2) * 256, (j % 2 + 1) * 256)
                tt(moe_gbuf[:, cols], ps[:, j % 2, 0:256], moe_sgm[:, cols], ALU.mult).then_inc(g_half, 1)
                dve.wait_ge(g_half, (p + 1) * SLICES + j + 1)
                tt(moe_gbuf[:, cols], ps[:, j % 2, 256:512], moe_gbuf[:, cols], ALU.mult).then_inc(g_ready, 1)

            def lo(p, j):
                dve.wait_ge(g_hi, (p + 1) * SLICES + j + 1)
                tt(moe_gT3[1][:, 2 * j:2 * j + 2, :], ps[:, 4 + j % 2, 0:256].rearrange("p (a n) -> p a n", a=2),
                   moe_gT3[0][:, 2 * j:2 * j + 2, :].bitcast(F32), ALU.subtract).then_inc(g_lo, 1)

            def add_back(p, e, r):
                t, n = divmod(r, 2)
                dve.wait_ge(sc_done, p * 4 + r + 1)
                v = h[:, t, n * 512:(n + 1) * 512]
                stt(v, ps[:, 6 + r % 2, :], comb[:, t, bass.ds(e, 1)], v, ALU.mult, ALU.add).then_inc(h_add, 1)

            def expert(p, b, U, j0, e, places, last_split, scatter_prev, e_next, scatter_here, first=False):
                if first:
                    select(b, e, places)
                    for j in range(AHEAD):
                        split_lo(dve, U, j0 + j)
                for j in range(SLICES):
                    if j >= 1:
                        g(p, U, j0, j - 1)
                    if j >= 2:
                        lo(p, j - 2)
                    if 2 <= j <= 5 and scatter_prev is not None:
                        add_back(p - 1, scatter_prev, j - 2)
                    if j == 7 and e_next is not None:
                        select(1 - b, e_next, places)
                    for a in range(2):
                        split_lo(dve, U, j0 + 2 * j + AHEAD + a)
                for u in range(SLICES):
                    if u == 0:
                        g(p, U, j0, SLICES - 1)
                        lo(p, SLICES - 2)
                    if u == 1:
                        lo(p, SLICES - 1)
                    if 2 * SLICES + u + AHEAD <= last_split:
                        split_lo(dve, U, j0 + 2 * SLICES + u + AHEAD)
                if scatter_here:
                    for r in range(4):
                        add_back(p, e, r)

            expert(0, 0, Units(MOE_BASE), 0, 0, rank, FFN_UNITS + 1, None, 1, False)
            with dve.Fori(0, E // 2 - 1) as i:
                U = Units(MOE_BASE + FFN_UNITS, i, 2 * FFN_UNITS)
                expert(2 * i + 1, 1, U, 0, 2 * i + 1, rank, FFN_UNITS + 1, 2 * i, 2 * i + 2, False)
                expert(2 * i + 2, 0, U, FFN_UNITS, 2 * i + 2, rank, FFN_UNITS + 1, 2 * i + 1, 2 * i + 3, False)
            U = Units(MOE_BASE)
            expert(E - 1, 1, U, (E - 1) * FFN_UNITS, E - 1, rank, FFN_UNITS - 1, E - 2, None, True)
            dve.wait_ge(table_ready, 1)
            n_over = dve.value_load(otab[0:1, 0:1], min_val=0, max_val=3)
            with dve.If(n_over > 0):
                with dve.Fori(0, n_over) as k:
                    e = dve.value_load(otab[0:1, bass.ds(k + 8, 1)], min_val=0, max_val=E - 1)
                    expert(k + E, 0, Units(OVER_BASE, k, FFN_UNITS, SPLIT), 0, e, rank2, FFN_UNITS - 1,
                           None, None, True, True)


def lambda_init(layer):
    return 0.8 - 0.6 * math.exp(-0.3 * layer)


BIG = ["w_in", "w_proj_da", "w_proj_ret", "w_out", "dense_w1", "dense_w3", "dense_w2", "moe_w1", "moe_w3",
       "moe_w2"]


def packed(inp):
    def chunked(g):
        return g.reshape(DEPTH, KC, P).transpose(2, 0, 1).reshape(P, DEPTH * KC)
    c = tables()
    c["g_attn"], c["g_ffn"] = chunked(inp["attn_norm"]), chunked(inp["ffn_norm"])
    c["g_sub"] = inp["da_subln"].T
    c["wr"] = inp["w_router"][0].reshape(KC, P, E).transpose(1, 0, 2).reshape(P, KC * E)
    r = {"g_qk": np.stack([inp["da_q_norm"], inp["da_k_norm"]], 1),
         "lam": np.stack([inp[n] for n in ("lam_q1", "lam_k1", "lam_q2", "lam_k2")]),
         "g_moe": inp["ffn_norm"][DEPTH - 1]}
    cols = np.concatenate([c[n] for n in COLS], axis=1)
    rows = np.concatenate([r[n].reshape(1, -1) for n in ROWS], axis=1)
    assert cols.shape == (P, COLS_W) and rows.shape == (1, ROWS_W)
    return np.ascontiguousarray(cols), np.ascontiguousarray(rows)


def kernel(**inputs):
    import concourse.bacc as bacc
    from concourse.bass_utils import run_bass_kernel_spmd

    nc = bacc.Bacc("TRN2", target_bir_lowering=False, num_devices=1)
    arrays, args = {}, []
    inp = {n: np.ascontiguousarray(a) for n, a in inputs.items()}
    cols, rows = packed(inp)
    tensors = [("x", inp["x"]), ("positions", np.ascontiguousarray(inp["positions"].reshape(TT, P).T))]
    tensors += [(n, inp[n]) for n in BIG] + [("cols", cols), ("rows", rows)]
    for name, a in tensors:
        arrays[f"in_{name}"] = a
        args.append(nc.dram_tensor(f"in_{name}", a.shape, mybir.dt.from_np(a.dtype), kind="ExternalInput").ap())
    args.append(nc.dram_tensor("out", (1, SEQ, D), F32, kind="ExternalOutput").ap())
    build(nc, *args)
    r = run_bass_kernel_spmd(nc, [arrays], core_ids=[0])
    return r.results[0]["out"]
```

```python
import math
from contextlib import ExitStack

import numpy as np

import concourse.bass as bass
from concourse import mybir

F32 = mybir.dt.float32
F32R = mybir.dt.float32r
I32 = mybir.dt.int32
U32 = mybir.dt.uint32
ALU = mybir.AluOpType
ACT = mybir.ActivationFunctionType
AX = mybir.AxisListType

P = 128
SEQ = 256
TT = SEQ // P
D = 1024
KC = D // P
DEPTH = 2
HEADS = 4
HD = 64
VD = 128
AW = HEADS * VD
IN_W = 5120
FF = 2816
FC = FF // P
E = 8
EPS = 1e-6
DA_SCALE = HD ** -0.5
DA_THETA, RET_THETA = 500000.0, 10000.0
DA_HALF, RET_HALF = HD // 8, HD // 2
NF = DA_HALF + RET_HALF
MASKED = -1.0e30

UNIT = 2048
RAW, SPLIT = 6, 3
SLICES = FF // 256
IN_GROUPS = IN_W // 512
MIX_UNITS = 2 * IN_GROUPS + 4 + 4
FFN_UNITS = 2 * SLICES + FC // 2
MIX_BASE = [0, MIX_UNITS + FFN_UNITS]
DENSE_BASE = MIX_UNITS
MOE_BASE = MIX_BASE[1] + MIX_UNITS
OVER_BASE = MOE_BASE + E * FFN_UNITS
IN_ORDER = [0, 1, 3, 4, 5, 2, 6, 7, 8, 9]
ROOTS = 6
PROJ_BANK = [0, 2, 6, 2]
AHEAD = 2

ZQK, ZV, ZR, ZRV, ZG = 0, 2048, 3072, 4096, 5120
SGA, SGB = 6144, 8192
QKT, RETT = 10240, 12288
RIN = 13312
MIX_WORDS = RIN + HEADS * 384


def _columns(widths):
    at, out = 0, {}
    for name, w in widths:
        out[name] = (at, w)
        at += w
    return out, at


COLS, COLS_W = _columns([("g_attn", DEPTH * KC), ("ident", P), ("g_ffn", DEPTH * KC), ("g_sub", DEPTH),
                         ("freq", NF), ("mask", P), ("iota", P), ("before", P), ("wr", KC * E),
                         ("stack", E), ("decay", HEADS * SEQ)])
COLS_FIRST = DEPTH * KC
COLS_LAST = COLS["decay"][0]
ROWS, ROWS_W = _columns([("g_qk", 2 * DEPTH * HD), ("lam", 4 * DEPTH * HD), ("g_moe", D)])


def tables():
    i = np.arange(P)
    c = {}
    c["ident"] = np.eye(P)
    c["mask"] = np.where(i[None, :] <= i[:, None], 0.0, MASKED)
    lg = np.log1p(-np.exp2(-5.0 - np.arange(HEADS)))
    rel = np.arange(SEQ)[None, :] - i[:, None]
    dec = np.where(rel[:, None] >= 0, np.exp(lg[None, :, None] * np.maximum(rel, 0)[:, None]), 0.0)
    c["decay"] = (dec * HD ** -0.5).reshape(P, HEADS * SEQ)
    f = np.concatenate([1.0 / np.power(np.float32(th), np.arange(n, dtype=np.float32) / np.float32(n))
                        for th, n in ((DA_THETA, DA_HALF), (RET_THETA, RET_HALF))])
    c["freq"] = np.broadcast_to(f, (P, NF))
    c["iota"] = np.broadcast_to(i, (P, P))
    c["stack"] = (i[:, None] < 2 * E) & (i[:, None] % E == np.arange(E)[None, :])
    c["before"] = i[:, None] < i[None, :]
    return {k: v.astype(np.float32) for k, v in c.items()}


def build(nc, x, xT, positions, w_in, w_proj_da, w_proj_ret, w_out, dense_w1, dense_w3, dense_w2,
          moe_w1, moe_w3, moe_w2, cols_d, rows_d, out):
    ctx = ExitStack()
    with ctx:
        def sb(name, shape, dt=F32):
            return ctx.enter_context(nc.sbuf_tensor(name, shape, dt))

        def sem(name):
            return ctx.enter_context(nc.semaphore(name))

        arena_at = (nc.sbuf_base + 31) // 32 * 32
        mix = sb("mix", [P, MIX_WORDS])
        place = [arena_at]

        def over(name, words, dt=F32):
            t = nc.alloc_sbuf_tensor_at(name, [P, words], dt, offset=place[0])
            place[0] += 4 * words
            return t
        gT_h = over("gT_h", FC * SEQ, F32R)
        gT_l = over("gT_l", FC * SEQ, F32R)
        sgm = over("sgm", 2 * 512)
        gbuf = over("gbuf", 2 * 512)
        assert place[0] <= arena_at + 4 * MIX_WORDS
        place[0] = arena_at + 4 * (2 * FC * P)
        hn_h = over("hn_h", TT * D, F32R)
        hn_l = over("hn_l", TT * D, F32R)
        place[0] = arena_at + 4 * (2 * FC * P + 2 * TT * D)
        moe_gT_h = nc.alloc_sbuf_tensor_at("moe_gT_h", [P, FC * P], F32R, offset=arena_at)
        moe_gT_l = nc.alloc_sbuf_tensor_at("moe_gT_l", [P, FC * P], F32R, offset=arena_at + 4 * FC * P)
        YR_h = nc.alloc_sbuf_tensor_at("YR_h", [P, HEADS, SEQ], F32R, offset=arena_at + 4 * ZQK)
        YR_l = nc.alloc_sbuf_tensor_at("YR_l", [P, HEADS, SEQ], F32R, offset=arena_at + 4 * (ZQK + HEADS * SEQ))
        MT_h = nc.alloc_sbuf_tensor_at("MT_h", [P, KC, SEQ], F32R, offset=arena_at + 4 * QKT)
        MT_l = nc.alloc_sbuf_tensor_at("MT_l", [P, KC, SEQ], F32R, offset=arena_at + 4 * (QKT + KC * SEQ))
        assert QKT + 2 * KC * SEQ <= MIX_WORDS
        moe_sgm = over("moe_sgm", 2 * 256)
        moe_gbuf = over("moe_gbuf", 2 * 256)
        sel_r = over("sel_r", 2 * TT * P, F32R)
        selT = over("selT", 2 * TT * P)
        assert place[0] <= arena_at + 4 * MIX_WORDS

        raw = sb("raw", [P, RAW, UNIT])
        wh = sb("wh", [P, SPLIT, UNIT], F32R)
        wl = sb("wl", [P, SPLIT, UNIT], F32R)
        XT_h = sb("XT_h", [P, KC, SEQ], F32R)
        XT_l = sb("XT_l", [P, KC, SEQ], F32R)
        h = sb("h", [P, TT, D])
        xs = sb("xs", [P, TT * D])
        cols = sb("cols", [P, COLS_W])
        rows = sb("rows", [P, ROWS_W])
        ones = sb("ones", [P, P])

        def col(name):
            return cols[:, COLS[name][0]:COLS[name][0] + COLS[name][1]]

        def row(name):
            return rows[:, ROWS[name][0]:ROWS[name][0] + ROWS[name][1]]
        ident, mask, iota, before, freq, g_sub, stack = (col(n) for n in ("ident", "mask", "iota", "before", "freq", "g_sub",
                                                                          "stack"))
        decay = col("decay").rearrange("p (h q) -> p h q", h=HEADS)
        g_attn = col("g_attn").rearrange("p (l c) -> p l c", l=DEPTH)
        g_ffn = col("g_ffn").rearrange("p (l c) -> p l c", l=DEPTH)
        wr = col("wr").rearrange("p (c e) -> p c e", c=KC)
        g_moe = row("g_moe")
        g_qk = row("g_qk").rearrange("p (l a d) -> p l a d", l=DEPTH, a=2)
        lamv = row("lam").rearrange("p (a l d) -> p a l d", a=4, l=DEPTH)
        pos_i = sb("pos_i", [P, TT], I32)
        pos_f = sb("pos_f", [P, TT])
        cos = sb("cos", [P, TT, NF])
        sin = sb("sin", [P, TT, NF])
        ang = sb("ang", [P, 3, TT, NF])
        g_subs = sb("g_subs", [P, DEPTH])
        lamp = sb("lamp", [P, 2, DEPTH, HD])
        lams = sb("lams", [P, 2, DEPTH])
        lame = sb("lame", [P, 2, DEPTH])
        lamn = sb("lamn", [P, DEPTH])
        wr_hl = sb("wr_hl", [P, KC, 2 * E], F32R)
        lgT = sb("lgT", [2 * E, SEQ])
        nhalf = sb("nhalf", [P, 32])
        ssq = sb("ssq", [P, 32])
        rst = sb("rst", [P, 32])
        rn = sb("rn", [P, TT])
        mxs = sb("mxs", [P, 2, 8])
        nbs = sb("nbs", [P, 2, 8])
        sms = sb("sms", [P, 2, 8])
        rcs = sb("rcs", [P, 2, 8])
        mu = sb("mu", [P, 8])
        rsq = sb("rsq", [P, 2, HEADS])
        yaf = sb("yaf", [P, 8])
        lg = sb("lg", [P, TT, E])
        top = sb("top", [P, TT, 8])
        tidx = sb("tidx", [P, TT, 8], U32)
        tif = sb("tif", [P, TT, 8])
        tdf = sb("tdf", [P, TT])
        te = sb("te", [P, TT])
        tw = sb("tw", [P, 3, TT])
        oh = sb("oh", [P, 2, TT, E])
        comb = sb("comb", [P, TT, E])
        routed = sb("routed", [P, TT, E])
        rank1 = sb("rank1", [P, TT, E])
        rank = sb("rank", [P, TT, E])
        rank2 = sb("rank2", [P, TT, E])
        okey = sb("okey", [P, 3, E])
        nover = sb("nover", [P, 1])
        otab = sb("otab", [P, 16], I32)

        ps = ctx.enter_context(nc.psum_tensor("ps", [P, 8, 512], F32))

        first_in = sem("first_in")
        consts_in = sem("consts_in")
        decay_in = sem("decay_in")
        xT_in = [sem(f"xT_in{n}") for n in range(2)]
        x_in = sem("x_in")
        first_half = [sem(f"first_half{u}") for u in range(2)]
        hi_first = sem("hi_first")
        lo_first = sem("lo_first")
        landed = [sem(f"landed{s}") for s in range(RAW)]
        hi_ready = sem("hi_ready")
        lo_ready = sem("lo_ready")
        unit_used = sem("unit_used")
        dchain = sem("dchain")
        sin_ready = sem("sin_ready")
        ang_ready = sem("ang_ready")
        lam_sum = sem("lam_sum")
        lam_exp = sem("lam_exp")
        pool_const = sem("pool_const")
        ms_ready = sem("ms_ready")
        rs_ready = sem("rs_ready")
        sq_done = sem("sq_done")
        xt_tr = sem("xt_tr")
        xt_hi = sem("xt_hi")
        xt_lo = sem("xt_lo")
        in_evac = sem("in_evac")
        zqk_ready = sem("zqk_ready")
        zr_ready = sem("zr_ready")
        silu_ready = sem("silu_ready")
        zt_tr = sem("zt_tr")
        zt_cp = sem("zt_cp")
        ret_s = sem("ret_s")
        ret_w = sem("ret_w")
        ret_o = sem("ret_o")
        da_s = sem("da_s")
        nb_ready = sem("nb_ready")
        exp_done = sem("exp_done")
        pd_ready = sem("pd_ready")
        pd_tr = sem("pd_tr")
        pd_cp = sem("pd_cp")
        da_o = sem("da_o")
        pchain = sem("pchain")
        mu_ready = sem("mu_ready")
        gn_sq = sem("gn_sq")
        osq = sem("osq")
        down_half = sem("down_half")
        yr_ready = sem("yr_ready")
        ya_ready = sem("ya_ready")
        yt_tr = sem("yt_tr")
        yt_hi = sem("yt_hi")
        yt_lo = sem("yt_lo")
        proj_evac = sem("proj_evac")
        m_ready = sem("m_ready")
        mt_tr = sem("mt_tr")
        mt_hi = sem("mt_hi")
        mt_lo = sem("mt_lo")
        h_half = sem("h_half")
        sig_done = sem("sig_done")
        g_half = sem("g_half")
        g_ready = sem("g_ready")
        g_tr = sem("g_tr")
        g_hi = sem("g_hi")
        g_lo = sem("g_lo")
        wr_hi = sem("wr_hi")
        wr_lo = sem("wr_lo")
        hn_hi = sem("hn_hi")
        hn_lo = sem("hn_lo")
        hg_ready = sem("hg_ready")
        logit = sem("logit")
        lgt_cp = sem("lgt_cp")
        te_in = sem("te_in")
        te_out = sem("te_out")
        routed_ready = sem("routed_ready")
        ranked = sem("ranked")
        counted = sem("counted")
        table_ready = sem("table_ready")
        sel_ready = sem("sel_ready")
        gat = sem("gat")
        gat_cp = sem("gat_cp")
        st_tr = sem("st_tr")
        st_cp = sem("st_cp")
        y_first = sem("y_first")
        y_cp = sem("y_cp")
        sc_done = sem("sc_done")
        h_add = sem("h_add")
        stored = sem("stored")

        w_in_v = [w_in[l].rearrange("(c p) n -> p c n", p=P) for l in range(DEPTH)]
        pr_v = [w_proj_ret[l].rearrange("(c p) n -> p c n", p=P) for l in range(DEPTH)]
        pd_v = [w_proj_da[l].rearrange("(c p) n -> p c n", p=P) for l in range(DEPTH)]
        wo_v = [w_out[l].rearrange("(c p) n -> p c n", p=P) for l in range(DEPTH)]
        dn_v = [w[0].rearrange("(c p) n -> p c n", p=P) for w in (dense_w1, dense_w3, dense_w2)]
        me_v = [w[0].rearrange("e (c p) n -> e p c n", p=P) for w in (moe_w1, moe_w3, moe_w2)]

        def mixer_unit(l, u):
            if u < 2 * IN_GROUPS:
                g, half = divmod(u, 2)
                b = IN_ORDER[g]
                return [w_in_v[l][:, half * 4 + 2 * a:half * 4 + 2 * a + 2, b * 512:(b + 1) * 512] for a in (0, 1)]
            u -= 2 * IN_GROUPS
            if u < 4:
                v = (pr_v, pd_v)[u % 2][l]
                n = u // 2
                return [v[:, 2 * a:2 * a + 2, n * 512:(n + 1) * 512] for a in (0, 1)]
            n, half = divmod(u - 4, 2)
            return [wo_v[l][:, half * 4 + 2 * a:half * 4 + 2 * a + 2, n * 512:(n + 1) * 512] for a in (0, 1)]

        def ffn_unit(w1, w3, w2, slot, u):
            if u < 2 * SLICES:
                j, half = divmod(u, 2)
                to = raw[:, slot, :].rearrange("p (c w n) -> p c w n", c=4, w=2)
                return [(to[:, :, a, :], w[:, half * 4:half * 4 + 4, j * 256:(j + 1) * 256])
                        for a, w in ((0, w1), (1, w3))]
            c = 2 * (u - 2 * SLICES)
            return [(raw[:, slot, a * D:(a + 1) * D], w2[:, c + a, :]) for a in (0, 1)]

        class Units:
            def __init__(self, base, i=None, per=0, raw_slots=RAW):
                self.base, self.i, self.per, self.raw_slots = base, i, per, raw_slots
                assert i is None or (per % raw_slots == 0 and per % SPLIT == 0)

            def at(self, const, per):
                return const if self.i is None else const + self.i * per

            def count(self, j):
                return self.at(self.base + j + 1, self.per)

            def before(self, j, n):
                c = self.base + j + 1 - n
                return None if self.i is None and c < 1 else self.at(c, self.per)

            def split_slot(self, j):
                return (self.base + j) % SPLIT

            def raw_slot(self, j):
                return (self.base + j) % self.raw_slots

            def landed(self, j):
                n, s = self.base + j, self.raw_slot(j)
                if self.raw_slots == RAW:
                    c = n // RAW + 1
                else:
                    c = len([m for m in range(OVER_BASE) if m % RAW == s])
                    c += len([m for m in range(OVER_BASE, n + 1) if m % SPLIT == s])
                return self.at(32 * c, 32 * (self.per // self.raw_slots))

        def load_unit(eng, U, j, pairs):
            v = U.before(j, U.raw_slots)
            if v is not None:
                eng.wait_ge(lo_ready, v)
            for to, of in pairs:
                eng.dma_start(to, of).then_inc(landed[U.raw_slot(j)], 16)

        def split_hi(act, U, j):
            act.wait_ge(landed[U.raw_slot(j)], U.landed(j))
            v = U.before(j, SPLIT)
            if v is not None:
                act.wait_ge(unit_used, v)
            nc.scalar.activation(wh[:, U.split_slot(j), :], raw[:, U.raw_slot(j), :], ACT.Copy).then_inc(hi_ready, 1)

        def split_lo(dve, U, j):
            dve.wait_ge(hi_ready, U.count(j))
            v = U.before(j, SPLIT)
            if v is not None:
                dve.wait_ge(unit_used, v)
            s = U.split_slot(j)
            nc.vector.tensor_tensor(wl[:, s, :], raw[:, U.raw_slot(j), :], wh[:, s, :].bitcast(F32),
                                    ALU.subtract).then_inc(lo_ready, 1)

        def product(o, xh, xl, bh, bl, start, stop):
            nc.tensor.matmul(o, xh, bh, start=start, stop=False)
            nc.tensor.matmul(o, xh, bl, start=False, stop=False)
            return nc.tensor.matmul(o, xl, bh, start=False, stop=stop)

        def gemm_unit(pe, U, j, outs, xT, chunks, start, stop, between=None):
            first = U.i is None and U.base + j < 2
            pe.wait_ge(*((lo_first, j + 1) if first else (lo_ready, U.count(j))))
            s = U.split_slot(j)
            for a, c in enumerate(chunks):
                if a == 2 and first:
                    pe.wait_ge(lo_ready, j + 1)
                if a == 2 and between is not None:
                    between()
                for o, cols in outs:
                    last = product(o, xT[0][:, c, cols], xT[1][:, c, cols],
                                   wh[:, s, a * 512:(a + 1) * 512], wl[:, s, a * 512:(a + 1) * 512],
                                   start and a == 0, stop and a == len(chunks) - 1)
            last.then_inc(unit_used, 1)

        tok = [slice(t * P, (t + 1) * P) for t in range(TT)]
        gT3 = [g[:, :].rearrange("p (c n) -> p c n", c=FC) for g in (gT_h, gT_l)]
        moe_gT3 = [g[:, :].rearrange("p (c n) -> p c n", c=FC) for g in (moe_gT_h, moe_gT_l)]
        xs3 = xs[:, :].rearrange("p (t n) -> p t n", t=TT)

        def mx(off, words):
            return mix[:, off:off + words]

        def hT(n, c):
            return mx(ZQK + c * SEQ, SEQ) if n == 0 else ps[:, 4 + c // 2, (c % 2) * SEQ:(c % 2 + 1) * SEQ]

        block = ctx.enter_context(nc.Block())

        @block.sync
        def _(sp):
            def load_xT(half):
                sp.dma_start(mx(ZQK + half * D, D).rearrange("p (c n) -> p c n", c=4),
                             xT[:, 4 * half:4 * half + 4, :]).then_inc(xT_in[half], 16)

            load_xT(0)
            for l in range(DEPTH):
                U = Units(MIX_BASE[l])
                for u in range(MIX_UNITS):
                    to = raw[:, U.raw_slot(u), :].rearrange("p (a c n) -> p a c n", a=2, c=2)
                    if l == 0 and u < 2:
                        s0, s1 = mixer_unit(0, u)
                        sp.dma_start(to[:, 0], s0).then_inc(first_half[u], 16)
                        for c in range(2):
                            sp.dma_start(to[:, 1, c:c + 1], s1[:, c:c + 1]).then_inc(landed[u], 16)
                        if u == 0:
                            load_xT(1)
                        continue
                    load_unit(sp, U, u, [(to[:, a], s) for a, s in enumerate(mixer_unit(l, u))])
                    if l == 0 and u == 2:
                        sp.dma_start(h[:, :, :], x[0].rearrange("(t p) d -> p t d", p=P)).then_inc(x_in, 16)
                    if l == 0 and u == 3:
                        sp.dma_start(pos_i[:, :], positions).then_inc(consts_in, 16)
                        sp.dma_start(cols[:, COLS_FIRST:COLS_LAST], cols_d[:, COLS_FIRST:COLS_LAST])\
                            .then_inc(consts_in, 16)
                        sp.dma_start(rows[:, :], rows_d.to_broadcast([P, ROWS_W])).then_inc(consts_in, 16)
                    if l == 0 and u == 5:
                        sp.dma_start(cols[:, COLS_LAST:], cols_d[:, COLS_LAST:]).then_inc(decay_in, 16)
                if l == 0:
                    U = Units(DENSE_BASE)
                    for u in range(FFN_UNITS):
                        load_unit(sp, U, u, ffn_unit(*dn_v, U.raw_slot(u), u))
            with sp.Fori(0, E // 2) as i:
                U = Units(MOE_BASE, i, 2 * FFN_UNITS)
                for half in range(2):
                    w = [v[2 * i + half] for v in me_v]
                    for u in range(FFN_UNITS):
                        j = half * FFN_UNITS + u
                        load_unit(sp, U, j, ffn_unit(*w, U.raw_slot(j), u))
            sp.wait_ge(table_ready, 1)
            n_over = sp.value_load(otab[0:1, 0:1], min_val=0, max_val=3)
            with sp.If(n_over > 0):
                with sp.Fori(0, n_over) as k:
                    e = sp.value_load(otab[0:1, bass.ds(k + 8, 1)], min_val=0, max_val=E - 1)
                    U = Units(OVER_BASE, k, FFN_UNITS, SPLIT)
                    w = [v[e] for v in me_v]
                    for u in range(FFN_UNITS):
                        load_unit(sp, U, u, ffn_unit(*w, U.raw_slot(u), u))
            out_v = out[0].rearrange("(t p) d -> p t d", p=P)
            for n in range(2):
                sp.wait_ge(h_add, n_over * 4 + 4 * E - 2 + 2 * n)
                sp.dma_start(out_v[:, :, n * 512:(n + 1) * 512], h[:, :, n * 512:(n + 1) * 512]).then_inc(stored, 16)
            sp.wait_ge(stored, 32)

        @block.gpsimd
        def _(pool):
            nc.gpsimd.memset(nhalf[:, :], -0.5).then_inc(pool_const, 1)
            nc.gpsimd.memset(ones[:, :], 1.0).then_inc(pool_const, 1)
            pool.wait_ge(pool_const, 2)
            n_roots, chain = [0], [0]

            def root(to, of):
                n_roots[0] += 1
                pool.wait_ge(ms_ready, n_roots[0])
                nc.gpsimd.tensor_tensor(to, of, nhalf[:, 0:of.shape[-1]], ALU.pow).then_inc(rs_ready, 1)

            for l in range(DEPTH):
                root(rn[:, :], ssq[:, 0:TT])
                root(rst[:, :], ssq[:, :])
                pool.wait_ge(sin_ready, 1)
                pool.wait_ge(in_evac, IN_GROUPS * l + 3)
                zr4 = mx(ZR, 1024).rearrange("p (t g d) -> p t g d", t=TT, d=HD)
                x1, x2 = zr4[:, :, :, 0:RET_HALF], zr4[:, :, :, RET_HALF:HD]
                cs, sn = (v[:, :, DA_HALF:NF].unsqueeze(2).to_broadcast([P, TT, 8, RET_HALF]) for v in (cos, sin))
                tmp = [mx(SGB + a * 512, 512).rearrange("p (t g d) -> p t g d", t=TT, d=RET_HALF) for a in range(4)]
                tt = nc.gpsimd.tensor_tensor
                tt(tmp[0], x1, cs, ALU.mult)
                tt(tmp[1], x2, sn, ALU.mult)
                tt(tmp[2], x1, sn, ALU.mult)
                tt(tmp[3], x2, cs, ALU.mult).then_inc(pchain, 1)
                pool.wait_ge(pchain, l + 1)
                tt(x1, tmp[0], tmp[1], ALU.subtract)
                tt(x2, tmp[2], tmp[3], ALU.add).then_inc(zr_ready, 1)
                pool.wait_ge(in_evac, IN_GROUPS * l + 5)
                tt(mx(ZG, 1024), mx(ZG, 1024), mx(SGA, 1024), ALU.mult).then_inc(silu_ready, 1)
                root(rst[:, 0:8], ssq[:, 0:8])
                root(rst[:, 12:16], ssq[:, 12:16])
                root(rst[:, 8:12], ssq[:, 8:12])
                root(rn[:, :], ssq[:, 0:TT])

        @block.scalar
        def _(act):
            act.dma_start(cols[:, 0:COLS_FIRST], cols_d[:, 0:COLS_FIRST]).then_inc(first_in, 16)
            act.wait_ge(pool_const, 1)
            nc.scalar.activation(mu[:, 0:1], nhalf[:, 0:1], ACT.Copy)
            act.wait_ge(first_in, 16)

            split_to = [0]

            def split_until(U, j):
                while split_to[0] <= U.base + j:
                    split_hi(act, Units(0), split_to[0])
                    split_to[0] += 1

            def norm_hi(n, half, gain):
                for r in (2 * half, 2 * half + 1):
                    if n == 0:
                        act.wait_ge(xT_in[half], 16)
                    else:
                        act.wait_ge(xt_tr, 4 * (n - 1) + r + 1)
                    for a in range(2):
                        c = 2 * r + a
                        ins = nc.scalar.activation(XT_h[:, c, :], hT(n, c), ACT.Copy, scale=gain[:, c:c + 1])
                    ins.then_inc(xt_hi, 1)

            def squares(n, to=xs3):
                if n == 0:
                    act.wait_ge(x_in, 16)
                else:
                    act.wait_ge(h_half, 2 * n)
                for t in range(TT):
                    nc.scalar.activation(to[:, t, :], h[:, t, :], ACT.Square, accum_out=ssq[:, t:t + 1])\
                        .then_inc(sq_done, 1)

            def small_tables():
                act.wait_ge(ang_ready, 1)
                nc.scalar.activation(sin[:, :, :], ang[:, 0], ACT.Sin)
                nc.scalar.activation(cos[:, :, :], ang[:, 1], ACT.Sin).then_inc(sin_ready, 1)

            def lambda_exps():
                act.wait_ge(lam_sum, 1)
                nc.scalar.activation(lame[:, :, :], lams[:, :, :], ACT.Exp).then_inc(lam_exp, 1)
                nc.scalar.activation(wr_hl[:, :, 0:E], wr, ACT.Copy).then_inc(wr_hi, 1)

            def mixers(l):
                U = Units(MIX_BASE[l])
                gain = g_attn[:, l, :]
                if l == 0:
                    norm_hi(0, 0, gain)
                    for u in range(2):
                        act.wait_ge(first_half[u], 16)
                        nc.scalar.activation(wh[:, u, 0:UNIT // 2], raw[:, u, 0:UNIT // 2], ACT.Copy)\
                            .then_inc(hi_first, 1)
                        act.wait_ge(landed[u], 32)
                        nc.scalar.activation(wh[:, u, UNIT // 2:], raw[:, u, UNIT // 2:], ACT.Copy)\
                            .then_inc(hi_ready, 1)
                        if u == 0:
                            norm_hi(0, 1, gain)
                    split_to[0] = 2
                qkT = mx(QKT, 2048).rearrange("p (r n) -> p r n", r=4)
                retT = mx(RETT, 1024).rearrange("p (r n) -> p r n", r=2)
                e0 = mx(ZR, 1024).rearrange("p (c h n) -> p c h n", c=2, h=HEADS)
                e1 = mx(ZQK, 2048).rearrange("p (c h n) -> p c h n", c=2, h=HEADS)

                def evac(g):
                    act.wait_ge(unit_used, U.count(2 * g + 1))
                    if g == 0:
                        act.wait_ge(rs_ready, ROOTS * l + 1)
                    for t in range(TT):
                        acc = ps[:, 2 * (g % 2) + t, :]
                        if g < 2:
                            to = mx(ZQK + t * 1024 + g * 512, 512)
                        elif g < 6:
                            to = mx((ZR, ZRV, ZG, ZV)[g - 2] + t * 512, 512)
                        else:
                            to = mx((SGA, SGB)[(g - 6) // 2] + t * 1024 + (g % 2) * 512, 512)
                        if g < 2:
                            at = t * 1024 + g * 512
                            nc.scalar.activation(xs[:, at:at + 512], acc, ACT.Square, scale=rn[:, t:t + 1])
                        if g == 4:
                            nc.scalar.activation(mx(SGA + t * 512, 512), acc, ACT.Sigmoid, scale=rn[:, t:t + 1])
                        ins = nc.scalar.activation(to, acc, ACT.Copy if g < 6 else ACT.Sigmoid, scale=rn[:, t:t + 1])
                    ins.then_inc(in_evac, 1)

                def zt_copy(r):
                    act.wait_ge(zt_tr, 6 * l + r + 1)
                    nc.scalar.activation(qkT[:, r] if r < 4 else retT[:, r - 4], ps[:, 4 + r % 4, :], ACT.Copy)\
                        .then_inc(zt_cp, 1)

                def exps(k):
                    act.wait_ge(nb_ready, 3 * l + k + 1)
                    for c in range(2):
                        for hd in ((0, 1), (2, 3), (0, 1, 2, 3))[k]:
                            t, n = (1, SEQ) if k < 2 else (0, P)
                            bank = (6, 6, 4)[k] + c
                            a = hd % 2 if k < 2 else hd
                            ins = nc.scalar.activation((e0 if t == 0 else e1)[:, c, hd],
                                                       ps[:, bank, a * n:(a + 1) * n], ACT.Exp,
                                                       bias=nbs[:, t, 4 * c + hd:4 * c + hd + 1], scale=DA_SCALE,
                                                       accum_out=sms[:, t, 4 * c + hd:4 * c + hd + 1])
                    ins.then_inc(exp_done, 1)

                pdT = mx(QKT, 1536).rearrange("p (r n) -> p r n", r=3)

                def pd_copy(r):
                    act.wait_ge(pd_tr, 3 * l + r + 1)
                    nc.scalar.activation(pdT[:, r], ps[:, (4, 5, 5)[r], :], ACT.Copy).then_inc(pd_cp, 1)

                def group_squares():
                    act.wait_ge(mu_ready, l + 1)
                    for g in range(8):
                        ins = nc.scalar.activation(mx(RIN + g * VD, VD), ps[:, 6 + g // 4, (g % 4) * VD:(g % 4 + 1) * VD],
                                                   ACT.Square, bias=mu[:, g:g + 1], accum_out=ssq[:, g:g + 1])
                    ins.then_inc(gn_sq, 1)

                def out_squares(t):
                    act.wait_ge(da_o, 2 * l + 2 - t)
                    nc.scalar.activation(mx(RETT + t * 512, 512), ps[:, 5 - t, :], ACT.Square).then_inc(osq, 1)

                def yt(r):
                    act.wait_ge(yt_tr, 4 * l + r + 1)
                    c = 2 * (r % 2)
                    nc.scalar.activation((YR_h if r < 2 else XT_h)[:, c:c + 2, :],
                                         ps[:, (6, 7, 4, 5)[r], :].rearrange("p (a n) -> p a n", a=2),
                                         ACT.Copy, scale=1.0 if r < 2 else g_subs[:, l:l + 1]).then_inc(yt_hi, 1)

                for n in range(2 * IN_GROUPS):
                    if n == 0 and l > 0:
                        norm_hi(2 * l, 1, gain)
                    if n == 1 - l:
                        squares(2 * l)
                    if n == 4 and l == 0:
                        small_tables()
                    if n == 10 and l == 0:
                        lambda_exps()
                    if n == 10:
                        for r in range(4):
                            zt_copy(r)
                    if n in (13, 15, 16):
                        exps((13, 15, 16).index(n))
                    if n == 14:
                        act.wait_ge(silu_ready, l + 1)
                    if n == 17:
                        group_squares()
                        pd_copy(0)
                        pd_copy(1)
                    if n % 2 == 0 and n > 0:
                        evac(n // 2 - 1)
                    if n == 11:
                        zt_copy(4)
                        zt_copy(5)
                    if n == 18:
                        pd_copy(2)
                        out_squares(1)
                    if n == 19:
                        yt(0)
                        yt(1)
                        out_squares(0)
                    split_until(U, n + AHEAD)

                evac(IN_GROUPS - 1)
                split_until(U, 22)
                yt(2)
                yt(3)
                split_until(U, 24)

                def mt(half):
                    for r in (2 * half, 2 * half + 1):
                        act.wait_ge(mt_tr, 4 * l + r + 1)
                        nc.scalar.activation(MT_h[:, 2 * r:2 * r + 2, :],
                                             ps[:, 4 + r, :].rearrange("p (a n) -> p a n", a=2), ACT.Copy)\
                            .then_inc(mt_hi, 1)
                mt(0)
                split_until(U, 26)
                mt(1)
                split_until(U, 28)
                norm_hi(2 * l + 1, 0, g_ffn[:, l, :])
                split_until(U, 29)

            def sigmoid_slice(products, bank, buf):
                act.wait_ge(unit_used, products)
                nc.scalar.activation(buf, bank, ACT.Sigmoid).then_inc(sig_done, 1)

            def dense():
                def sigm(j):
                    act.wait_ge(unit_used, Units(DENSE_BASE).count(2 * j + 1))
                    if j == 0:
                        act.wait_ge(rs_ready, ROOTS)
                    for t in range(TT):
                        ins = nc.scalar.activation(sgm[:, (2 * (j % 2) + t) * 256:(2 * (j % 2) + t + 1) * 256],
                                                   ps[:, 2 * (j % 2) + t, 0:256], ACT.Sigmoid, scale=rn[:, t:t + 1])
                    ins.then_inc(sig_done, 1)

                def hi(j):
                    act.wait_ge(g_tr, j + 1)
                    nc.scalar.activation(gT3[0][:, 2 * j:2 * j + 2, :],
                                         ps[:, 4 + j % 2, :].rearrange("p (a n) -> p a n", a=2), ACT.Copy)\
                        .then_inc(g_hi, 1)
                for j in range(SLICES):
                    if j == 0:
                        norm_hi(1, 1, g_ffn[:, 0, :])
                        squares(1)
                    if j >= 1:
                        sigm(j - 1)
                    if j >= 2:
                        hi(j - 2)
                    split_until(Units(DENSE_BASE), 2 * j + 1 + AHEAD)
                for u in range(SLICES):
                    if u == 0:
                        sigm(SLICES - 1)
                        hi(SLICES - 2)
                    if u == 1:
                        hi(SLICES - 1)
                    if u == SLICES - 1:
                        norm_hi(2, 0, g_attn[:, 1, :])
                    split_until(Units(DENSE_BASE), 2 * SLICES + u + AHEAD)

            mixers(0)
            dense()
            mixers(1)
            norm_hi(3, 1, g_ffn[:, 1, :])
            squares(3, mx(ZQK, 2048).rearrange("p (t n) -> p t n", t=TT))
            act.wait_ge(logit, 1)
            nc.scalar.activation(lgT[:, :], ps[0:2 * E, 0, 0:SEQ], ACT.Copy).then_inc(lgt_cp, 1)
            act.wait_ge(hg_ready, 1)
            act.wait_ge(rs_ready, 2 * ROOTS)
            for t in range(TT):
                ins = nc.scalar.activation(hn_h[:, t * D:(t + 1) * D], xs3[:, t, :], ACT.Copy, scale=rn[:, t:t + 1])
            ins.then_inc(hn_hi, 1)
            act.wait_ge(te_in, 1)
            nc.scalar.activation(te[:, :], tdf[:, :], ACT.Exp).then_inc(te_out, 1)

            def gather_copy(base, part):
                for r in range(4 * part, 4 * part + 4):
                    act.wait_ge(gat, base + r + 1)
                    nc.scalar.activation((XT_h, XT_l)[r // 4][:, 2 * (r % 4):2 * (r % 4) + 2, :],
                                         ps[:, 6 + r % 2, :].rearrange("p (c n) -> p c n", c=2), ACT.Copy)\
                        .then_inc(gat_cp, 1)

            def sigm(U, j0, j):
                sigmoid_slice(U.count(j0 + 2 * j + 1), ps[:, j % 2, 0:256], moe_sgm[:, (j % 2) * 256:(j % 2 + 1) * 256])

            def hi(q, j):
                act.wait_ge(g_tr, q * SLICES + j + 1)
                nc.scalar.activation(moe_gT3[0][:, 2 * j:2 * j + 2, :],
                                     ps[:, 4 + j % 2, 0:256].rearrange("p (a n) -> p a n", a=2), ACT.Copy)\
                    .then_inc(g_hi, 1)

            def expert(p, b, U, j0, last_split, gather_next, first=None):
                if first is not None:
                    gather_copy(first, 0)
                    gather_copy(first, 1)
                    for j in range(AHEAD):
                        split_hi(act, U, j0 + j)
                for j in range(SLICES):
                    if j >= 1:
                        sigm(U, j0, j - 1)
                    if j >= 2:
                        hi(p + 1, j - 2)
                    if j == 7:
                        act.wait_ge(st_tr, p + 1)
                        nc.scalar.activation(selT[:, b * SEQ:(b + 1) * SEQ], ps[:, 6, 0:SEQ], ACT.Copy)\
                            .then_inc(st_cp, 1)
                    for a in range(2):
                        split_hi(act, U, j0 + 2 * j + AHEAD + a)
                for u in range(SLICES):
                    if u == 0:
                        sigm(U, j0, SLICES - 1)
                        hi(p + 1, SLICES - 2)
                    if u < 2 and gather_next is not None:
                        gather_copy(gather_next, u)
                    if u == 1:
                        hi(p + 1, SLICES - 1)
                    if 2 * SLICES + u + AHEAD <= last_split:
                        split_hi(act, U, j0 + 2 * SLICES + u + AHEAD)
                act.wait_ge(y_first, p + 1)
                nc.scalar.activation(xs3[:, b, 0:512], ps[:, 2, :], ACT.Copy).then_inc(y_cp, 1)
                act.wait_ge(unit_used, U.count(j0 + FFN_UNITS - 1))
                nc.scalar.activation(xs3[:, b, 512:D], ps[:, 3, :], ACT.Copy).then_inc(y_cp, 1)

            gather_copy(0, 0)
            gather_copy(0, 1)
            expert(0, 0, Units(MOE_BASE), 0, FFN_UNITS + 1, None)
            with act.Fori(0, E // 2 - 1) as i:
                U = Units(MOE_BASE + FFN_UNITS, i, 2 * FFN_UNITS)
                expert(2 * i + 1, 1, U, 0, FFN_UNITS + 1, 8 * i + 8)
                expert(2 * i + 2, 0, U, FFN_UNITS, FFN_UNITS + 1, None)
            expert(E - 1, 1, Units(MOE_BASE), (E - 1) * FFN_UNITS, FFN_UNITS - 1, None)
            act.wait_ge(table_ready, 1)
            n_over = act.value_load(otab[0:1, 0:1], min_val=0, max_val=3)
            with act.If(n_over > 0):
                with act.Fori(0, n_over) as k:
                    expert(k + E, 0, Units(OVER_BASE, k, FFN_UNITS, SPLIT), 0, FFN_UNITS - 1, None, 8 * k + 4 * E)

        @block.tensor
        def _(pe):

            def transpose(o, i):
                return nc.tensor.transpose(o, i, ident)

            def norm_T(n, half):
                pe.wait_ge(h_half, 2 * (n - 1) + half + 1)
                for r in (2 * half, 2 * half + 1):
                    for a in range(2):
                        for t in range(TT):
                            c = 2 * r + a
                            last = transpose(ps[:, 4 + r, a * SEQ + t * P:a * SEQ + (t + 1) * P],
                                             h[:, t, c * P:(c + 1) * P])
                    last.then_inc(xt_tr, 1)

            def mixers(l):
                U = Units(MIX_BASE[l])
                zqk = mx(ZQK, 2048).rearrange("p (t n) -> p t n", t=TT)
                zr = mx(ZR, 1024).rearrange("p (t n) -> p t n", t=TT)
                qkT = mx(QKT, 2048).rearrange("p (b n) -> p b n", b=8)
                retT = mx(RETT, 1024).rearrange("p (b n) -> p b n", b=4)
                rin = mx(RIN, HEADS * 384).rearrange("p (h n) -> p h n", h=HEADS)
                rv = mx(ZRV, 1024).rearrange("p (t n) -> p t n", t=TT)
                va = mx(ZV, 1024).rearrange("p (t n) -> p t n", t=TT)
                pd0 = mx(ZR, 512).rearrange("p (h n) -> p h n", h=4)
                pd1 = mx(ZQK, 1024).rearrange("p (h n) -> p h n", h=4)
                pdT = mx(QKT, 1536).rearrange("p (b n) -> p b n", b=12)

                def zt(r):
                    for a in range(2):
                        for t in range(TT):
                            src = zqk[:, t, (2 * r + a) * P:(2 * r + a + 1) * P] if r < 4 else \
                                zr[:, t, (2 * (r - 4) + a) * P:(2 * (r - 4) + a + 1) * P]
                            last = transpose(ps[:, 4 + r % 4, (a * 2 + t) * P:(a * 2 + t + 1) * P], src)
                    last.then_inc(zt_tr, 1)

                def ret_scores(hd):
                    part = slice((hd % 2) * HD, (hd % 2 + 1) * HD)
                    q, k = retT[part, hd // 2], retT[part, 2 + hd // 2]
                    bank = 4 + hd % 2
                    nc.tensor.matmul(ps[:, bank, 0:SEQ], k[:, 0:P], q, start=True, stop=True)
                    nc.tensor.matmul(ps[:, bank, SEQ:SEQ + P], k[:, P:SEQ], q[:, P:SEQ], start=True, stop=True)\
                        .then_inc(ret_s, 1)

                def da_scores(k):
                    t = 1 if k < 2 else 0
                    n = P * (t + 1)
                    for hd in ((0, 1), (2, 3), (0, 1, 2, 3))[k]:
                        a = hd % 2 if k < 2 else hd
                        for c in range(2):
                            part = slice(c * HD, (c + 1) * HD)
                            last = nc.tensor.matmul(ps[:, (6, 6, 4)[k] + c, a * n:(a + 1) * n],
                                                    qkT[part, hd, tok[t]], qkT[part, 4 + hd, 0:n],
                                                    start=True, stop=True)
                    last.then_inc(da_s, 1)

                def ret_out():
                    for hd in range(HEADS):
                        cs = slice(hd * VD, (hd + 1) * VD)
                        nc.tensor.matmul(ps[:, 6, cs], rin[:, hd, 0:P], rv[:, 0, cs], start=True, stop=True)
                        nc.tensor.matmul(ps[:, 7, cs], rin[:, hd, P:SEQ], rv[:, 0, cs], start=True, stop=False)
                        last = nc.tensor.matmul(ps[:, 7, cs], rin[:, hd, SEQ:SEQ + P], rv[:, 1, cs],
                                                start=False, stop=True)
                    last.then_inc(ret_o, 1)

                def da_out(t):
                    for hd in range(HEADS):
                        cs = slice(hd * VD, (hd + 1) * VD)
                        if t == 1:
                            nc.tensor.matmul(ps[:, 4, cs], pdT[:, 2 * hd], va[:, 0, cs], start=True, stop=False)
                            last = nc.tensor.matmul(ps[:, 4, cs], pdT[:, 1 + 2 * hd], va[:, 1, cs],
                                                    start=False, stop=True)
                        else:
                            last = nc.tensor.matmul(ps[:, 5, cs], pdT[:, 8 + hd], va[:, 0, cs], start=True, stop=True)
                    last.then_inc(da_o, 1)

                yv = xs[:, :].rearrange("p (m t n) -> p m t n", m=2, t=TT)

                def yt(m):
                    pe.wait_ge(yr_ready if m else ya_ready, l + 1)
                    for r in range(2):
                        for a in range(2):
                            for t in range(TT):
                                c = 2 * r + a
                                last = transpose(ps[:, (4, 6)[m] + r, (a * 2 + t) * P:(a * 2 + t + 1) * P],
                                                 yv[:, m, t, c * P:(c + 1) * P])
                        last.then_inc(yt_tr, 1)

                for n in range(2 * IN_GROUPS):
                    g, half = divmod(n, 2)
                    if n < 2:
                        pe.wait_ge(xt_lo, 8 * l + 2 * n + 2)
                    if half == 0 and g >= 2:
                        pe.wait_ge(in_evac, IN_GROUPS * l + g - 1)
                    outs = [(ps[:, 2 * (g % 2) + t, :], tok[t]) for t in range(TT)]
                    late = (lambda: norm_T(2 * l, 1)) if n == 0 and l > 0 else (lambda: yt(1)) if n == 18 else None
                    gemm_unit(pe, U, n, outs, (XT_h, XT_l), range(4 * half, 4 * half + 4), half == 0, half == 1,
                              late)
                    if n == 9:
                        pe.wait_ge(consts_in, 48)
                        pe.wait_ge(zqk_ready, l + 1)
                        for r in range(4):
                            zt(r)
                    if n == 10:
                        pe.wait_ge(zr_ready, l + 1)
                        pe.wait_ge(zt_cp, 6 * l + 2)
                        zt(4)
                        zt(5)
                    if n == 11:
                        pe.wait_ge(zt_cp, 6 * l + 4)
                        da_scores(0)
                        pe.wait_ge(zt_cp, 6 * l + 6)
                        ret_scores(0)
                        ret_scores(1)
                    if n == 12:
                        pe.wait_ge(ret_w, 4 * l + 2)
                        ret_scores(2)
                        ret_scores(3)
                    if n == 13:
                        pe.wait_ge(exp_done, 3 * l + 1)
                        da_scores(1)
                    if n == 14:
                        pe.wait_ge(ret_w, 4 * l + 4)
                        da_scores(2)
                    if n == 15:
                        pe.wait_ge(exp_done, 3 * l + 2)
                        ret_out()
                    if n == 16:
                        pe.wait_ge(exp_done, 3 * l + 3)
                        pe.wait_ge(pd_ready, 2 * l + 1)
                        for r in range(2):
                            for a in range(4):
                                last = transpose(ps[:, 4 + r, a * P:(a + 1) * P], pd1[:, 2 * r + a // 2, tok[a % 2]])
                            last.then_inc(pd_tr, 1)
                    if n == 17:
                        pe.wait_ge(pd_cp, 3 * l + 2)
                        da_out(1)
                        pe.wait_ge(pd_ready, 2 * l + 2)
                        for hd in range(HEADS):
                            last = transpose(ps[:, 5, hd * P:(hd + 1) * P], pd0[:, hd])
                        last.then_inc(pd_tr, 1)
                    if n == 18:
                        pe.wait_ge(pd_cp, 3 * l + 3)
                        da_out(0)
                mg = mx(SGA, 2048).rearrange("p (t n) -> p t n", t=TT)

                def mt(half):
                    pe.wait_ge(m_ready, 2 * l + half + 1)
                    for r in (2 * half, 2 * half + 1):
                        for a in range(2):
                            for t in range(TT):
                                c = 2 * r + a
                                last = transpose(ps[:, 4 + r, (a * 2 + t) * P:(a * 2 + t + 1) * P],
                                                 mg[:, t, c * P:(c + 1) * P])
                        last.then_inc(mt_tr, 1)

                for u in range(4):
                    if u == 0:
                        pe.wait_ge(yt_lo, 4 * l + 2)
                        pe.wait_ge(in_evac, IN_GROUPS * l + 9)
                    if u == 1:
                        pe.wait_ge(yt_lo, 4 * l + 4)
                        pe.wait_ge(in_evac, IN_GROUPS * l + 10)
                    b = PROJ_BANK[u]
                    between = (lambda: yt(0)) if u == 0 else None
                    gemm_unit(pe, U, 2 * IN_GROUPS + u, [(ps[:, b + t, :], tok[t]) for t in range(TT)],
                              (XT_h, XT_l) if u % 2 else (YR_h, YR_l), range(4), True, True, between)
                    if u == 2:
                        mt(0)
                for u in range(4):
                    n, half = divmod(u, 2)
                    if u < 2:
                        pe.wait_ge(mt_lo, 4 * l + 2 * u + 2)
                    outs = [(ps[:, 2 * n + t, :], tok[t]) for t in range(TT)]
                    between = {0: lambda: mt(1), 2: lambda: norm_T(2 * l + 1, 0)}.get(u)
                    gemm_unit(pe, U, 2 * IN_GROUPS + 4 + u, outs, (MT_h, MT_l), range(4 * half, 4 * half + 4),
                              half == 0, half == 1, between)

            def dense():
                U = Units(DENSE_BASE)

                def g_transposes(j):
                    pe.wait_ge(g_ready, j + 1)
                    if j >= 2:
                        pe.wait_ge(g_lo, j - 1)
                    gv = gbuf[:, (j % 2) * 512:(j % 2 + 1) * 512].rearrange("p (t n) -> p t n", t=TT)
                    for a in range(2):
                        for t in range(TT):
                            last = transpose(ps[:, 4 + j % 2, (a * 2 + t) * P:(a * 2 + t + 1) * P],
                                             gv[:, t, a * P:(a + 1) * P])
                    last.then_inc(g_tr, 1)
                for j in range(SLICES):
                    if j >= 2:
                        pe.wait_ge(g_ready, j - 1)
                    outs = [(ps[:, 2 * (j % 2) + t, :], tok[t]) for t in range(TT)]
                    for half in range(2):
                        if j == 0:
                            pe.wait_ge(xt_lo, 4 + 2 * half + 2)
                            pe.wait_ge(h_half, 1)
                        late = (lambda: norm_T(1, 1)) if j == 0 and half == 0 else None
                        gemm_unit(pe, U, 2 * j + half, outs, (XT_h, XT_l), range(4 * half, 4 * half + 4),
                                  half == 0, half == 1, late)
                    if j >= 1:
                        g_transposes(j - 1)
                down_outs = [((2, 3), tok[0]), ((6, 7), tok[1])]
                for u in range(SLICES - 2):
                    pe.wait_ge(g_lo, u + 1)
                    down_unit(pe, U, 2 * SLICES + u, down_outs, gT3, u)
                    if u == 0:
                        g_transposes(SLICES - 1)
                pe.wait_ge(g_lo, SLICES)
                pe.wait_ge(lo_ready, U.count(FFN_UNITS - 1))
                for n in range(2):
                    for u in (SLICES - 2, SLICES - 1):
                        s = U.split_slot(2 * SLICES + u)
                        for a in range(2):
                            b = slice(a * D + n * 512, a * D + (n + 1) * 512)
                            for banks, cols in down_outs:
                                last = product(ps[:, banks[n], :], gT3[0][:, 2 * u + a, cols], gT3[1][:, 2 * u + a, cols],
                                               wh[:, s, b], wl[:, s, b], False, u == SLICES - 1 and a == 1)
                            if n == 1 and u == SLICES - 2 and a == 0:
                                norm_T(2, 0)
                        if n == 1:
                            last.then_inc(unit_used, 1)
                    if n == 0:
                        last.then_inc(down_half, 1)

            def down_unit(pe, U, j, outs, gT, u, halves=None):
                pe.wait_ge(lo_ready, U.count(j))
                s = U.split_slot(j)
                steps = [(a, n) for a in range(2) for n in range(2)]
                if halves is not None:
                    steps.sort(key=lambda step: step[1])
                for a, n in steps:
                    b = slice(a * D + n * 512, a * D + (n + 1) * 512)
                    for banks, cols in outs:
                        last = product(ps[:, banks[n], :], gT[0][:, 2 * u + a, cols], gT[1][:, 2 * u + a, cols],
                                       wh[:, s, b], wl[:, s, b], u == 0 and a == 0, u == SLICES - 1 and a == 1)
                    if halves is not None and (a, n) == (1, 0):
                        last.then_inc(halves, 1)
                last.then_inc(unit_used, 1)

            mixers(0)
            dense()
            mixers(1)
            pe.wait_ge(wr_lo, 1)
            for c in range(KC):
                if c == 0:
                    pe.wait_ge(xt_lo, 14)
                    pe.wait_ge(h_half, 5)
                if c == KC // 2:
                    norm_T(3, 1)
                    pe.wait_ge(xt_lo, 16)
                for a, xT in enumerate((XT_h, XT_l)):
                    last = nc.tensor.matmul(ps[0:2 * E, 0, 0:SEQ], wr_hl[:, c, :], xT[:, c, :],
                                            start=c == 0 and a == 0, stop=c == KC - 1 and a == 1)
            last.then_inc(logit, 1)
            pe.wait_ge(consts_in, 48)
            pe.wait_ge(lgt_cp, 1)
            for t in range(TT):
                last = nc.tensor.matmul(ps[:, 2, t * E:(t + 1) * E], lgT[:, tok[t]], stack[0:2 * E, :],
                                        start=True, stop=True)
            last.then_inc(logit, 1)
            pe.wait_ge(routed_ready, 1)
            pe.wait_ge(pool_const, 2)
            nc.tensor.matmul(ps[:, 1, 0:2 * E].rearrange("p (t e) -> p t e", t=TT), before, routed[:, :, :],
                             start=True, stop=False)
            nc.tensor.matmul(ps[:, 1, E:2 * E], ones[:, :], routed[:, 0, :], start=False, stop=True)\
                .then_inc(ranked, 1)

            def gather(sels, base, part):
                pe.wait_ge(sel_ready, sels)
                pe.wait_ge((hn_hi, hn_lo)[part], 1)
                for r in range(4 * part, 4 * part + 4):
                    if r >= 2:
                        pe.wait_ge(gat_cp, base + r - 1)
                    hn = (hn_h, hn_l)[r // 4][:, :].rearrange("p (t n) -> p t n", t=TT)
                    for a in range(2):
                        c = 2 * (r % 4) + a
                        for t in range(TT):
                            last = nc.tensor.matmul(ps[:, 6 + r % 2, a * SEQ:(a + 1) * SEQ],
                                                    hn[:, t, c * P:(c + 1) * P], sel_r[:, t * SEQ:(t + 1) * SEQ],
                                                    start=t == 0, stop=t == TT - 1)
                    last.then_inc(gat, 1)

            def sel_transposes(p, b):
                for t in range(TT):
                    last = transpose(ps[:, 6, tok[t]], sel_r[:, t * SEQ + b * P:t * SEQ + (b + 1) * P].bitcast(F32))
                last.then_inc(st_tr, 1)

            def g_transposes(p, j):
                pe.wait_ge(g_ready, (p + 1) * SLICES + j + 1)
                if j >= 2:
                    pe.wait_ge(g_lo, (p + 1) * SLICES + j - 1)
                for a in range(2):
                    last = transpose(ps[:, 4 + j % 2, a * P:(a + 1) * P],
                                     moe_gbuf[:, (j % 2) * 256 + a * P:(j % 2) * 256 + (a + 1) * P])
                last.then_inc(g_tr, 1)

            def scatter(p, b, r):
                n, t = divmod(r, 2)
                if r == 0:
                    pe.wait_ge(st_cp, p + 1)
                if t == 0:
                    pe.wait_ge(y_cp, p * 2 + n + 1)
                if r >= 2:
                    pe.wait_ge(h_add, p * 4 + r - 1)
                nc.tensor.matmul(ps[:, 6 + r % 2, :], selT[:, b * SEQ + t * P:b * SEQ + (t + 1) * P],
                                 xs3[:, b, n * 512:(n + 1) * 512], start=True, stop=True).then_inc(sc_done, 1)

            def expert(p, b, U, j0, first, x_ready, scatter_prev, gather_next, scatter_here):
                if first:
                    gather(*first, 0)
                    gather(*first, 1)
                pe.wait_ge(gat_cp, x_ready)
                for j in range(SLICES):
                    if j >= 2:
                        pe.wait_ge(g_ready, (p + 1) * SLICES + j - 1)
                    for half in range(2):
                        gemm_unit(pe, U, j0 + 2 * j + half, [(ps[:, j % 2, :], tok[b])], (XT_h, XT_l),
                                         range(4 * half, 4 * half + 4), half == 0, half == 1)
                    if j >= 1:
                        g_transposes(p, j - 1)
                    if 1 <= j <= 4 and scatter_prev:
                        scatter(p - 1, 1 - b, j - 1)
                    if j == 6:
                        if scatter_prev:
                            pe.wait_ge(h_add, p * 4)
                        sel_transposes(p, b)
                for u in range(SLICES):
                    if u < 2 and gather_next:
                        if u == 0:
                            pe.wait_ge(st_cp, p + 1)
                        gather(*gather_next, u)
                    pe.wait_ge(g_lo, (p + 1) * SLICES + u + 1)
                    down_unit(pe, U, j0 + 2 * SLICES + u, [((2, 3), slice(0, P))], moe_gT3, u,
                              y_first if u == SLICES - 1 else None)
                    if u == 0:
                        g_transposes(p, SLICES - 1)
                if scatter_here:
                    if scatter_prev:
                        pe.wait_ge(h_add, p * 4)
                    for r in range(4):
                        scatter(p, b, r)
                    pe.wait_ge(h_add, p * 4 + 4)

            gather(2, 0, 0)
            gather(2, 0, 1)
            for t in range(TT):
                last = nc.tensor.matmul(ps[:, 3, 0:E], ones[:, :], routed[:, t, :], start=t == 0, stop=t == TT - 1)
            last.then_inc(counted, 1)
            expert(0, 0, Units(MOE_BASE), 0, None, 8, False, None, False)
            with pe.Fori(0, E // 2 - 1) as i:
                U = Units(MOE_BASE + FFN_UNITS, i, 2 * FFN_UNITS)
                expert(2 * i + 1, 1, U, 0, None, 8 * i + 8, True, (2 * i + 4, 8 * i + 8), False)
                expert(2 * i + 2, 0, U, FFN_UNITS, None, 8 * i + 16, True, None, False)
            expert(E - 1, 1, Units(MOE_BASE), (E - 1) * FFN_UNITS, None, 4 * E, True, None, True)
            pe.wait_ge(table_ready, 1)
            n_over = pe.value_load(otab[0:1, 0:1], min_val=0, max_val=3)
            with pe.If(n_over > 0):
                with pe.Fori(0, n_over) as k:
                    expert(k + E, 0, Units(OVER_BASE, k, FFN_UNITS, SPLIT), 0, (k + E + 1, 8 * k + 4 * E),
                           8 * k + 4 * E + 8, False, None, True)

        @block.vector
        def _(dve):
            chain = [0]

            def link(ins):
                chain[0] += 1
                ins.then_inc(dchain, 1)
                dve.wait_ge(dchain, chain[0])

            tt, ts, stt = nc.vector.tensor_tensor, nc.vector.tensor_scalar, nc.vector.scalar_tensor_tensor
            copy, reduce = nc.vector.tensor_copy, nc.vector.tensor_reduce
            roots = [0]

            def ask_root(cols, scale):
                ts(ssq[:, cols], ssq[:, cols], scale, EPS, ALU.mult, ALU.add).then_inc(ms_ready, 1)
                roots[0] += 1

            def wait_root():
                dve.wait_ge(rs_ready, roots[0])

            def small_tables():
                dve.wait_ge(consts_in, 48)
                link(copy(pos_f[:, :], pos_i[:, :]))
                for t in range(TT):
                    ins = ts(ang[:, 2, t, :], freq, pos_f[:, t:t + 1], None, ALU.mult)
                link(ins)
                magic = 1.5 * 2 ** 23
                turn = 2 * math.pi
                c1 = 6.28125
                c2 = float((np.array([turn - c1], np.float32).view(np.uint32) & np.uint32(0xFFFFF000)).view(np.float32)[0])
                c3 = turn - c1 - c2
                for a, k in ((0, sin), (1, cos)):
                    k, r = k[:, :, :], ang[:, a]
                    if a:
                        link(ts(k, ang[:, 2], 1 / turn, 0.25, ALU.mult, ALU.add))
                        link(ts(k, k, magic, magic, ALU.add, ALU.subtract))
                    else:
                        link(ts(k, ang[:, 2], 1 / turn, magic, ALU.mult, ALU.add))
                        link(ts(k, k, magic, None, ALU.subtract))
                    link(stt(r, k, -c1, ang[:, 2], ALU.mult, ALU.add))
                    link(stt(r, k, -c2, r, ALU.mult, ALU.add))
                    link(stt(r, k, -c3, r, ALU.mult, ALU.add))
                    if a:
                        link(ts(r, r, math.pi / 2, None, ALU.add))
                    pi = 3.1415925
                    ins = ts(r, r, pi, -pi, ALU.min, ALU.max)
                ins.then_inc(ang_ready, 1)

            def lambda_sums():
                link(tt(lamp[:, :, :, :], lamv[:, 0::2], lamv[:, 1::2], ALU.mult))
                reduce(lams[:, :, :], lamp[:, :, :, :], AX.X, ALU.add).then_inc(lam_sum, 1)
                for l in range(DEPTH):
                    ts(g_subs[:, l:l + 1], g_sub[:, l:l + 1], 1.0 - lambda_init(l), None, ALU.mult)

            def small_tables_end():
                dve.wait_ge(lam_exp, 1)
                link(tt(lamn[:, :], lame[:, 1], lame[:, 0], ALU.subtract))
                for l in range(DEPTH):
                    ins = ts(lamn[:, l:l + 1], lamn[:, l:l + 1], -lambda_init(l), None, ALU.add)
                link(ins)
                dve.wait_ge(wr_hi, 1)
                tt(wr_hl[:, :, E:2 * E], wr, wr_hl[:, :, 0:E].bitcast(F32), ALU.subtract).then_inc(wr_lo, 1)

            split_to = [0]

            def split_until(U, j):
                while split_to[0] <= U.base + j:
                    split_lo(dve, Units(0), split_to[0])
                    split_to[0] += 1

            def norm_lo(n, half, gain):
                for r in (2 * half, 2 * half + 1):
                    dve.wait_ge(xt_hi, 4 * n + r + 1)
                    for a in range(2):
                        c = 2 * r + a
                        ins = stt(XT_l[:, c, :], hT(n, c), gain[:, c:c + 1],
                                  XT_h[:, c, :].bitcast(F32), ALU.mult, ALU.subtract)
                    ins.then_inc(xt_lo, 1)

            def norm_factors(n):
                dve.wait_ge(sq_done, 2 * n + 2)
                ts(ssq[:, 0:TT], ssq[:, 0:TT], 1.0 / D, EPS, ALU.mult, ALU.add).then_inc(ms_ready, 1)
                roots[0] += 1

            def rotate(x1, x2, cs, sn, tmp):
                tt(tmp[0], x1, cs, ALU.mult)
                tt(tmp[1], x2, sn, ALU.mult)
                tt(tmp[2], x1, sn, ALU.mult)
                link(tt(tmp[3], x2, cs, ALU.mult))
                tt(x1, tmp[0], tmp[1], ALU.subtract)
                return tt(x2, tmp[2], tmp[3], ALU.add)

            def mixers(l):
                U = Units(MIX_BASE[l])
                gain = g_attn[:, l, :]
                if l == 0:
                    norm_lo(0, 0, gain)
                    for u in range(2):
                        dve.wait_ge(hi_first, u + 1)
                        tt(wl[:, u, 0:UNIT // 2], raw[:, u, 0:UNIT // 2], wh[:, u, 0:UNIT // 2].bitcast(F32),
                           ALU.subtract).then_inc(lo_first, 1)
                        dve.wait_ge(hi_ready, u + 1)
                        tt(wl[:, u, UNIT // 2:], raw[:, u, UNIT // 2:], wh[:, u, UNIT // 2:].bitcast(F32),
                           ALU.subtract).then_inc(lo_ready, 1)
                        if u == 0:
                            norm_lo(0, 1, gain)
                    split_to[0] = 2
                zq = mx(ZQK, 2048)
                zq32 = zq.rearrange("p (g d) -> p g d", d=HD)
                zq4 = zq.rearrange("p (t g d) -> p t g d", t=TT, d=HD)
                rin = mx(RIN, HEADS * 384).rearrange("p (h n) -> p h n", h=HEADS)
                ya = xs[:, 0:1024].rearrange("p (t h n) -> p t h n", t=TT, h=HEADS)
                ro = ps[:, 6:8, :].rearrange("p b (h n) -> p (b h) n", h=HEADS)

                def decay_scores(hd):
                    dve.wait_ge(ret_s, 4 * l + hd + 1)
                    bank = 4 + hd % 2
                    tt(rin[:, hd, 0:SEQ], ps[:, bank, 0:SEQ], decay[:, hd, :], ALU.mult)
                    tt(rin[:, hd, SEQ:384], ps[:, bank, SEQ:384], decay[:, hd, 0:P], ALU.mult).then_inc(ret_w, 1)

                def maxima(k):
                    dve.wait_ge(da_s, 3 * l + k + 1)
                    b, m = (6, 6, 4)[k], (2, 2, 4)[k]
                    for c in range(2):
                        sc = ps[:, b + c, :].rearrange("p (h n) -> p h n", h=m)
                        diag = sc[:, :, P:SEQ] if k < 2 else sc
                        ins = tt(diag, diag, mask.unsqueeze(1).to_broadcast([P, m, P]), ALU.add)
                    link(ins)
                    t = 1 if k < 2 else 0
                    cols = slice(2 * k, 2 * k + 2) if k < 2 else slice(0, 4)
                    mv = mxs[:, t, :].rearrange("p (c h) -> p c h", c=2)[:, :, cols]
                    nv = nbs[:, t, :].rearrange("p (c h) -> p c h", c=2)[:, :, cols]
                    link(reduce(mv, ps[:, b:b + 2, :].rearrange("p c (h n) -> p c h n", h=m), AX.X, ALU.max))
                    ts(nv, mv, -DA_SCALE, None, ALU.mult).then_inc(nb_ready, 1)

                def probabilities(t):
                    e, n = ((mx(ZR, 1024), P), (mx(ZQK, 2048), SEQ))[t]
                    e = e.rearrange("p (a n) -> p a n", a=8)
                    dve.wait_ge(exp_done, 3 * l + (3, 2)[t])
                    link(nc.vector.reciprocal(rcs[:, t, :], sms[:, t, :]))
                    link(stt(rcs[:, t, 4:8], rcs[:, t, 4:8], lamn[:, l:l + 1], sms[:, t, 0:4], ALU.mult, ALU.mult))
                    tt(rsq[:, t, :], rcs[:, t, 0:HEADS], rcs[:, t, 0:HEADS], ALU.mult)
                    for hd in range(HEADS):
                        ins = stt(e[:, hd], e[:, 4 + hd], rcs[:, t, 4 + hd:5 + hd], e[:, hd], ALU.mult, ALU.add)
                    ins.then_inc(pd_ready, 1)

                def retention_means():
                    dve.wait_ge(ret_o, l + 1)
                    link(reduce(mu[:, :], ro, AX.X, ALU.add))
                    ts(mu[:, :], mu[:, :], -1.0 / VD, None, ALU.mult).then_inc(mu_ready, 1)

                def retention_output():
                    dve.wait_ge(gn_sq, l + 1)
                    ask_root(slice(0, 8), 1.0 / VD)
                    wait_root()
                    dve.wait_ge(mu_ready, l + 1)
                    for g in range(8):
                        ins = ts(xs[:, 1024 + g * VD:1024 + (g + 1) * VD],
                                 ps[:, 6 + g // 4, (g % 4) * VD:(g % 4 + 1) * VD], mu[:, g:g + 1], rst[:, g:g + 1],
                                 ALU.add, ALU.mult)
                    link(ins)
                    dve.wait_ge(silu_ready, l + 1)
                    tt(xs[:, 1024:2048], xs[:, 1024:2048], mx(ZG, 1024), ALU.mult).then_inc(yr_ready, 1)

                def out_root(t):
                    dve.wait_ge(osq, 2 * l + 2 - t)
                    cols = slice(8 + 4 * t, 12 + 4 * t)
                    link(reduce(ssq[:, cols], mx(RETT + 512 * t, 512).rearrange("p (h n) -> p h n", h=HEADS),
                                AX.X, ALU.add))
                    link(tt(ssq[:, cols], ssq[:, cols], rsq[:, t, :], ALU.mult))
                    ask_root(cols, 1.0 / VD)

                def attention_output(t):
                    dve.wait_ge(rs_ready, roots[0] - t)
                    link(tt(yaf[:, 4 * t:4 * t + 4], rst[:, 8 + 4 * t:12 + 4 * t], rcs[:, t, 0:HEADS], ALU.mult))
                    o = ps[:, 5 - t, :].rearrange("p (h n) -> p h n", h=HEADS)
                    return tt(ya[:, t], o, yaf[:, 4 * t:4 * t + 4].unsqueeze(2).to_broadcast([P, HEADS, VD]), ALU.mult)

                def yt(r):
                    dve.wait_ge(yt_hi, 4 * l + r + 1)
                    c = slice(2 * (r % 2), 2 * (r % 2) + 2)
                    hi, lo = (YR_h, YR_l) if r < 2 else (XT_h, XT_l)
                    stt(lo[:, c, :], ps[:, (6, 7, 4, 5)[r], :].rearrange("p (a n) -> p a n", a=2),
                        1.0 if r < 2 else g_subs[:, l:l + 1], hi[:, c, :].bitcast(F32),
                        ALU.mult, ALU.subtract).then_inc(yt_lo, 1)

                for n in range(2 * IN_GROUPS):
                    if n == 0 and l > 0:
                        norm_lo(2 * l, 1, gain)
                    if n == 1 - l:
                        norm_factors(2 * l)
                    if l == 0 and n == 3:
                        small_tables()
                    if l == 0 and n == 9:
                        lambda_sums()
                    if l == 0 and n == 11:
                        small_tables_end()
                    if n == 5:
                        dve.wait_ge(in_evac, IN_GROUPS * l + 2)
                        link(reduce(ssq[:, 0:32], xs[:, :].rearrange("p (g d) -> p g d", d=HD), AX.X, ALU.add))
                        ask_root(slice(0, 32), 1.0 / HD)
                    if n == 7:
                        for t in range(TT):
                            for a in range(2):
                                v = zq4[:, t, 8 * a:8 * a + 8]
                                ins = tt(v, v, g_qk[:, l, a, :].unsqueeze(1).to_broadcast([P, 8, HD]), ALU.mult)
                        link(ins)
                    if n == 8:
                        dve.wait_ge(sin_ready, 1)
                        shape = [P, TT, 16, DA_HALF]
                        tmp = [xs[:, a * 256:(a + 1) * 256].rearrange("p (t g d) -> p t g d", t=TT, d=DA_HALF)
                               for a in range(4)]
                        rotate(zq4[:, :, :, 0:DA_HALF], zq4[:, :, :, DA_HALF:2 * DA_HALF],
                               cos[:, :, 0:DA_HALF].unsqueeze(2).to_broadcast(shape),
                               sin[:, :, 0:DA_HALF].unsqueeze(2).to_broadcast(shape), tmp).then_inc(zqk_ready, 1)
                    if n == 12:
                        dve.wait_ge(decay_in, 16)
                        maxima(0)
                        decay_scores(0)
                        decay_scores(1)
                    if n == 13:
                        decay_scores(2)
                        decay_scores(3)
                    if n == 14:
                        maxima(1)
                    if n == 15:
                        maxima(2)
                    if n == 16:
                        probabilities(1)
                        retention_means()
                    if n == 17:
                        probabilities(0)
                        retention_output()
                    if n == 19:
                        yt(0)
                        yt(1)
                        out_root(1)
                    split_until(U, n + AHEAD)
                    if n == 6:
                        wait_root()
                        link(tt(zq32, zq32, rst[:, 0:32].unsqueeze(2).to_broadcast([P, 32, HD]), ALU.mult))
                out_root(0)
                attention_output(1)
                attention_output(0).then_inc(ya_ready, 1)
                split_until(U, 22)
                yt(2)
                yt(3)

                def gate_proj(u):
                    n = u // 2
                    gate = mx(SGA if u % 2 else SGB, 2048)
                    gate = gate.rearrange("p (t n) -> p t n", t=TT)[:, :, n * 512:(n + 1) * 512]
                    dve.wait_ge(unit_used, U.count(2 * IN_GROUPS + u))
                    ins = tt(gate, gate, ps[:, PROJ_BANK[u]:PROJ_BANK[u] + 2, :], ALU.mult)
                    if u % 2 == 0:
                        ins.then_inc(proj_evac, 1)
                    else:
                        link(ins)
                        dve.wait_ge(proj_evac, 2 * l + n + 1)
                        other = mx(SGB, 2048).rearrange("p (t n) -> p t n", t=TT)[:, :, n * 512:(n + 1) * 512]
                        tt(gate, gate, other, ALU.add).then_inc(m_ready, 1)

                def mt(half):
                    for r in (2 * half, 2 * half + 1):
                        dve.wait_ge(mt_hi, 4 * l + r + 1)
                        v = ps[:, 4 + r, :].rearrange("p (a n) -> p a n", a=2)
                        tt(MT_l[:, 2 * r:2 * r + 2, :], v, MT_h[:, 2 * r:2 * r + 2, :].bitcast(F32), ALU.subtract)\
                            .then_inc(mt_lo, 1)

                def add_h(n):
                    dve.wait_ge(unit_used, U.count(2 * IN_GROUPS + 4 + 2 * n + 1))
                    v = h[:, :, n * 512:(n + 1) * 512]
                    tt(v, ps[:, 2 * n:2 * n + 2, :], v, ALU.add).then_inc(h_half, 1)

                gate_proj(0)
                split_until(U, 23)
                gate_proj(1)
                split_until(U, 24)
                gate_proj(2)
                mt(0)
                split_until(U, 25)
                gate_proj(3)
                mt(1)
                split_until(U, 27)
                add_h(0)
                split_until(U, 28)
                norm_lo(2 * l + 1, 0, g_ffn[:, l, :])
                split_until(U, 29)
                add_h(1)

            def dense():
                U = Units(DENSE_BASE)

                def g(j):
                    dve.wait_ge(sig_done, j + 1)
                    if j == 0:
                        dve.wait_ge(rs_ready, ROOTS)
                    b = 2 * (j % 2)
                    at = [slice((b + t) * 256, (b + t + 1) * 256) for t in range(TT)]
                    for t in range(TT):
                        ins = stt(gbuf[:, at[t]], ps[:, b + t, 0:256], rn[:, t:t + 1], sgm[:, at[t]], ALU.mult, ALU.mult)
                    ins.then_inc(g_half, 1)
                    dve.wait_ge(g_half, j + 1)
                    for t in range(TT):
                        ins = stt(gbuf[:, at[t]], ps[:, b + t, 256:512], rn[:, t:t + 1], gbuf[:, at[t]],
                                  ALU.mult, ALU.mult)
                    ins.then_inc(g_ready, 1)

                def lo(j):
                    dve.wait_ge(g_hi, j + 1)
                    tt(gT3[1][:, 2 * j:2 * j + 2, :], ps[:, 4 + j % 2, :].rearrange("p (a n) -> p a n", a=2),
                       gT3[0][:, 2 * j:2 * j + 2, :].bitcast(F32), ALU.subtract).then_inc(g_lo, 1)
                for j in range(SLICES):
                    if j == 0:
                        norm_lo(1, 1, g_ffn[:, 0, :])
                        norm_factors(1)
                    if j >= 1:
                        g(j - 1)
                    if j >= 2:
                        lo(j - 2)
                    split_until(U, 2 * j + 1 + AHEAD)
                for u in range(SLICES):
                    if u == 0:
                        g(SLICES - 1)
                        lo(SLICES - 2)
                    if u == 1:
                        lo(SLICES - 1)
                    if u < SLICES - 1:
                        split_until(U, 2 * SLICES + u + AHEAD)
                for n in range(2):
                    if n == 0:
                        dve.wait_ge(down_half, 1)
                    else:
                        dve.wait_ge(unit_used, U.count(FFN_UNITS - 1))
                    for t in range(TT):
                        v = h[:, t, n * 512:(n + 1) * 512]
                        ins = tt(v, ps[:, (2, 6)[t] + n, :], v, ALU.add)
                    ins.then_inc(h_half, 1)
                    if n == 0:
                        norm_lo(2, 0, g_attn[:, 1, :])
                split_until(U, FFN_UNITS + 1)

            mixers(0)
            dense()
            mixers(1)
            def select(b, e, places):
                for t in range(TT):
                    r = places[:, t, bass.ds(e, 1)]
                    ins = ts(sel_r[:, t * SEQ + b * P:t * SEQ + (b + 1) * P], iota, r, None, ALU.is_equal)
                ins.then_inc(sel_ready, 1)

            def hidden_lo(t):
                v = slice(t * D, (t + 1) * D)
                return stt(hn_l[:, v], xs3[:, t, :], rn[:, t:t + 1], hn_h[:, v].bitcast(F32), ALU.mult, ALU.subtract)

            norm_lo(3, 1, g_ffn[:, 1, :])
            dve.wait_ge(h_half, 6)
            tt(xs3, h[:, :, :], g_moe.unsqueeze(1).to_broadcast([P, TT, D]), ALU.mult).then_inc(hg_ready, 1)
            norm_factors(3)
            dve.wait_ge(rs_ready, 2 * ROOTS)
            dve.wait_ge(logit, 2)
            link(tt(lg[:, :, :], ps[:, 2, 0:TT * E].rearrange("p (t e) -> p t e", t=TT),
                    rn[:, :].unsqueeze(2).to_broadcast([P, TT, E]), ALU.mult))
            for t in range(TT):
                ins = nc.vector.max(top[:, t, :], lg[:, t, :])
            link(ins)
            for t in range(TT):
                ins = nc.vector.max_index(tidx[:, t, :], top[:, t, :], lg[:, t, :])
            link(ins)
            tt(tdf[:, :], top[:, :, 1], top[:, :, 0], ALU.subtract).then_inc(te_in, 1)
            link(copy(tif[:, :, :], tidx[:, :, :]))
            for a in range(2):
                ins = tt(oh[:, a], iota[:, 0:E].unsqueeze(1).to_broadcast([P, TT, E]),
                         tif[:, :, a:a + 1].to_broadcast([P, TT, E]), ALU.is_equal)
            link(ins)
            tt(routed[:, :, :], oh[:, 0], oh[:, 1], ALU.add).then_inc(routed_ready, 1)
            dve.wait_ge(hg_ready, 1)
            dve.wait_ge(hn_hi, 1)
            hidden_lo(0)
            dve.wait_ge(routed_ready, 1)
            dve.wait_ge(ranked, 1)
            link(stt(rank1[:, :, :], ps[:, 1, 0:TT * E].rearrange("p (t e) -> p t e", t=TT), 1.0, routed[:, :, :],
                     ALU.add, ALU.mult))
            link(ts(rank[:, :, :], rank1[:, :, :], -1.0, None, ALU.add))
            select(0, 0, rank)
            select(1, 1, rank)
            hidden_lo(1).then_inc(hn_lo, 1)
            ts(rank2[:, :, :], rank1[:, :, :], -1.0 - P, None, ALU.add)
            dve.wait_ge(te_out, 1)
            link(ts(tw[:, 0, :], te[:, :], 1.0, None, ALU.add))
            link(nc.vector.reciprocal(tw[:, 1, :], tw[:, 0, :]))
            link(tt(tw[:, 2, :], te[:, :], tw[:, 1, :], ALU.mult))
            for t in range(TT):
                ins = ts(comb[:, t, :], oh[:, 0, t, :], tw[:, 1, t:t + 1], None, ALU.mult)
            link(ins)
            for t in range(TT):
                ins = stt(comb[:, t, :], oh[:, 1, t, :], tw[:, 2, t:t + 1], comb[:, t, :], ALU.mult, ALU.add)
            link(ins)
            dve.wait_ge(counted, 1)
            link(ts(okey[:, 0, :], ps[:, 3, 0:E], float(P), None, ALU.is_gt))
            reduce(nover[:, :], okey[:, 0, :], AX.X, ALU.add)
            link(ts(okey[:, 1, :], iota[:, 0:E], -1.0, float(E), ALU.mult, ALU.add))
            link(tt(okey[:, 1, :], okey[:, 1, :], okey[:, 0, :], ALU.mult))
            link(nc.vector.max(okey[:, 2, :], okey[:, 1, :]))
            link(ts(okey[:, 2, :], okey[:, 2, :], -1.0, float(E), ALU.mult, ALU.add))
            ts(otab[:, 8:16], okey[:, 2, :], float(E - 1), None, ALU.min)
            copy(otab[:, 0:1], nover[:, :]).then_inc(table_ready, 1)

            def g(p, U, j0, j):
                dve.wait_ge(sig_done, (p + 1) * SLICES + j + 1)
                cols = slice((j % 2) * 256, (j % 2 + 1) * 256)
                tt(moe_gbuf[:, cols], ps[:, j % 2, 0:256], moe_sgm[:, cols], ALU.mult).then_inc(g_half, 1)
                dve.wait_ge(g_half, (p + 1) * SLICES + j + 1)
                tt(moe_gbuf[:, cols], ps[:, j % 2, 256:512], moe_gbuf[:, cols], ALU.mult).then_inc(g_ready, 1)

            def lo(p, j):
                dve.wait_ge(g_hi, (p + 1) * SLICES + j + 1)
                tt(moe_gT3[1][:, 2 * j:2 * j + 2, :], ps[:, 4 + j % 2, 0:256].rearrange("p (a n) -> p a n", a=2),
                   moe_gT3[0][:, 2 * j:2 * j + 2, :].bitcast(F32), ALU.subtract).then_inc(g_lo, 1)

            def add_back(p, e, r):
                n, t = divmod(r, 2)
                dve.wait_ge(sc_done, p * 4 + r + 1)
                v = h[:, t, n * 512:(n + 1) * 512]
                stt(v, ps[:, 6 + r % 2, :], comb[:, t, bass.ds(e, 1)], v, ALU.mult, ALU.add).then_inc(h_add, 1)

            def expert(p, b, U, j0, e, places, last_split, scatter_prev, e_next, scatter_here, first=False):
                if first:
                    select(b, e, places)
                    for j in range(AHEAD):
                        split_lo(dve, U, j0 + j)
                for j in range(SLICES):
                    if j >= 1:
                        g(p, U, j0, j - 1)
                    if j >= 2:
                        lo(p, j - 2)
                    if 2 <= j <= 5 and scatter_prev is not None:
                        add_back(p - 1, scatter_prev, j - 2)
                    if j in (8, 9) and e_next is not None:
                        if j == 8:
                            dve.wait_ge(st_tr, p + 1)
                        select(j - 8, e_next + j - 8, places)
                    for a in range(2):
                        split_lo(dve, U, j0 + 2 * j + AHEAD + a)
                for u in range(SLICES):
                    if u == 0:
                        g(p, U, j0, SLICES - 1)
                        lo(p, SLICES - 2)
                    if u == 1:
                        lo(p, SLICES - 1)
                    if 2 * SLICES + u + AHEAD <= last_split:
                        split_lo(dve, U, j0 + 2 * SLICES + u + AHEAD)
                if scatter_here:
                    for r in range(4):
                        add_back(p, e, r)

            expert(0, 0, Units(MOE_BASE), 0, 0, rank, FFN_UNITS + 1, None, None, False)
            with dve.Fori(0, E // 2 - 1) as i:
                U = Units(MOE_BASE + FFN_UNITS, i, 2 * FFN_UNITS)
                expert(2 * i + 1, 1, U, 0, 2 * i + 1, rank, FFN_UNITS + 1, 2 * i, 2 * i + 2, False)
                expert(2 * i + 2, 0, U, FFN_UNITS, 2 * i + 2, rank, FFN_UNITS + 1, 2 * i + 1, None, False)
            U = Units(MOE_BASE)
            expert(E - 1, 1, U, (E - 1) * FFN_UNITS, E - 1, rank, FFN_UNITS - 1, E - 2, None, True)
            dve.wait_ge(table_ready, 1)
            n_over = dve.value_load(otab[0:1, 0:1], min_val=0, max_val=3)
            with dve.If(n_over > 0):
                with dve.Fori(0, n_over) as k:
                    e = dve.value_load(otab[0:1, bass.ds(k + 8, 1)], min_val=0, max_val=E - 1)
                    expert(k + E, 0, Units(OVER_BASE, k, FFN_UNITS, SPLIT), 0, e, rank2, FFN_UNITS - 1,
                           None, None, True, True)


def lambda_init(layer):
    return 0.8 - 0.6 * math.exp(-0.3 * layer)


BIG = ["w_in", "w_proj_da", "w_proj_ret", "w_out", "dense_w1", "dense_w3", "dense_w2", "moe_w1", "moe_w3",
       "moe_w2"]


def packed(inp):
    def chunked(g):
        return g.reshape(DEPTH, KC, P).transpose(2, 0, 1).reshape(P, DEPTH * KC)
    c = tables()
    c["g_attn"], c["g_ffn"] = chunked(inp["attn_norm"]), chunked(inp["ffn_norm"])
    c["g_sub"] = inp["da_subln"].T
    c["wr"] = inp["w_router"][0].reshape(KC, P, E).transpose(1, 0, 2).reshape(P, KC * E)
    r = {"g_qk": np.stack([inp["da_q_norm"], inp["da_k_norm"]], 1),
         "lam": np.stack([inp[n] for n in ("lam_q1", "lam_k1", "lam_q2", "lam_k2")]),
         "g_moe": inp["ffn_norm"][DEPTH - 1]}
    cols = np.concatenate([c[n] for n in COLS], axis=1)
    rows = np.concatenate([r[n].reshape(1, -1) for n in ROWS], axis=1)
    assert cols.shape == (P, COLS_W) and rows.shape == (1, ROWS_W)
    return np.ascontiguousarray(cols), np.ascontiguousarray(rows)


def kernel(**inputs):
    import concourse.bacc as bacc
    from concourse.bass_utils import run_bass_kernel_spmd

    nc = bacc.Bacc("TRN2", target_bir_lowering=False, num_devices=1)
    arrays, args = {}, []
    inp = {n: np.ascontiguousarray(a) for n, a in inputs.items()}
    cols, rows = packed(inp)
    xT = np.ascontiguousarray(inp["x"][0].T.reshape(KC, P, SEQ).transpose(1, 0, 2))
    tensors = [("x", inp["x"]), ("xT", xT), ("positions", np.ascontiguousarray(inp["positions"].reshape(TT, P).T))]
    tensors += [(n, inp[n]) for n in BIG] + [("cols", cols), ("rows", rows)]
    for name, a in tensors:
        arrays[f"in_{name}"] = a
        args.append(nc.dram_tensor(f"in_{name}", a.shape, mybir.dt.from_np(a.dtype), kind="ExternalInput").ap())
    args.append(nc.dram_tensor("out", (1, SEQ, D), F32, kind="ExternalOutput").ap())
    build(nc, *args)
    r = run_bass_kernel_spmd(nc, [arrays], core_ids=[0])
    return r.results[0]["out"]
```
